# Optimizing a Trainium2 kernel written in Bass

```python
import math
import jax, jax.numpy as jnp
from jax import lax
import numpy as np

D_MODEL = 1024
BATCH = 1
SEQ = 256
DEPTH = 2

HEAD_DIM = 64
ROPE_THETA = 10000.0
NORM_EPS = 1e-6
NEG_INF = -1e30
D_FF = 4 * D_MODEL
Q_BLOCK = 128
MAX_POS_OFFSET = 4096

MLA_HEADS = 8
MLA_Q_RANK = 384
MLA_KV_RANK = 256
MLA_NOPE = 64
MLA_ROPE = 32
MLA_V = 64

DIL_CONFIGS = ((128, 1), (512, 4), (2048, 16))
DIL_GROUPS = len(DIL_CONFIGS)
DIL_HEADS = 4

DIFF_HEADS = 4
DIFF_DIM = 64

MOBA_HEADS = 8
MOBA_BLOCK = 256
MOBA_TOPK = 3
MOBA_Q_CHUNK = 32

N_EVEN = (DEPTH + 1) // 2
N_ODD = DEPTH // 2

EVEN_IN = MLA_Q_RANK + MLA_KV_RANK + MLA_ROPE + 3 * DIL_GROUPS * DIL_HEADS * HEAD_DIM
EVEN_OUT = MLA_HEADS * MLA_V + DIL_HEADS * HEAD_DIM
ODD_IN = 3 * DIFF_HEADS * 2 * DIFF_DIM + 3 * MOBA_HEADS * HEAD_DIM
ODD_OUT = DIFF_HEADS * 2 * DIFF_DIM + MOBA_HEADS * HEAD_DIM


def rms_norm(x, w):
    xf = x.astype(jnp.float32)
    y = xf * lax.rsqrt(jnp.mean(xf * xf, axis=-1, keepdims=True) + NORM_EPS)
    return (y * w.astype(jnp.float32)).astype(x.dtype)

def apply_rope(x, positions):
    half = x.shape[-1] // 2
    inv_freq = ROPE_THETA ** (-jnp.arange(half, dtype=jnp.float32) / half)
    ang = positions.astype(jnp.float32)[:, :, None] * inv_freq
    bshape = ang.shape[:2] + (1,) * (x.ndim - 3) + (half,)
    cos = jnp.cos(ang).reshape(bshape)
    sin = jnp.sin(ang).reshape(bshape)
    xf = x.astype(jnp.float32)
    x1, x2 = xf[..., :half], xf[..., half:]
    return jnp.concatenate([x1 * cos - x2 * sin, x2 * cos + x1 * sin], axis=-1).astype(x.dtype)

def dense_causal_attention(q, k, v):
    b, s, h, dk = q.shape
    nq = s // Q_BLOCK
    scale = dk ** -0.5
    qb = q.reshape(b, nq, Q_BLOCK, h, dk).transpose(1, 0, 2, 3, 4)
    kpos = jnp.arange(s)

    def one_block(args):
        i, qi = args
        sc = jnp.einsum('bqhd,bkhd->bhqk', qi, k, preferred_element_type=jnp.float32) * scale
        qpos = i * Q_BLOCK + jnp.arange(Q_BLOCK)
        sc = jnp.where(qpos[:, None] >= kpos[None, :], sc, NEG_INF)
        p = jax.nn.softmax(sc, axis=-1)
        return jnp.einsum('bhqk,bkhe->bqhe', p.astype(v.dtype), v)

    out = lax.map(one_block, (jnp.arange(nq), qb))
    return out.transpose(1, 0, 2, 3, 4).reshape(b, s, h, v.shape[-1])

def diff_causal_attention(q, k, v, lam):
    b, s, h, _, d = q.shape
    nq = s // Q_BLOCK
    scale = d ** -0.5
    qb = q.reshape(b, nq, Q_BLOCK, h, 2, d).transpose(1, 0, 2, 3, 4, 5)
    kpos = jnp.arange(s)

    def one_block(args):
        i, qi = args
        sc = jnp.einsum('bqhmd,bkhmd->bmhqk', qi, k, preferred_element_type=jnp.float32) * scale
        qpos = i * Q_BLOCK + jnp.arange(Q_BLOCK)
        sc = jnp.where(qpos[:, None] >= kpos[None, :], sc, NEG_INF)
        p = jax.nn.softmax(sc, axis=-1)
        pd = p[:, 0] - lam * p[:, 1]
        return jnp.einsum('bhqk,bkhe->bqhe', pd.astype(v.dtype), v)

    out = lax.map(one_block, (jnp.arange(nq), qb))
    return out.transpose(1, 0, 2, 3, 4).reshape(b, s, h, v.shape[-1])

def sliding_window_lse(q, k, v, window):
    n, l, h, d = q.shape
    blk = window
    lp = -(-l // blk) * blk
    pad = ((0, 0), (0, lp - l), (0, 0), (0, 0))
    q, k, v = jnp.pad(q, pad), jnp.pad(k, pad), jnp.pad(v, pad)
    nb = lp // blk
    qb = q.reshape(n, nb, blk, h, d)
    kb = k.reshape(n, nb, blk, h, d)
    vb = v.reshape(n, nb, blk, h, d)
    prev_pad = ((0, 0), (1, 0), (0, 0), (0, 0), (0, 0))
    kk = jnp.concatenate([jnp.pad(kb[:, :-1], prev_pad), kb], axis=2)
    vv = jnp.concatenate([jnp.pad(vb[:, :-1], prev_pad), vb], axis=2)
    sc = jnp.einsum('nbqhd,nbkhd->nbhqk', qb, kk, preferred_element_type=jnp.float32) * d ** -0.5
    qloc = jnp.arange(blk) + blk
    kloc = jnp.arange(2 * blk)
    rel = qloc[:, None] - kloc[None, :]
    band = (rel >= 0) & (rel <= window)
    kabs = jnp.arange(nb)[:, None, None] * blk + kloc[None, None, :] - blk
    mask = band[None] & (kabs >= 0)
    sc = jnp.where(mask[None, :, None], sc, NEG_INF)
    lse = jax.nn.logsumexp(sc, axis=-1)
    p = jnp.exp(sc - lse[..., None])
    out = jnp.einsum('nbhqk,nbkhd->nbqhd', p.astype(v.dtype), vv).reshape(n, lp, h, d)[:, :l]
    lse = lse.transpose(0, 1, 3, 2).reshape(n, lp, h)[:, :l]
    return out, lse

def dilated_group(q, k, v, window, dilation):
    b, s, h, d = q.shape
    m = s // dilation

    def split(t):
        return t.reshape(b, m, dilation, h, d).transpose(0, 2, 1, 3, 4).reshape(b * dilation, m, h, d)

    out, lse = sliding_window_lse(split(q), split(k), split(v), window // dilation)
    out = out.reshape(b, dilation, m, h, d).transpose(0, 2, 1, 3, 4).reshape(b, s, h, d)
    lse = lse.reshape(b, dilation, m, h).transpose(0, 2, 1, 3).reshape(b, s, h)
    return out, lse

def dilated_mixture(q, k, v):
    outs, lses = [], []
    for g, (w, r) in enumerate(DIL_CONFIGS):
        o, l = dilated_group(q[:, :, g], k[:, :, g], v[:, :, g], w, r)
        outs.append(o)
        lses.append(l)
    alpha = jax.nn.softmax(jnp.stack(lses), axis=0)
    out = jnp.sum(alpha[..., None] * jnp.stack(outs).astype(jnp.float32), axis=0)
    return out.astype(q.dtype)

def moba_attention(q, k, v):
    b, s, h, d = q.shape
    blk = MOBA_BLOCK
    sp = -(-s // blk) * blk
    nb = sp // blk
    scale = d ** -0.5
    pad = ((0, 0), (0, sp - s), (0, 0), (0, 0))
    qp, kp, vp = jnp.pad(q, pad), jnp.pad(k, pad), jnp.pad(v, pad)
    qb = qp.reshape(b, nb, blk, h, d)
    kb = kp.reshape(b, nb, blk, h, d)
    vb = vp.reshape(b, nb, blk, h, d)

    s_own = jnp.einsum('bnqhd,bnkhd->bnhqk', qb, kb, preferred_element_type=jnp.float32) * scale
    s_own = jnp.where(jnp.tril(jnp.ones((blk, blk), dtype=bool)), s_own, NEG_INF)
    lse_own = jax.nn.logsumexp(s_own, axis=-1)
    o_own = jnp.einsum('bnhqk,bnkhd->bnqhd', jnp.exp(s_own - lse_own[..., None]).astype(v.dtype), vb)
    o_own = o_own.reshape(b, sp, h, d)[:, :s].astype(jnp.float32)
    lse_own = lse_own.transpose(0, 1, 3, 2).reshape(b, sp, h)[:, :s]

    kmean = jnp.mean(kb.astype(jnp.float32), axis=2)
    gate = jnp.einsum('bshd,bnhd->bhsn', q.astype(jnp.float32), kmean)
    qblk = jnp.arange(s) // blk
    past = jnp.arange(nb)[None, :] < qblk[:, None]
    gate = jnp.where(past, gate, NEG_INF)
    n_sel = min(MOBA_TOPK, nb)
    _, idx = lax.top_k(gate, n_sel)
    valid = idx < qblk[None, None, :, None]

    kbh = kb.transpose(0, 3, 1, 2, 4)
    vbh = vb.transpose(0, 3, 1, 2, 4)
    nc = s // MOBA_Q_CHUNK
    qc_all = q.transpose(0, 2, 1, 3).reshape(b, h, nc, MOBA_Q_CHUNK, d).transpose(2, 0, 1, 3, 4)
    ic_all = idx.reshape(b, h, nc, MOBA_Q_CHUNK, n_sel).transpose(2, 0, 1, 3, 4)
    vc_all = valid.reshape(b, h, nc, MOBA_Q_CHUNK, n_sel).transpose(2, 0, 1, 3, 4)
    bidx = jnp.arange(b)[:, None, None, None]
    hidx = jnp.arange(h)[None, :, None, None]

    def chunk(args):
        qc, ic, vc = args
        kg = kbh[bidx, hidx, ic]
        vg = vbh[bidx, hidx, ic]
        sc = jnp.einsum('bhqd,bhqjkd->bhqjk', qc, kg, preferred_element_type=jnp.float32) * scale
        sc = jnp.where(vc[..., None], sc, NEG_INF).reshape(b, h, MOBA_Q_CHUNK, n_sel * blk)
        lse = jax.nn.logsumexp(sc, axis=-1)
        p = jnp.exp(sc - lse[..., None]).reshape(b, h, MOBA_Q_CHUNK, n_sel, blk)
        o = jnp.einsum('bhqjk,bhqjkd->bhqd', p.astype(vg.dtype), vg)
        return o, lse

    o_sel, lse_sel = lax.map(chunk, (qc_all, ic_all, vc_all))
    o_sel = o_sel.transpose(1, 0, 3, 2, 4).reshape(b, s, h, d).astype(jnp.float32)
    lse_sel = lse_sel.transpose(1, 0, 3, 2).reshape(b, s, h)

    lse_tot = jnp.logaddexp(lse_own, lse_sel)
    out = (jnp.exp(lse_own - lse_tot)[..., None] * o_own
           + jnp.exp(lse_sel - lse_tot)[..., None] * o_sel)
    return out.astype(q.dtype)

def even_mixer(h, positions, w_in, w_out, q_lat_norm, kv_lat_norm, w_uq, w_ukv,
               mla_qn, mla_kn, dil_qn, dil_kn):
    b, s, _ = h.shape
    u = h @ w_in
    o1 = MLA_Q_RANK
    o2 = o1 + MLA_KV_RANK
    o3 = o2 + MLA_ROPE
    c_q, c_kv, k_r, u_dil = u[..., :o1], u[..., o1:o2], u[..., o2:o3], u[..., o3:]

    q = jnp.einsum('bsr,rhd->bshd', rms_norm(c_q, q_lat_norm), w_uq)
    kv = jnp.einsum('bsr,rhd->bshd', rms_norm(c_kv, kv_lat_norm), w_ukv)
    k_nope, v_a = kv[..., :MLA_NOPE], kv[..., MLA_NOPE:]
    k_rope = jnp.broadcast_to(k_r[:, :, None, :], (b, s, MLA_HEADS, MLA_ROPE))
    k = jnp.concatenate([k_nope, k_rope], axis=-1)
    q, k = rms_norm(q, mla_qn), rms_norm(k, mla_kn)
    q = jnp.concatenate([q[..., :MLA_NOPE], apply_rope(q[..., MLA_NOPE:], positions)], axis=-1)
    k = jnp.concatenate([k[..., :MLA_NOPE], apply_rope(k[..., MLA_NOPE:], positions)], axis=-1)
    o_a = dense_causal_attention(q, k, v_a)

    qkv = u_dil.reshape(b, s, 3, DIL_GROUPS, DIL_HEADS, HEAD_DIM)
    qd = apply_rope(rms_norm(qkv[:, :, 0], dil_qn), positions)
    kd = apply_rope(rms_norm(qkv[:, :, 1], dil_kn), positions)
    o_b = dilated_mixture(qd, kd, qkv[:, :, 2])

    o = jnp.concatenate([o_a.reshape(b, s, -1), o_b.reshape(b, s, -1)], axis=-1)
    return o @ w_out

def odd_mixer(h, positions, w_in, w_out, diff_qn, diff_kn, diff_lambda, diff_subln,
              moba_qn, moba_kn, lam_init):
    b, s, _ = h.shape
    u = h @ w_in
    nqk = DIFF_HEADS * 2 * DIFF_DIM

    qc = u[..., :nqk].reshape(b, s, DIFF_HEADS, 2, DIFF_DIM)
    kc = u[..., nqk:2 * nqk].reshape(b, s, DIFF_HEADS, 2, DIFF_DIM)
    vc = u[..., 2 * nqk:3 * nqk].reshape(b, s, DIFF_HEADS, 2 * DIFF_DIM)
    qc = apply_rope(rms_norm(qc, diff_qn), positions)
    kc = apply_rope(rms_norm(kc, diff_kn), positions)
    lv = diff_lambda.astype(jnp.float32)
    lam = jnp.exp(jnp.sum(lv[0] * lv[1])) - jnp.exp(jnp.sum(lv[2] * lv[3])) + lam_init
    o_c = diff_causal_attention(qc, kc, vc, lam)
    o_c = rms_norm(o_c, diff_subln) * (1.0 - lam_init)

    m = u[..., 3 * nqk:].reshape(b, s, 3, MOBA_HEADS, HEAD_DIM)
    qm = apply_rope(rms_norm(m[:, :, 0], moba_qn), positions)
    km = apply_rope(rms_norm(m[:, :, 1], moba_kn), positions)
    o_d = moba_attention(qm, km, m[:, :, 2])

    o = jnp.concatenate([o_c.reshape(b, s, -1), o_d.reshape(b, s, -1)], axis=-1)
    return o @ w_out

def squared_relu_mlp(h, w1, w2):
    a = jax.nn.relu(h @ w1)
    return (a * a) @ w2

def modulate(xn, shift, scale):
    return xn * (1.0 + scale[:, None, :]) + shift[:, None, :]

def first_inputs(seed: int = 0) -> dict:
    key = jax.random.key(seed)
    ks = jax.random.split(key, 27)
    f32 = jnp.float32

    def nrm(k, shape, scale):
        return jax.random.normal(k, shape, f32) * scale

    def gain(k, shape):
        return 1.0 + 0.1 * jax.random.normal(k, shape, f32)

    offset = jax.random.randint(ks[2], (BATCH, 1), 0, MAX_POS_OFFSET, dtype=jnp.int32)
    positions = offset + jnp.arange(SEQ, dtype=jnp.int32)[None, :]
    return {
        "x": nrm(ks[0], (BATCH, SEQ, D_MODEL), 1.0),
        "c": nrm(ks[1], (BATCH, D_MODEL), 1.0),
        "positions": positions,
        "ada_w": nrm(ks[3], (DEPTH, D_MODEL, 6 * D_MODEL), 0.5 * D_MODEL ** -0.5),
        "ada_b": nrm(ks[4], (DEPTH, 6 * D_MODEL), 0.02),
        "norm_mix": gain(ks[5], (DEPTH, D_MODEL)),
        "norm_mlp": gain(ks[6], (DEPTH, D_MODEL)),
        "mlp_w1": nrm(ks[7], (DEPTH, D_MODEL, D_FF), D_MODEL ** -0.5),
        "mlp_w2": nrm(ks[8], (DEPTH, D_FF, D_MODEL), D_FF ** -0.5),
        "even_w_in": nrm(ks[9], (N_EVEN, D_MODEL, EVEN_IN), D_MODEL ** -0.5),
        "even_w_out": nrm(ks[10], (N_EVEN, EVEN_OUT, D_MODEL), EVEN_OUT ** -0.5),
        "mla_q_lat_norm": gain(ks[11], (N_EVEN, MLA_Q_RANK)),
        "mla_kv_lat_norm": gain(ks[12], (N_EVEN, MLA_KV_RANK)),
        "mla_w_uq": nrm(ks[13], (N_EVEN, MLA_Q_RANK, MLA_HEADS, MLA_NOPE + MLA_ROPE), MLA_Q_RANK ** -0.5),
        "mla_w_ukv": nrm(ks[14], (N_EVEN, MLA_KV_RANK, MLA_HEADS, MLA_NOPE + MLA_V), MLA_KV_RANK ** -0.5),
        "mla_q_norm": gain(ks[15], (N_EVEN, MLA_NOPE + MLA_ROPE)),
        "mla_k_norm": gain(ks[16], (N_EVEN, MLA_NOPE + MLA_ROPE)),
        "dil_q_norm": gain(ks[17], (N_EVEN, HEAD_DIM)),
        "dil_k_norm": gain(ks[18], (N_EVEN, HEAD_DIM)),
        "odd_w_in": nrm(ks[19], (N_ODD, D_MODEL, ODD_IN), D_MODEL ** -0.5),
        "odd_w_out": nrm(ks[20], (N_ODD, ODD_OUT, D_MODEL), ODD_OUT ** -0.5),
        "diff_q_norm": gain(ks[21], (N_ODD, DIFF_DIM)),
        "diff_k_norm": gain(ks[22], (N_ODD, DIFF_DIM)),
        "diff_lambda": nrm(ks[23], (N_ODD, 4, DIFF_DIM), 0.1),
        "diff_subln": gain(ks[24], (N_ODD, 2 * DIFF_DIM)),
        "moba_q_norm": gain(ks[25], (N_ODD, HEAD_DIM)),
        "moba_k_norm": gain(ks[26], (N_ODD, HEAD_DIM)),
    }

def first_block(x, c, positions, ada_w, ada_b, norm_mix, norm_mlp, mlp_w1, mlp_w2,
              even_w_in, even_w_out, mla_q_lat_norm, mla_kv_lat_norm, mla_w_uq, mla_w_ukv,
              mla_q_norm, mla_k_norm, dil_q_norm, dil_k_norm,
              odd_w_in, odd_w_out, diff_q_norm, diff_k_norm, diff_lambda, diff_subln,
              moba_q_norm, moba_k_norm):
    cond = jax.nn.silu(c.astype(jnp.float32)).astype(x.dtype)
    for layer in range(DEPTH):
        mod = cond @ ada_w[layer] + ada_b[layer]
        sh1, sc1, g1, sh2, sc2, g2 = jnp.split(mod, 6, axis=-1)
        h = modulate(rms_norm(x, norm_mix[layer]), sh1, sc1)
        i = layer // 2
        if layer % 2 == 0:
            y = even_mixer(h, positions, even_w_in[i], even_w_out[i], mla_q_lat_norm[i],
                           mla_kv_lat_norm[i], mla_w_uq[i], mla_w_ukv[i], mla_q_norm[i],
                           mla_k_norm[i], dil_q_norm[i], dil_k_norm[i])
        else:
            lam_init = 0.8 - 0.6 * math.exp(-0.3 * layer)
            y = odd_mixer(h, positions, odd_w_in[i], odd_w_out[i], diff_q_norm[i], diff_k_norm[i],
                          diff_lambda[i], diff_subln[i], moba_q_norm[i], moba_k_norm[i], lam_init)
        x = x + g1[:, None, :] * y
        h = modulate(rms_norm(x, norm_mlp[layer]), sh2, sc2)
        x = x + g2[:, None, :] * squared_relu_mlp(h, mlp_w1[layer], mlp_w2[layer])
    return x


DEPTH_2 = 1

GRID_W = 64
CTX_LEN = 256
MIX_WIDTH = D_MODEL // 2
GQA_HEADS = MIX_WIDTH // HEAD_DIM
GQA_KV_HEADS = GQA_HEADS // 4
NA_HEADS = MIX_WIDTH // HEAD_DIM
NA_WIN_ROWS = 8
NA_WIN_COLS = 16
FOURIER_WIDTH = MIX_WIDTH
FOURIER_GROUPS = 4
FOURIER_GROUP_DIM = FOURIER_WIDTH // FOURIER_GROUPS
CONV_WIDTH = MIX_WIDTH
CONV_KERNEL = 31
N_BRANCHES = 4
N_EXPERTS = 16
N_EXPERT_GROUPS = 4
EXPERTS_PER_GROUP = N_EXPERTS // N_EXPERT_GROUPS
TOP_K = 2
EXPERT_FF = D_MODEL // 2
EPS = 1e-6
ATTN_SCALE = HEAD_DIM ** -0.5

GQA_Q_WIDTH = GQA_HEADS * HEAD_DIM
GQA_KV_WIDTH = GQA_KV_HEADS * HEAD_DIM
NA_WIDTH = NA_HEADS * HEAD_DIM
PROJ_SIZES = (GQA_Q_WIDTH, GQA_KV_WIDTH, GQA_KV_WIDTH, NA_WIDTH, NA_WIDTH, NA_WIDTH,
              FOURIER_WIDTH, 2 * CONV_WIDTH, N_BRANCHES * D_MODEL)
PROJ_SPLITS = tuple(int(v) for v in np.cumsum(PROJ_SIZES)[:-1])
IN_WIDTH = sum(PROJ_SIZES)


def rms_norm_2(x, g):
    xf = x.astype(jnp.float32)
    y = xf * lax.rsqrt(jnp.mean(xf * xf, axis=-1, keepdims=True) + EPS)
    return (y * g.astype(jnp.float32)).astype(x.dtype)

def axial_rope(n_tokens):
    t = jnp.arange(n_tokens, dtype=jnp.int32)
    row = (t // GRID_W).astype(jnp.float32)
    col = (t % GRID_W).astype(jnp.float32)
    n_pairs = HEAD_DIM // 4
    inv_freq = ROPE_THETA ** (-jnp.arange(n_pairs, dtype=jnp.float32) / n_pairs)
    ang = jnp.concatenate([row[:, None] * inv_freq, col[:, None] * inv_freq], axis=-1)
    return jnp.cos(ang), jnp.sin(ang)

def apply_rope_2(x, cos, sin):
    xf = x.astype(jnp.float32).reshape(*x.shape[:-1], HEAD_DIM // 2, 2)
    x1, x2 = xf[..., 0], xf[..., 1]
    c = cos[None, :, None, :]
    s = sin[None, :, None, :]
    return jnp.stack([x1 * c - x2 * s, x1 * s + x2 * c], axis=-1).reshape(x.shape).astype(x.dtype)

def attend(qg, k, v):
    s = jnp.einsum('bqhgd,bkhd->bhgqk', qg, k, preferred_element_type=jnp.float32) * ATTN_SCALE
    p = jax.nn.softmax(s, axis=-1).astype(v.dtype)
    return jnp.einsum('bhgqk,bkhd->bqhgd', p, v)

def dense_attention(q, k, v):
    B, L, hq, _ = q.shape
    hkv = k.shape[2]
    out = attend(q.reshape(B, L, hkv, hq // hkv, HEAD_DIM), k, v)
    return out.reshape(B, L, hq * HEAD_DIM)

def gqa_latent(q, k, v, k_ctx, v_ctx):
    B, S = q.shape[:2]
    g = GQA_HEADS // GQA_KV_HEADS
    k_all = jnp.concatenate([k, k_ctx], axis=1)
    v_all = jnp.concatenate([v, v_ctx], axis=1)
    nb = S // Q_BLOCK
    qb = q.reshape(B, nb, Q_BLOCK, GQA_KV_HEADS, g, HEAD_DIM).transpose(1, 0, 2, 3, 4, 5)
    out = lax.map(lambda qblk: attend(qblk, k_all, v_all), qb)
    return out.transpose(1, 0, 2, 3, 4, 5).reshape(B, S, GQA_Q_WIDTH)

def neighbourhood_latent(q, k, v, k_ctx, v_ctx, rpb):
    B, S = q.shape[:2]
    rows = S // GRID_W
    wr = min(NA_WIN_ROWS, rows)
    qg = q.reshape(B, rows, GRID_W, NA_HEADS, HEAD_DIM)
    kg = k.reshape(B, rows, GRID_W, NA_HEADS, HEAD_DIM)
    vg = v.reshape(B, rows, GRID_W, NA_HEADS, HEAD_DIM)
    cols = np.arange(GRID_W)
    col_start = np.clip(cols - NA_WIN_COLS // 2, 0, GRID_W - NA_WIN_COLS)
    col_idx = col_start[:, None] + np.arange(NA_WIN_COLS)[None, :]
    col_bias_idx = col_idx - cols[:, None] + (NA_WIN_COLS - 1)
    row_starts = jnp.clip(jnp.arange(rows) - NA_WIN_ROWS // 2, 0, rows - wr)
    rpb_f = rpb.astype(jnp.float32)
    n_win = wr * NA_WIN_COLS

    def row_block(args):
        r, r0, q_row = args
        k_band = lax.dynamic_slice_in_dim(kg, r0, wr, axis=1)
        v_band = lax.dynamic_slice_in_dim(vg, r0, wr, axis=1)
        k_win = k_band[:, :, col_idx]
        v_win = v_band[:, :, col_idx]
        s_win = jnp.einsum('bqhd,bwqjhd->bhqwj', q_row, k_win,
                           preferred_element_type=jnp.float32) * ATTN_SCALE
        row_bias_idx = r0 + jnp.arange(wr) - r + (NA_WIN_ROWS - 1)
        bias = rpb_f[:, row_bias_idx][:, :, col_bias_idx]
        s_win = s_win + bias.transpose(0, 2, 1, 3)[None]
        s_ctx = jnp.einsum('bqhd,bkhd->bhqk', q_row, k_ctx,
                           preferred_element_type=jnp.float32) * ATTN_SCALE
        s = jnp.concatenate([s_win.reshape(B, NA_HEADS, GRID_W, n_win), s_ctx], axis=-1)
        p = jax.nn.softmax(s, axis=-1).astype(v.dtype)
        p_win = p[..., :n_win].reshape(B, NA_HEADS, GRID_W, wr, NA_WIN_COLS)
        p_ctx = p[..., n_win:]
        return (jnp.einsum('bhqwj,bwqjhd->bqhd', p_win, v_win)
                + jnp.einsum('bhqk,bkhd->bqhd', p_ctx, v_ctx))

    out = lax.map(row_block, (jnp.arange(rows), row_starts, qg.transpose(1, 0, 2, 3, 4)))
    return out.transpose(1, 0, 2, 3, 4).reshape(B, S, NA_WIDTH)

def fourier_mix(u):
    B, L = u.shape[:2]
    ug = u.astype(jnp.float32).reshape(B, L, FOURIER_GROUPS, FOURIER_GROUP_DIM)
    y = jnp.fft.fft2(ug, axes=(1, 3), norm='ortho').real
    return y.reshape(B, L, FOURIER_WIDTH).astype(u.dtype)

def conformer_conv(u, conv_w, conv_b, conv_g):
    a, b = jnp.split(u, 2, axis=-1)
    z = a * jax.nn.sigmoid(b)
    z = lax.conv_general_dilated(z, conv_w[:, None, :], window_strides=(1,),
                                 padding=[(CONV_KERNEL // 2, CONV_KERNEL // 2)],
                                 dimension_numbers=('NWC', 'WIO', 'NWC'),
                                 feature_group_count=CONV_WIDTH) + conv_b
    return jax.nn.silu(rms_norm_2(z, conv_g))

def merge_branches(branches, gate_logits, w_branch, w_out):
    y = jnp.stack(branches, axis=-2)
    z = jnp.einsum('blnc,ncd->blnd', y, w_branch)
    g = jax.nn.sigmoid(gate_logits.reshape(*gate_logits.shape[:-1], N_BRANCHES, D_MODEL)
                       .astype(jnp.float32)).astype(z.dtype)
    return jnp.sum(g * z, axis=-2) @ w_out

def token_mixer(h, hc, w_in, q_g, k_g, rpb, conv_w, conv_b, conv_g, w_branch, w_out, cos, sin, update_ctx):
    B, S, _ = h.shape
    C = hc.shape[1]
    gq, gk, gv, nq, nk, nv, fu, cu, gl = jnp.split(h @ w_in, PROJ_SPLITS, axis=-1)
    cgq, cgk, cgv, cnq, cnk, cnv, cfu, ccu, cgl = jnp.split(hc @ w_in, PROJ_SPLITS, axis=-1)
    q = apply_rope_2(rms_norm_2(gq.reshape(B, S, GQA_HEADS, HEAD_DIM), q_g), cos, sin)
    k = apply_rope_2(rms_norm_2(gk.reshape(B, S, GQA_KV_HEADS, HEAD_DIM), k_g), cos, sin)
    v = gv.reshape(B, S, GQA_KV_HEADS, HEAD_DIM)
    kc = rms_norm_2(cgk.reshape(B, C, GQA_KV_HEADS, HEAD_DIM), k_g)
    vc = cgv.reshape(B, C, GQA_KV_HEADS, HEAD_DIM)
    y_gqa = gqa_latent(q, k, v, kc, vc)
    nkc = cnk.reshape(B, C, NA_HEADS, HEAD_DIM)
    nvc = cnv.reshape(B, C, NA_HEADS, HEAD_DIM)
    y_na = neighbourhood_latent(nq.reshape(B, S, NA_HEADS, HEAD_DIM), nk.reshape(B, S, NA_HEADS, HEAD_DIM),
                                nv.reshape(B, S, NA_HEADS, HEAD_DIM), nkc, nvc, rpb)
    y_fn = fourier_mix(fu)
    y_cv = conformer_conv(cu, conv_w, conv_b, conv_g)
    out = merge_branches((y_gqa, y_na, y_fn, y_cv), gl, w_branch, w_out)
    if not update_ctx:
        return out, None
    qc = rms_norm_2(cgq.reshape(B, C, GQA_HEADS, HEAD_DIM), q_g)
    yc_gqa = dense_attention(qc, kc, vc)
    yc_na = dense_attention(cnq.reshape(B, C, NA_HEADS, HEAD_DIM), nkc, nvc)
    yc_fn = fourier_mix(cfu)
    yc_cv = conformer_conv(ccu, conv_w, conv_b, conv_g)
    out_c = merge_branches((yc_gqa, yc_na, yc_fn, yc_cv), cgl, w_branch, w_out)
    return out, out_c

def moe(h, w_router, router_bias, w_gu, w_down):
    lead = h.shape[:-1]
    t = h.reshape(-1, D_MODEL)
    scores = jax.nn.sigmoid((t @ w_router).astype(jnp.float32))
    sel = scores + router_bias.astype(jnp.float32)
    group_score = lax.top_k(sel.reshape(-1, N_EXPERT_GROUPS, EXPERTS_PER_GROUP), TOP_K)[0].sum(-1)
    g_idx = jnp.argmax(group_score, axis=-1)
    in_group = (jnp.arange(N_EXPERTS) // EXPERTS_PER_GROUP)[None, :] == g_idx[:, None]
    _, top_idx = lax.top_k(jnp.where(in_group, sel, -jnp.inf), TOP_K)
    w = jnp.take_along_axis(scores, top_idx, axis=-1)
    w = w / jnp.sum(w, axis=-1, keepdims=True)
    gate = jnp.sum(jax.nn.one_hot(top_idx, N_EXPERTS, dtype=jnp.float32) * w[..., None], axis=1).astype(t.dtype)
    out = jnp.zeros_like(t)
    for e in range(N_EXPERTS):
        a, b = jnp.split(t @ w_gu[e], 2, axis=-1)
        out = out + gate[:, e:e + 1] * ((jax.nn.silu(a) * b) @ w_down[e])
    return out.reshape(*lead, D_MODEL)

def second_inputs(seed: int = 0) -> dict:
    key = jax.random.key(seed)
    ks = jax.random.split(key, 22)
    D = D_MODEL

    def nrm(k, shape, std):
        return jax.random.normal(k, shape, jnp.float32) * std

    return {
        "x": nrm(ks[0], (BATCH, SEQ, D), 1.0),
        "c": nrm(ks[1], (BATCH, D), 1.0),
        "ctx": nrm(ks[2], (BATCH, CTX_LEN, D), 1.0),
        "c_ctx": nrm(ks[3], (D,), 1.0),
        "w_mod": nrm(ks[4], (DEPTH_2, D, 6 * D), 0.5 * D ** -0.5),
        "b_mod": nrm(ks[5], (DEPTH_2, 6 * D), 0.02),
        "norm1_g": 1.0 + nrm(ks[6], (DEPTH_2, D), 0.02),
        "norm2_g": 1.0 + nrm(ks[7], (DEPTH_2, D), 0.02),
        "w_in": nrm(ks[8], (DEPTH_2, D, IN_WIDTH), D ** -0.5),
        "q_norm_g": 1.0 + nrm(ks[9], (DEPTH_2, HEAD_DIM), 0.02),
        "k_norm_g": 1.0 + nrm(ks[10], (DEPTH_2, HEAD_DIM), 0.02),
        "na_rpb": nrm(ks[11], (DEPTH_2, NA_HEADS, 2 * NA_WIN_ROWS - 1, 2 * NA_WIN_COLS - 1), 0.02),
        "conv_w": nrm(ks[12], (DEPTH_2, CONV_KERNEL, CONV_WIDTH), CONV_KERNEL ** -0.5),
        "conv_b": nrm(ks[13], (DEPTH_2, CONV_WIDTH), 0.01),
        "conv_norm_g": 1.0 + nrm(ks[14], (DEPTH_2, CONV_WIDTH), 0.02),
        "w_branch": nrm(ks[15], (DEPTH_2, N_BRANCHES, MIX_WIDTH, D), MIX_WIDTH ** -0.5),
        "w_out": nrm(ks[16], (DEPTH_2, D, D), D ** -0.5),
        "w_router": nrm(ks[17], (D, N_EXPERTS), D ** -0.5),
        "router_bias": nrm(ks[18], (N_EXPERTS,), 0.01),
        "w_expert_gu": nrm(ks[19], (DEPTH_2, N_EXPERTS, D, 2 * EXPERT_FF), D ** -0.5),
        "w_expert_down": nrm(ks[20], (DEPTH_2, N_EXPERTS, EXPERT_FF, D), EXPERT_FF ** -0.5),
        "final_norm_g": 1.0 + nrm(ks[21], (D,), 0.02),
    }

def second_block(x, c, ctx, c_ctx, w_mod, b_mod, norm1_g, norm2_g, w_in, q_norm_g, k_norm_g, na_rpb,
              conv_w, conv_b, conv_norm_g, w_branch, w_out, w_router, router_bias,
              w_expert_gu, w_expert_down, final_norm_g):
    S = x.shape[1]
    cos, sin = axial_rope(S)
    xc = ctx
    for l in range(DEPTH_2):
        update_ctx = l < DEPTH_2 - 1
        m = jax.nn.silu(c) @ w_mod[l] + b_mod[l]
        sh1, sc1, g1, sh2, sc2, g2 = [t[:, None, :] for t in jnp.split(m, 6, axis=-1)]
        mc = jax.nn.silu(c_ctx) @ w_mod[l] + b_mod[l]
        csh1, csc1, cg1, csh2, csc2, cg2 = jnp.split(mc, 6, axis=-1)
        h = rms_norm_2(x, norm1_g[l]) * (1.0 + sc1) + sh1
        hc = rms_norm_2(xc, norm1_g[l]) * (1.0 + csc1) + csh1
        y, yc = token_mixer(h, hc, w_in[l], q_norm_g[l], k_norm_g[l], na_rpb[l], conv_w[l], conv_b[l],
                            conv_norm_g[l], w_branch[l], w_out[l], cos, sin, update_ctx)
        x = x + g1 * y
        h2 = rms_norm_2(x, norm2_g[l]) * (1.0 + sc2) + sh2
        if update_ctx:
            xc = xc + cg1 * yc
            h2c = rms_norm_2(xc, norm2_g[l]) * (1.0 + csc2) + csh2
            z = moe(jnp.concatenate([h2, h2c], axis=1), w_router, router_bias, w_expert_gu[l], w_expert_down[l])
            x = x + g2 * z[:, :S]
            xc = xc + cg2 * z[:, S:]
        else:
            x = x + g2 * moe(h2, w_router, router_bias, w_expert_gu[l], w_expert_down[l])
    return rms_norm_2(x, final_norm_g)


def setup_inputs(seed=0):
    out = dict(first_inputs(seed))
    for name, value in second_inputs(seed + 1).items():
        if name != "x":
            out[name + "_2"] = value
    return out


def reference(
    x, c, positions, ada_w, ada_b, norm_mix, norm_mlp, mlp_w1, mlp_w2, even_w_in, even_w_out,
    mla_q_lat_norm, mla_kv_lat_norm, mla_w_uq, mla_w_ukv, mla_q_norm, mla_k_norm, dil_q_norm,
    dil_k_norm, odd_w_in, odd_w_out, diff_q_norm, diff_k_norm, diff_lambda, diff_subln,
    moba_q_norm, moba_k_norm, c_2, ctx_2, c_ctx_2, w_mod_2, b_mod_2, norm1_g_2, norm2_g_2,
    w_in_2, q_norm_g_2, k_norm_g_2, na_rpb_2, conv_w_2, conv_b_2, conv_norm_g_2, w_branch_2,
    w_out_2, w_router_2, router_bias_2, w_expert_gu_2, w_expert_down_2, final_norm_g_2,
):
    x = first_block(
        x, c, positions, ada_w, ada_b, norm_mix, norm_mlp, mlp_w1, mlp_w2, even_w_in,
        even_w_out, mla_q_lat_norm, mla_kv_lat_norm, mla_w_uq, mla_w_ukv, mla_q_norm,
        mla_k_norm, dil_q_norm, dil_k_norm, odd_w_in, odd_w_out, diff_q_norm, diff_k_norm,
        diff_lambda, diff_subln, moba_q_norm, moba_k_norm,
    )
    return second_block(
        x, c_2, ctx_2, c_ctx_2, w_mod_2, b_mod_2, norm1_g_2, norm2_g_2, w_in_2, q_norm_g_2,
        k_norm_g_2, na_rpb_2, conv_w_2, conv_b_2, conv_norm_g_2, w_branch_2, w_out_2,
        w_router_2, router_bias_2, w_expert_gu_2, w_expert_down_2, final_norm_g_2,
    )


_drawn_inputs = setup_inputs


def setup_inputs(seed=0):
    import zlib

    import numpy as np

    out = dict(_drawn_inputs(seed))
    spreads = {}
    factors = {'mla_q_lat_norm': 8.0,
     'mla_kv_lat_norm': 5.971,
     'mla_q_norm': 6.568,
     'mla_k_norm': 5.599,
     'dil_q_norm': 8.0,
     'dil_k_norm': 8.0,
     'diff_q_norm': 4.539,
     'diff_k_norm': 8.0,
     'diff_subln': 3.087,
     'moba_q_norm': 8.0,
     'moba_k_norm': 8.0,
     'norm1_g_2': 8.0,
     'q_norm_g_2': 8.0,
     'k_norm_g_2': 8.0,
     'na_rpb_2': 64.0,
     'conv_b_2': 64.0,
     'conv_norm_g_2': 62.477,
     'final_norm_g_2': 8.284,
     'norm2_g_2': 8.0,
     'router_bias_2': 4.167}
    for name, (base, spread) in spreads.items():
        noise = np.random.default_rng([zlib.crc32(name.encode()), seed]).standard_normal(out[name].shape)
        drawn = base * np.exp(spread * noise) if base else spread * noise
        out[name] = __import__('jax').numpy.asarray(drawn.astype(out[name].dtype))
    for name, factor in factors.items():
        out[name] = (out[name] * factor).astype(out[name].dtype)
    return out
```

```python
from contextlib import ExitStack

import numpy as np

import concourse.bass as bass
from concourse import mybir

F32 = mybir.dt.float32
I32 = mybir.dt.int32
ALU = mybir.AluOpType
ACT = mybir.ActivationFunctionType
AX = mybir.AxisListType.X

P = 128
D = 1024
SEQ = 256
KT = D // P
TT = SEQ // P
W = 512
FF = 4 * D
HD = 64
EPS = 1e-6
NEG = -1e30
QR, KVR, NOPE, ROPE, MH = 384, 256, 64, 32, 8
QKD = NOPE + ROPE
DIL = ((128, 1), (512, 4), (2048, 16))
DG, DH = 3, 4
E_IN = QR + KVR + ROPE + 3 * DG * DH * HD
E_OUT = MH * HD + DH * HD
O_IN = 6 * 512
NEXP, EFF = 16, 512
GATE0 = 3840
TAPS = 31
PADT = SEQ + TAPS - 1
LAM_INIT = 0.8 - 0.6 * float(np.exp(-0.3))
RING = 4
SLOT = KT * W
TWO_PI = 2.0 * float(np.pi)
PI_LO = 3.1415925

CONSTS = (("ident", 128), ("c0", 128), ("c1", 256), ("d0", 384), ("d1", 768), ("na", 512), ("ax", 128),
          ("invf", 48), ("tri", 16))
DFT = (("CL", 512), ("SL", 512), ("CD", 128), ("SD", 128))
COLS = (("c", 24), ("adab", 144), ("nmix", 16), ("nmlp", 16), ("n1", 8), ("n2", 8), ("qlat", 3), ("kvlat", 2),
        ("subln", 1), ("convw", 124), ("convb", 4), ("convg", 4))
ROWS = (("mlaq", 96), ("mlak", 96), ("dilq", 64), ("dilk", 64), ("diffq", 64), ("diffk", 64), ("mobaq", 64),
        ("mobak", 64), ("gqaq", 64), ("gqak", 64), ("lam", 256), ("rbias", 16))


def offsets(parts):
    at, out = 0, {}
    for name, n in parts:
        out[name] = (at, at + n)
        at += n
    return out, at


def shape_constants():
    out = {"ident": np.eye(P)}
    q, k = np.arange(SEQ)[:, None], np.arange(SEQ)[None, :]
    neg = lambda keep: np.where(keep, 0.0, NEG)
    causal = neg(q >= k)
    out["c0"], out["c1"] = causal[:P, :P], causal[P:]
    dil = [neg((q >= k) & ((q - k) % r == 0) & (q - k <= w)) for w, r in DIL]
    out["d0"] = np.concatenate([m[:P, :P] for m in dil], 1)
    out["d1"] = np.concatenate([m[P:] for m in dil], 1)
    qc, kc = q % 64, k % 64
    start = np.clip(qc - 8, 0, 48)
    na = neg((kc >= start) & (kc < start + 16))
    out["na"] = np.concatenate([na[:P], na[P:]], 1)
    t = np.arange(SEQ)
    f = np.float32(10000.0) ** (-np.arange(16, dtype=np.float32) / np.float32(16))
    f32_ = np.float32(10000.0) ** (-np.arange(32, dtype=np.float32) / np.float32(32))
    ang = np.concatenate([(t // 64).astype(np.float32)[:, None] * f, (t % 64).astype(np.float32)[:, None] * f], 1)
    cs, sn = np.cos(ang.astype(np.float64)), np.sin(ang.astype(np.float64))
    out["ax"] = np.concatenate([cs[:P], cs[P:], sn[:P], sn[P:]], 1)
    out["invf"] = np.tile(np.concatenate([f, f32_])[None], (P, 1))
    out["tri"] = np.tile((np.arange(4)[None, :] < np.arange(4)[:, None]).astype(np.float32).reshape(1, 16), (P, 1))
    al = 2 * np.pi * ((q * k) % SEQ) / SEQ
    tiles = lambda m: m.reshape(TT, P, SEQ).transpose(1, 0, 2).reshape(P, -1)
    out["CL"], out["SL"] = tiles(np.cos(al)), tiles(np.sin(al))
    d = np.arange(P)
    ad = 2 * np.pi * ((d[:, None] * d[None, :]) % P) / P
    norm = 1.0 / np.sqrt(SEQ * P)
    out["CD"], out["SD"] = np.cos(ad) * norm, -np.sin(ad) * norm
    return [np.ascontiguousarray(np.concatenate([out[n] for n, _ in part], 1).astype(np.float32)) for part in (CONSTS, DFT)]


def weight_stream(t):
    S = []

    def add(name, src, k, n):
        S.append((name, src.rearrange("(k p) n -> p k n", p=P), k, n))

    def mod(l, j):
        w = t["ada_w"][l] if l < 2 else t["w_mod_2"][0]
        add(("mod", l, j), w[:, j * W:(j + 1) * W], KT, W)

    for j in range(4):
        mod(0, j)
    for i in range(6):
        n = min(W, E_IN - i * W)
        add(("ein", i), t["even_w_in"][0][:, i * W:i * W + n], KT, n)
        mod(0, 4 + i)
    mod(0, 10)
    mod(0, 11)
    add(("uq",), t["mla_w_uq"][0].rearrange("r h d -> r (h d)"), 3, 768)
    add(("ukv",), t["mla_w_ukv"][0].rearrange("r h d -> r (h d)"), 2, 1024)
    for n in range(2):
        add(("eout", n), t["even_w_out"][0][:, n * W:(n + 1) * W], 6, W)

    def mlp(l):
        for j in range(FF // W):
            add(("w1", l, j), t["mlp_w1"][l][:, j * W:(j + 1) * W], KT, W)
            for m in mod_in_mlp(j):
                mod(l + 1, m)
            add(("w2", l, j), t["mlp_w2"][l][j * W:(j + 1) * W, :], 4, D)

    mlp(0)
    for i in range(6):
        add(("oin", i), t["odd_w_in"][0][:, i * W:(i + 1) * W], KT, W)
    for n in range(2):
        add(("oout", n), t["odd_w_out"][0][:, n * W:(n + 1) * W], KT, W)
    mlp(1)
    for i, (a, n) in enumerate(IN2):
        add(("in2", i), t["w_in_2"][0][:, a:a + n], KT, n)
    for b in range(4):
        add(("gate", 2 * b), t["w_in_2"][0][:, GATE0 + 2 * b * W:GATE0 + (2 * b + 1) * W], KT, W)
        add(("branch", b), t["w_branch_2"][0, b], 4, D)
        add(("gate", 2 * b + 1), t["w_in_2"][0][:, GATE0 + (2 * b + 1) * W:GATE0 + (2 * b + 2) * W], KT, W)
    for n in range(2):
        add(("out2", n), t["w_out_2"][0][:, n * W:(n + 1) * W], KT, W)
    return S


def mod_in_mlp(j):
    return (2 * j, 2 * j + 1) if j < 6 else ()


IN2 = ((0, 512), (512, 256), (768, 512), (1280, 512), (1792, 512), (2304, 512), (2816, 512), (3328, 512))
CTX_AT = {1: 0, 3: 256, 4: 768}
MODSEQ = [(0, j) for j in range(12)] + [(1, j) for j in range(12)]
for _j in range(12):
    MODSEQ += [(2, _j)] + ([(3, _j)] if _j < 4 else [])


def spread(ap, dim, n):
    ap = ap.unsqueeze(dim)
    shape = list(ap.shape)
    shape[dim] = n
    return ap.broadcast_to(shape)


def units():
    out = []
    for ph, heads in (("mla", MH), ("dil", DH), ("diff", 4), ("moba", 8), ("gqa", 8), ("na", 8)):
        out += [(ph, h, t) for h in range(heads) for t in range(TT)]
    return out


def program(nc, t, out):
    stream = weight_stream(t)
    number = {s[0]: n for n, s in enumerate(stream)}
    NSTREAM = len(stream)
    CO, NCO = offsets(CONSTS)
    CC, NCC = offsets(COLS)
    CR, NCR = offsets(ROWS)
    UNITS = units()
    ctx = ExitStack()
    with ctx:
        def sb(name, n, dt=F32):
            return ctx.enter_context(nc.sbuf_tensor(name, [P, n], dt))

        sems = {}

        def S(name):
            if name not in sems:
                sems[name] = ctx.enter_context(nc.semaphore(name))
            return sems[name]

        ring = sb("ring", RING * SLOT)
        consts = sb("consts", NCO)
        cols = sb("cols", NCC)
        rows = sb("rows", NCR)
        X = sb("X", TT * D)[:, :].rearrange("p (t n) -> p t n", t=TT)
        hTb = sb("hT", KT * SEQ)
        hT = hTb[:, :].rearrange("p (k n) -> p k n", k=KT)
        U = sb("U", 6144)
        AUX = sb("AUX", 4608)
        QK = sb("QK", 4608)
        OTb = sb("OT", KT * SEQ)
        OT = OTb[:, :].rearrange("p (k n) -> p k n", k=KT)
        G = sb("G", 4 * D)[:, :].rearrange("p (s n) -> p s n", s=4)
        Eb = sb("E", 3 * 768)[:, :].rearrange("p (s n) -> p s n", s=3)
        PTb = sb("PT", 2 * 768)[:, :].rearrange("p (s n) -> p s n", s=2)
        scratch = sb("scratch", 4 * W)
        acc = scratch[:, 0:2 * W].rearrange("p (s n) -> p s n", s=2)
        tmp = scratch[:, 2 * W:4 * W].rearrange("p (s n) -> p s n", s=2)
        nab = scratch[:, :].rearrange("p (s t n) -> p s t n", s=2, t=2)
        ones = sb("ones", P)
        zero = sb("zero", 1)
        cond = sb("cond", 24)
        modc = sb("modc", 4 * 48)[:, :].rearrange("p (l v k) -> p l v k", l=4, v=6)
        coef = sb("coef", 8 * 8)[:, :].rearrange("p (i k) -> p i k", i=8)
        ss = sb("ss", 32)
        wn = sb("wn", 3 * 256)[:, :].rearrange("p (s n) -> p s n", s=3)
        rope = sb("rope", 2 * 2 * 48)
        posi = sb("posi", 2, I32)
        posf = sb("posf", 2)
        mx = sb("mx", 3 * 2)[:, :].rearrange("p (s n) -> p s n", s=3)
        sm = sb("sm", 3 * 2)[:, :].rearrange("p (s n) -> p s n", s=3)
        rc = sb("rc", 3 * 2)[:, :].rearrange("p (s n) -> p s n", s=3)
        lam = sb("lam", 8)
        moe = QK[:, 0:640]
        rw = moe[:, 0:480].rearrange("p (s n) -> p s n", s=5)
        wrt = sb("wrt", KT * NEXP)
        ps = ctx.enter_context(nc.psum_tensor("ps", [P, 8, W], F32))

        DF, NDFT = offsets(DFT)
        dft_at = CO["c0"][0]
        assert CO["d1"][1] - dft_at >= NDFT
        dft = lambda n: consts[:, dft_at + DF[n][0]:dft_at + DF[n][1]]
        con = lambda n: consts[:, CO[n][0]:CO[n][1]]
        col = lambda n: cols[:, CC[n][0]:CC[n][1]]
        row = lambda n: rows[:, CR[n][0]:CR[n][1]]
        ident = con("ident")
        Cos = rope[:, 0:96].rearrange("p (t n) -> p t n", t=2)
        Sin = rope[:, 96:192].rearrange("p (t n) -> p t n", t=2)
        axcs = con("ax")[:, 0:64].rearrange("p (t n) -> p t n", t=2)
        axsn = con("ax")[:, 64:128].rearrange("p (t n) -> p t n", t=2)

        Ue = U[:, 0:2 * E_IN].rearrange("p (t n) -> p t n", t=2)
        Uo = U[:, :].rearrange("p (t n) -> p t n", t=2)
        U2 = U[:, 0:2 * 2816].rearrange("p (t n) -> p t n", t=2)
        Qm = AUX[:, 0:1536].rearrange("p (t h d) -> p t h d", t=2, h=MH)
        Km = AUX[:, 1536:3072].rearrange("p (t h d) -> p t h d", t=2, h=MH)
        Vm = AUX[:, 3072:4096].rearrange("p (t h d) -> p t h d", t=2, h=MH)
        work = PTb.rearrange("p s n -> p (s n)")[:, 0:1024]
        cT = hTb[:, 0:5 * SEQ].rearrange("p (k n) -> p k n", k=5)
        hc = AUX[:, 0:2048].rearrange("p (k n) -> p k n", k=KT)
        ctx_x = QK[:, 0:2048].rearrange("p (t n) -> p t n", t=2)
        xs = Eb.rearrange("p s n -> p (s n)")[:, 0:2048].rearrange("p (t n) -> p t n", t=2)
        Uc = AUX[:, 2048:4608].rearrange("p (t n) -> p t n", t=2)
        work2 = work
        zp = PTb.rearrange("p s n -> p (s n)")[:, 0:4 * PADT].rearrange("p (c n) -> p c n", c=4)
        HT = U[:, 0:2048].rearrange("p (s k n) -> p s k n", s=2, k=4)
        M2 = U[:, 0:2048].rearrange("p (k n) -> p k n", k=KT)
        YF = AUX[:, 0:1024].rearrange("p (k n) -> p k n", k=4)
        YC = AUX[:, 1024:2048].rearrange("p (k n) -> p k n", k=4)
        Z12 = QK[:, 0:2048].rearrange("p (g n) -> p g n", g=4)
        convy = YC
        convs = QK[:, 2048:3072].rearrange("p (k n) -> p k n", k=4)
        accY = AUX[:, 0:2048].rearrange("p (t n) -> p t n", t=2)

        def chunk(name):
            n = number[name]
            _, _, k, w = stream[n]
            s = n % RING
            return ring[:, s * SLOT:s * SLOT + k * w].rearrange("p (k n) -> p k n", k=k)

        def arrived(eng, name):
            n = number[name]
            eng.wait_ge(S(f"loaded{n % RING}"), 16 * (n // RING + 1))
            return chunk(name)

        def last_use(name):
            kind = name[0]
            if kind == "mod":
                return S("mod_acc"), 1 + max(q for q, (l, j) in enumerate(MODSEQ) if (min(l, 2), j) == name[1:])
            if kind in ("eout", "oout", "out2"):
                return S("res"), 4 * {"eout": 0, "oout": 2, "out2": 4}[kind] + 2 * name[1] + 2
            if kind == "w1":
                return S("hid"), 32 * name[1] + 4 * name[2] + 4
            if kind == "w2":
                l, j = name[1:]
                return (S("res"), 8 * l + 8) if j == 7 else (S("w2_used"), 7 * l + j + 1)
            if kind == "gate":
                return S("merge"), 4 * name[1] + 4
            if kind == "branch":
                return S("merge"), 8 * name[1] + 8
            if kind == "in2" and name[1] >= 6:
                return S("glu"), 4
            ph = {"uq": "lat", "ukv": "lat"}.get(kind, kind)
            return S("proj"), g0[ph] + 1 + max(j for j, g in enumerate(groups(ph)) if g[0] == name)

        loads_of = [len(range(s, NSTREAM, RING)) for s in range(RING)]

        def last_in(s):
            return stream[max(range(s, NSTREAM, RING))][0]

        def qkt(off, tiles):
            return QK[:, off:off + tiles * SEQ].rearrange("p (k n) -> p k n", k=tiles)

        mlaQ, mlaK = qkt(0, 8), qkt(2048, 8)
        dilQ, dilK = qkt(0, 6), qkt(1536, 6)
        diffQ, diffK, mobaQ, mobaK = qkt(0, 4), qkt(1024, 4), qkt(2048, 4), qkt(3072, 4)
        gqaQ, gqaK, gqaC = qkt(0, 4), qkt(1024, 1), qkt(1280, 1)
        naQ, naK, naC = qkt(1536, 4), qkt(2560, 4), qkt(3584, 4)

        def half(ap, h, a, n):
            return ap[64 * (h % 2):64 * (h % 2) + 64, h // 2, a:a + n]

        def scores_of(u):
            ph, h, t = u
            nk = P * (t + 1)
            q0 = P * t
            if ph == "mla":
                return [(0, mlaQ[0:QKD, h, q0:q0 + P], mlaK[0:QKD, h, 0:nk], nk)]
            if ph == "dil":
                return [(g * nk, half(dilQ, g * DH + h, q0, P), half(dilK, g * DH + h, 0, nk), nk) for g in range(DG)]
            if ph == "diff":
                return [(m * W, half(diffQ, 2 * h + m, q0, P), half(diffK, 2 * h + m, 0, nk), nk) for m in range(2)]
            if ph == "moba":
                return [(0, half(mobaQ, h, q0, P), half(mobaK, h, 0, nk), nk)]
            if ph == "gqa":
                r = 64 * (h // 4)
                q = gqaQ[r:r + 64, h % 4, q0:q0 + P]
                return [(0, q, gqaK[r:r + 64, 0, :], SEQ), (SEQ, q, gqaC[r:r + 64, 0, :], SEQ)]
            q = half(naQ, h, q0, P)
            return [(0, q, half(naK, h, 0, SEQ), SEQ), (SEQ, q, half(naC, h, 0, SEQ), SEQ)]

        def softmax_of(u):
            ph, h, t = u
            nk = P * (t + 1)
            if ph == "dil":
                return [(0, DG * nk, con(f"d{t}"))]
            if ph == "diff":
                return [(m * nk, nk, con(f"c{t}")) for m in range(2)]
            if ph in ("mla", "moba"):
                return [(0, nk, con(f"c{t}"))]
            if ph == "gqa":
                return [(0, 2 * SEQ, zero[:, :].broadcast_to([P, W]))]
            return [(0, 2 * SEQ, nab[:, h % 2, t, :])]

        def values_of(u):
            ph, h, t = u
            kb = range(t + 1)
            if ph == "mla":
                return [Vm[:, b, h, :] for b in kb]
            if ph == "dil":
                v0 = QR + KVR + ROPE + 2 * DG * DH * HD
                return [Ue[:, b, v0 + (g * DH + h) * HD:v0 + (g * DH + h + 1) * HD] for g in range(DG) for b in kb]
            if ph == "diff":
                return [Uo[:, b, 1024 + h * P:1024 + (h + 1) * P] for b in kb]
            if ph == "moba":
                return [Uo[:, b, 2560 + h * HD:2560 + (h + 1) * HD] for b in kb]
            if ph == "gqa":
                g = h // 4
                return ([U2[:, b, 640 + g * HD:640 + (g + 1) * HD] for b in range(2)]
                        + [Uc[:, b, 128 + g * HD:128 + (g + 1) * HD] for b in range(2)])
            return ([U2[:, b, 1792 + h * HD:1792 + (h + 1) * HD] for b in range(2)]
                    + [Uc[:, b, 768 + h * HD:768 + (h + 1) * HD] for b in range(2)])

        def output_of(u):
            ph, h, t = u
            if ph == "diff":
                return 0, P, OT[:, h, P * t:P * t + P]
            r = 64 * (h % 2)
            k = {"mla": 0, "dil": 4, "moba": 4, "gqa": 0, "na": 4}[ph] + h // 2
            return r, 64, OT[r:r + 64, k, P * t:P * t + P]

        def wide(u):
            return u[0] == "dil"

        def pt_bank(i):
            b = 4 if wide(UNITS[i]) else 4 + i % 2
            return ps[:, b:b + 2, :].rearrange("p b n -> p (b n)") if wide(UNITS[i]) else ps[:, b, :]

        def s_bank(i):
            return ps[:, 2 * (i % 2):2 * (i % 2) + 2, :].rearrange("p b n -> p (b n)")

        def span(ph):
            ids = [i for i, u in enumerate(UNITS) if u[0] == ph]
            return ids[0], ids[-1] + 1

        def tr_list(ph):
            o = QR + KVR + ROPE
            if ph == "mla":
                return [(lambda t, h=h: Qm[:, t, h, :], mlaQ[0:QKD, h, :]) for h in range(MH)] \
                    + [(lambda t, h=h: Km[:, t, h, :], mlaK[0:QKD, h, :]) for h in range(MH)]
            if ph == "dil":
                return [(lambda t, k=k: Ue[:, t, o + k * P:o + (k + 1) * P],
                         (dilQ[:, k, :] if k < 6 else dilK[:, k - 6, :])) for k in range(12)]
            if ph == "odd":
                dst = [diffQ, diffK, None, mobaQ, mobaK]
                return [(lambda t, c=c, k=k: Uo[:, t, c * 512 + k * P:c * 512 + (k + 1) * P], dst[c][:, k, :])
                        for c in (0, 1, 3, 4) for k in range(4)]
            out_ = []
            for j in range(4):
                out_.append((lambda t, j=j: gq_pairs[:, t, j, :], gqaQ[:, j, :]))
            out_.append((lambda t: U2[:, t, 512:640], gqaK[:, 0, :]))
            out_.append((lambda t: Uc[:, t, 0:128], gqaC[:, 0, :]))
            for k in range(4):
                out_.append((lambda t, k=k: U2[:, t, 768 + k * P:768 + (k + 1) * P], naQ[:, k, :]))
                out_.append((lambda t, k=k: U2[:, t, 1280 + k * P:1280 + (k + 1) * P], naK[:, k, :]))
                out_.append((lambda t, k=k: Uc[:, t, 256 + k * P:256 + (k + 1) * P], naC[:, k, :]))
            return out_

        gq_pairs = OTb[:, 0:1024].rearrange("p (t j n) -> p t j n", t=2, j=4)
        TRPH = ("mla", "dil", "odd", "b2")
        tr0 = {}
        at = 0
        for ph in TRPH:
            tr0[ph] = at
            at += len(tr_list(ph))

        def groups(ph):
            if ph == "ein":
                return [(("ein", i), hT, KT, tt, 0, min(W, E_IN - i * W)) for i in range(6) for tt in range(TT)]
            if ph == "lat":
                return ([(("uq",), cT, 3, tt, c, w) for tt in range(TT) for c, w in ((0, 512), (512, 256))]
                        + [(("ukv",), cT[:, 3:5, :], 2, tt, c, 512) for tt in range(TT) for c in (0, 512)])
            if ph == "oin":
                return [(("oin", i), hT, KT, tt, 0, W) for i in range(6) for tt in range(TT)]
            g = []
            for i in range(6):
                g += [(("in2", i), hT, KT, tt, 0, IN2[i][1]) for tt in range(TT)]
                if i in CTX_AT:
                    g += [(("in2", i), hc, KT, tt, 0, IN2[i][1]) for tt in range(TT)]
            return g

        g0 = {}
        at = 0
        for ph in ("ein", "lat", "oin", "in2"):
            g0[ph] = at
            at += len(groups(ph))

        def small_loads():
            return [(X, t["x"][0].rearrange("(t p) n -> p t n", p=P)), (consts[:, :], t["consts"]), (cols[:, :], t["cols"]),
                    (rows[:, :], t["rows"].partition_broadcast(P)), (posi[:, :], t["positions"]),
                    (wrt[:, :].rearrange("p (k n) -> p k n", k=KT), t["w_router_2"].rearrange("(k p) n -> p k n", p=P))]

        NSMALL = len(small_loads())
        RES = ("eout", "mlp0", "oout", "mlp1", "out2")
        NORMS = ("mix0", "mlp0", "mix1", "mlp1", "mix2", "ctx2", "mlp2")
        block = ctx.enter_context(nc.Block())

        @block.sync
        def _(sp):
            for n, (name, src, k, w) in enumerate(stream):
                if n >= RING:
                    sp.wait_ge(*last_use(stream[n - RING][0]))
                sp.dma_start(chunk(name), src).then_inc(S(f"loaded{n % RING}"), 16)
            def expert_loads(e, first):
                for m in range(12):
                    j, c, s = m // 3, m % 3, m % RING
                    if first and m < RING:
                        sp.wait_ge(*last_use(last_in(s)))
                    else:
                        jj, cc = (m - RING) // 3, (m - RING) % 3
                        if cc < 2:
                            sp.wait_ge(S("merge"), 32 + 4 * jj + 4 + e * 4)
                        else:
                            sp.wait_ge(S("res"), 20 + 4 * jj + 4 + e * 4)
                    if c < 2:
                        src = t["w_expert_gu_2"][0][bass.ds(e + j, 1), :, c * EFF:(c + 1) * EFF]
                        dst = ring[:, s * SLOT:s * SLOT + KT * EFF].rearrange("p (k n) -> p k n", k=KT)
                    else:
                        src = t["w_expert_down_2"][0][bass.ds(e + j, 1), :, :]
                        dst = ring[:, s * SLOT:(s + 1) * SLOT].rearrange("p (k n) -> p k n", k=4)
                    sp.dma_start(dst, src.rearrange("o (k p) n -> p (o k) n", p=P)).then_inc(S(f"loaded{s}"), 16)

            expert_loads(0, True)
            with sp.Fori(1, NEXP // 4) as it:
                expert_loads(it * 4, False)
            sp.wait_ge(S("final_done"), 2)
            sp.dma_start(out[0].rearrange("(t p) n -> p t n", p=P), xs).then_inc(S("stored"), 16)
            sp.wait_ge(S("stored"), 16)

        @block.tensor
        def _(pe):
            mm = nc.tensor.matmul
            pe.wait_ge(S("consts_in"), 16 * NSMALL)
            pe.wait_ge(S("ones_set"), 2)

            def mod_sum(q):
                pe.wait_ge(S("mod_acc"), q + 1)
                if q:
                    pe.wait_ge(S("mod_fin"), q)
                mm(ps[:, 6, :], ones[:, :], acc[:, q % 2, :], start=True, stop=True).then_inc(S("mod_sum"), 1)

            def norm_transposes(i):
                pe.wait_ge(S("norm_scaled"), 2 * (i + 1))
                for k in range(KT):
                    n = KT * i + k
                    if n >= 4 and k % 2 == 0:
                        pe.wait_ge(S("norm_out"), n - 2)
                    for tt in range(TT):
                        last = nc.tensor.transpose(ps[:, 4 + (k // 2) % 2, 256 * (k % 2) + P * tt:256 * (k % 2) + P * tt + P],
                                                   xs[:, tt, k * P:(k + 1) * P], ident)
                    last.then_inc(S("norm_tr"), 1)

            def projections(ph, after=None):
                gs = groups(ph)
                for j, (name, src, nk, tt, c, w) in enumerate(gs):
                    g = g0[ph] + j
                    wt = arrived(pe, name)
                    if g >= 4:
                        pe.wait_ge(S("proj_out"), g - 3)
                    for k in range(nk):
                        last = mm(ps[:, g % 4, 0:w], src[:, k, P * tt:P * tt + P], wt[:, k, c:c + w],
                                  start=(k == 0), stop=(k == nk - 1))
                    last.then_inc(S("proj"), 1)
                    if j + 1 == len(gs) or gs[j + 1][0] != name:
                        if after:
                            after(name)

            def head_transposes(ph):
                lst = tr_list(ph)
                for j, (src, dst) in enumerate(lst):
                    n = tr0[ph] + j
                    if n >= 4 and n % 2 == 0:
                        pe.wait_ge(S("qkt_out"), n - 2)
                    for tt in range(TT):
                        s = src(tt)
                        d = s.shape[-1]
                        last = nc.tensor.transpose(ps[0:d, 4 + (n // 2) % 2, 256 * (n % 2) + P * tt:256 * (n % 2) + P * tt + P],
                                                   s, ident)
                    last.then_inc(S("qkt"), 1)

            def attention(ph):
                a, b = span(ph)

                def score(i):
                    if i >= 2:
                        pe.wait_ge(S("masked"), i - 1)
                    for c, q, k, n in scores_of(UNITS[i]):
                        last = mm(s_bank(i)[:, c:c + n], q, k, start=True, stop=True)
                    last.then_inc(S("scored"), 1)

                def transposes(i):
                    pe.wait_ge(S("normed"), i + 1)
                    lag = 1 if wide(UNITS[i]) else 2
                    if i >= lag:
                        pe.wait_ge(S("pt_out"), i - lag + 1)
                    for j in range(len(values_of(UNITS[i]))):
                        last = nc.tensor.transpose(pt_bank(i)[:, j * P:(j + 1) * P], Eb[:, i % 3, j * P:(j + 1) * P], ident)
                    last.then_inc(S("pt"), 1)

                def weigh(i):
                    pe.wait_ge(S("pt_out"), i + 1)
                    if i >= 2:
                        pe.wait_ge(S("o_out"), i - 1)
                    vs = values_of(UNITS[i])
                    r, m, _ = output_of(UNITS[i])
                    for j, v in enumerate(vs):
                        last = mm(ps[r:r + m, 6 + i % 2, 0:P], v, PTb[:, i % 2, j * P:(j + 1) * P],
                                  start=(j == 0), stop=(j == len(vs) - 1))
                    last.then_inc(S("weighed"), 1)

                for i in range(a, b + 2):
                    if i < b:
                        score(i)
                    if a <= i - 1 < b:
                        transposes(i - 1)
                    if a <= i - 2:
                        weigh(i - 2)

            def out_projection(name, nk, r):
                for n in range(2):
                    wt = arrived(pe, (name, n))
                    for tt in range(TT):
                        for k in range(nk):
                            last = mm(ps[:, 2 * n + tt, :], (M2 if name == "out2" else OT)[:, k, P * tt:P * tt + P],
                                      wt[:, k, :], start=(k == 0), stop=(k == nk - 1))
                        last.then_inc(S("res"), 1)

            def mlp(l, q0, r):
                qd = [q0]
                for j in range(FF // W):
                    w1 = arrived(pe, ("w1", l, j))
                    for f in range(4):
                        n = 32 * l + 4 * j + f
                        if n >= 2:
                            pe.wait_ge(S("hid_read"), n - 1)
                        for k in range(KT):
                            last = mm(ps[:, 4 + n % 2, 0:SEQ], w1[:, k, f * P:(f + 1) * P], hT[:, k, :],
                                      start=(k == 0), stop=(k == KT - 1))
                        last.then_inc(S("hid"), 1)
                    w2 = arrived(pe, ("w2", l, j))
                    for k in range(4):
                        pe.wait_ge(S("hid_out"), 32 * l + 4 * j + k + 1)
                        for n in range(2):
                            for tt in range(TT):
                                last = mm(ps[:, 2 * n + tt, :], HT[:, j % 2, k, P * tt:P * tt + P],
                                          w2[:, k, n * W:(n + 1) * W],
                                          start=(j == 0 and k == 0), stop=(j == 7 and k == 3))
                                if j == 7 and k == 3:
                                    last.then_inc(S("res"), 1)
                    if j < 7:
                        last.then_inc(S("w2_used"), 1)
                    for m in mod_in_mlp(j):
                        mod_sum(qd[0])
                        qd[0] += 1
                        if l == 1 and m < 4:
                            mod_sum(qd[0])
                            qd[0] += 1

            for q in range(4):
                mod_sum(q)
            norm_transposes(0)
            pe.wait_ge(S("norm_out"), KT)
            projections("ein", after=lambda name: mod_sum(4 + name[1]) if name[0] == "ein" else None)
            mod_sum(10)
            mod_sum(11)
            pe.wait_ge(S("lat_scaled"), 1)
            pe.wait_ge(S("norm_out"), KT)
            for k in range(5):
                if k == 4:
                    pe.wait_ge(S("lat_out"), 2)
                for tt in range(TT):
                    last = nc.tensor.transpose(ps[:, 4 + (k // 2) % 2, 256 * (k % 2) + P * tt:256 * (k % 2) + P * tt + P],
                                               Ue[:, tt, k * P:(k + 1) * P], ident)
                last.then_inc(S("lat_tr"), 1)
            pe.wait_ge(S("lat_out"), 5)
            projections("lat")
            pe.wait_ge(S("roped"), 1)
            head_transposes("mla")
            pe.wait_ge(S("qkt_out"), 16)
            attention("mla")
            pe.wait_ge(S("roped"), 2)
            head_transposes("dil")
            pe.wait_ge(S("qkt_out"), tr0["odd"])
            attention("dil")
            pe.wait_ge(S("o_out"), span("dil")[1])
            out_projection("eout", 6, 0)
            norm_transposes(1)
            pe.wait_ge(S("norm_out"), 2 * KT)
            mlp(0, 12, 1)
            norm_transposes(2)
            pe.wait_ge(S("norm_out"), 3 * KT)
            projections("oin")
            pe.wait_ge(S("roped"), 3)
            head_transposes("odd")
            pe.wait_ge(S("qkt_out"), tr0["b2"])
            attention("diff")
            pe.wait_ge(S("sub_sq"), 1)
            for h in range(4):
                last = mm(ps[:, 6 - (h // 2) * 2, 256 * (h % 2):256 * (h % 2) + 256], ones[:, :], hTb[:, 256 * h:256 * h + 256],
                          start=True, stop=True)
            last.then_inc(S("sub_sum"), 1)
            attention("moba")
            pe.wait_ge(S("sub_done"), 1)
            pe.wait_ge(S("o_out"), span("moba")[1])
            out_projection("oout", 8, 2)
            norm_transposes(3)
            pe.wait_ge(S("norm_out"), 4 * KT)
            mlp(1, 24, 3)
            norm_transposes(4)
            norm_transposes(5)
            pe.wait_ge(S("norm_out"), 6 * KT)
            projections("in2")
            wa = arrived(pe, ("in2", 6))
            wb = arrived(pe, ("in2", 7))
            for f in range(4):
                if f >= 2:
                    pe.wait_ge(S("glu_out"), f - 1)
                for wt, c in ((wa, 0), (wb, SEQ)):
                    for k in range(KT):
                        last = mm(ps[:, 4 + f % 2, c:c + SEQ], wt[:, k, f * P:(f + 1) * P], hT[:, k, :],
                                  start=(k == 0), stop=(k == KT - 1))
                last.then_inc(S("glu"), 1)
            pe.wait_ge(S("glu_out"), 4)
            pe.wait_ge(S("roped"), 4)
            head_transposes("b2")
            pe.wait_ge(S("qkt_out"), tr0["b2"] + len(tr_list("b2")))
            attention("gqa")
            attention("na")
            pe.wait_ge(S("pt_out"), len(UNITS))
            pe.wait_ge(S("o_out"), len(UNITS))
            pe.wait_ge(S("dft_in"), 16)
            CL = dft("CL").rearrange("p (t n) -> p t n", t=2)
            SL = dft("SL").rearrange("p (t n) -> p t n", t=2)
            for g in range(4):
                for m, c in ((CL, 0), (SL, SEQ)):
                    for tt in range(TT):
                        last = mm(ps[:, g, c:c + SEQ], U2[:, tt, 2304 + g * P:2304 + (g + 1) * P], m[:, tt, :],
                                  start=(tt == 0), stop=(tt == TT - 1))
                last.then_inc(S("dft1"), 1)
            for g in range(4):
                pe.wait_ge(S("dft1_out"), g + 1)
                b, c = 4 + g // 2, SEQ * (g % 2)
                mm(ps[:, b, c:c + SEQ], dft("CD"), Z12[:, g, 0:SEQ], start=True, stop=False)
                mm(ps[:, b, c:c + SEQ], dft("SD"), Z12[:, g, SEQ:2 * SEQ], start=False, stop=True).then_inc(S("dft2"), 1)
            pe.wait_ge(S("conv_sq"), 1)
            for k in range(4):
                last = mm(ps[:, 6, 0:SEQ], ones[:, :], convs[:, k, :], start=(k == 0), stop=(k == 3))
            last.then_inc(S("conv_sum"), 1)
            pe.wait_ge(S("dft2_out"), 4)
            pe.wait_ge(S("conv_out"), 4)
            for b in range(4):
                wb = None
                for hf in range(2):
                    wg = arrived(pe, ("gate", 2 * b + hf))
                    if wb is None:
                        wb = arrived(pe, ("branch", b))
                    y = (OT[:, 0:4, :], OT[:, 4:8, :], YF, YC)[b]
                    for f in range(4):
                        n = 8 * b + 4 * hf + f
                        if n >= 2:
                            pe.wait_ge(S("merge_out"), n - 1)
                        for k in range(KT):
                            mm(ps[:, 4 + n % 2, 0:SEQ], wg[:, k, f * P:(f + 1) * P], hT[:, k, :],
                               start=(k == 0), stop=(k == KT - 1))
                        for k in range(4):
                            last = mm(ps[:, 4 + n % 2, SEQ:2 * SEQ], wb[:, k, (4 * hf + f) * P:(4 * hf + f + 1) * P], y[:, k, :],
                                      start=(k == 0), stop=(k == 3))
                        last.then_inc(S("merge"), 1)
            pe.wait_ge(S("merged"), 1)
            out_projection("out2", 8, 4)
            norm_transposes(6)
            pe.wait_ge(S("norm_out"), 7 * KT)
            wr = wrt[:, :].rearrange("p (k n) -> p k n", k=KT)
            for tt in range(TT):
                for k in range(KT):
                    last = mm(ps[:, 6, 16 * tt:16 * tt + 16], hT[:, k, P * tt:P * tt + P], wr[:, k, :],
                              start=(k == 0), stop=(k == KT - 1))
            last.then_inc(S("logits"), 1)
            def loaded(e, m):
                s = m % RING
                pe.wait_ge(S(f"loaded{s}"), 16 * (loads_of[s] + m // RING + 1) + e * 12)

            with pe.Fori(0, NEXP // 4) as it:
                e = it * 4
                for j in range(4):
                    sl = [(3 * j + c) % RING for c in range(3)]
                    wa, wb = (ring[:, s * SLOT:(s + 1) * SLOT].rearrange("p (k n) -> p k n", k=KT) for s in sl[0:2])
                    wd = ring[:, sl[2] * SLOT:(sl[2] + 1) * SLOT].rearrange("p (k n) -> p k n", k=4)
                    loaded(e, 3 * j)
                    loaded(e, 3 * j + 1)
                    for f in range(4):
                        pe.wait_ge(S("merge_out"), 32 + 4 * j + f - 1 + e * 4)
                        for wt, c in ((wa, 0), (wb, SEQ)):
                            for k in range(KT):
                                last = mm(ps[:, 4 + f % 2, c:c + SEQ], wt[:, k, f * P:(f + 1) * P], hT[:, k, :],
                                          start=(k == 0), stop=(k == KT - 1))
                        last.then_inc(S("merge"), 1)
                    loaded(e, 3 * j + 2)
                    pe.wait_ge(S("res_out"), 20 + 4 * j + e * 4)
                    for k in range(4):
                        pe.wait_ge(S("merge_out"), 32 + 4 * j + k + 1 + e * 4)
                        for n in range(2):
                            for tt in range(TT):
                                last = mm(ps[:, 2 * n + tt, :], HT[:, j % 2, k, P * tt:P * tt + P],
                                          wd[:, k, n * W:(n + 1) * W], start=(k == 0), stop=(k == 3))
                                if k == 3:
                                    last.then_inc(S("res"), 1)

        @block.scalar
        def _(act):
            A = nc.scalar.activation
            for dst, src in small_loads():
                act.dma_start(dst, src).then_inc(S("consts_in"), 16)
            act.wait_ge(S("consts_in"), 16 * NSMALL)
            A(cond[:, :], col("c"), ACT.Silu).then_inc(S("cond"), 1)
            act.wait_ge(S("angles"), 2)
            A(rope[:, 0:192], rope[:, 0:192], ACT.Sin).then_inc(S("sines"), 1)
            A(lam[:, 2:4], lam[:, 0:2], ACT.Exp).then_inc(S("lam_exp"), 1)

            def square_sums(i, src):
                for tt in range(TT):
                    A(xs[:, tt, :], src[:, tt, :], ACT.Square, accum_out=ss[:, 2 * (i % 2) + tt:2 * (i % 2) + tt + 1]) \
                        .then_inc(S("norm_sq"), 1)

            def norm_out(i, dst):
                l, v = ((0, 0), (0, 3), (1, 0), (1, 3), (2, 0), (3, 0), (2, 3))[i]
                act.wait_ge(S("coef"), i + 1)
                for k in range(KT):
                    act.wait_ge(S("norm_tr"), KT * i + (k | 1) + 1)
                    A(dst[:, k, :], ps[:, 4 + (k // 2) % 2, 256 * (k % 2):256 * (k % 2) + 256], ACT.Identity,
                      bias=modc[:, l, v, k:k + 1], scale=coef[:, i, k:k + 1]).then_inc(S("norm_out"), 1)

            def proj_out(ph, place):
                for j, (name, _, nk, tt, c, w) in enumerate(groups(ph)):
                    g = g0[ph] + j
                    act.wait_ge(S("proj"), g + 1)
                    cps = place(j, name, tt, c, w, ps[:, g % 4, 0:w])
                    for n, (dst, src) in enumerate(cps):
                        last = A(dst, src, ACT.Copy)
                    last.then_inc(S("proj_out"), 1)

            def qkt_out(ph):
                for j, (src, dst) in enumerate(tr_list(ph)):
                    n = tr0[ph] + j
                    act.wait_ge(S("qkt"), (n | 1) + 1)
                    d = dst.shape[0]
                    A(dst, ps[0:d, 4 + (n // 2) % 2, 256 * (n % 2):256 * (n % 2) + 256], ACT.Copy).then_inc(S("qkt_out"), 1)

            def attention(ph):
                a, b = span(ph)
                for i in range(a, b + 1):
                    if i < b:
                        act.wait_ge(S("masked"), i + 1)
                        for j, (c, n, _) in enumerate(softmax_of(UNITS[i])):
                            last = A(Eb[:, i % 3, c:c + n], Eb[:, i % 3, c:c + n], ACT.Exp, bias=mx[:, i % 3, j:j + 1],
                                     scale=-1.0, accum_out=sm[:, i % 3, j:j + 1])
                        last.then_inc(S("exped"), 1)
                    if i - 1 >= a:
                        m = i - 1
                        n = P * len(values_of(UNITS[m]))
                        act.wait_ge(S("pt"), m + 1)
                        if m >= 2:
                            act.wait_ge(S("weighed"), m - 1)
                        A(PTb[:, m % 2, 0:n], pt_bank(m)[:, 0:n], ACT.Copy).then_inc(S("pt_out"), 1)

            def mlp(l):
                for n in range(32):
                    m = 32 * l + n
                    act.wait_ge(S("hid"), m + 1)
                    if m >= 2:
                        act.wait_ge(S("hid_out"), m - 1)
                    A(tmp[:, m % 2, 0:SEQ], ps[:, 4 + m % 2, 0:SEQ], ACT.Relu).then_inc(S("hid_read"), 1)
                    act.wait_ge(S("hid_read"), m + 1)
                    if n >= 8 and n % 4 == 0:
                        act.wait_ge(S("w2_used"), 7 * l + n // 4 - 1)
                    A(HT[:, (n // 4) % 2, n % 4, :], tmp[:, m % 2, 0:SEQ], ACT.Square).then_inc(S("hid_out"), 1)

            square_sums(0, X)
            norm_out(0, hT)
            proj_out("ein", lambda j, name, tt, c, w, p: [(Ue[:, tt, name[1] * W:name[1] * W + w], p)])
            act.wait_ge(S("proj_out"), 12)
            for tt in range(TT):
                A(xs[:, 0, 0:QR], Ue[:, tt, 0:QR], ACT.Square, accum_out=ss[:, 8 + tt:9 + tt]).then_inc(S("lat_sq"), 1)
                A(xs[:, 1, 0:KVR], Ue[:, tt, QR:QR + KVR], ACT.Square, accum_out=ss[:, 10 + tt:11 + tt]).then_inc(S("lat_sq"), 1)
                act.wait_ge(S("lat_sq"), 2 * tt + 2)
            for k in range(5):
                act.wait_ge(S("lat_tr"), min((k | 1) + 1, 5))
                gain = col("qlat")[:, k:k + 1] if k < 3 else col("kvlat")[:, k - 3:k - 2]
                A(cT[:, k, :], ps[:, 4 + (k // 2) % 2, 256 * (k % 2):256 * (k % 2) + 256], ACT.Copy, scale=gain) \
                    .then_inc(S("lat_out"), 1)

            def lat_place(j, name, tt, c, w, p):
                if name[0] == "uq":
                    return [(AUX[:, 768 * tt + c:768 * tt + c + w], p)]
                h0 = c // P
                v = p.rearrange("p (h d) -> p h d", d=P)
                return [(Km[:, tt, h0:h0 + 4, 0:NOPE], v[:, :, 0:NOPE]), (Vm[:, tt, h0:h0 + 4, :], v[:, :, NOPE:])]

            proj_out("lat", lat_place)
            qkt_out("mla")
            attention("mla")
            act.wait_ge(S("weighed"), span("mla")[1])
            qkt_out("dil")
            attention("dil")
            act.wait_ge(S("res_out"), 4)
            square_sums(1, X)
            norm_out(1, hT)
            mlp(0)
            act.wait_ge(S("res_out"), 8)
            square_sums(2, X)
            norm_out(2, hT)
            proj_out("oin", lambda j, name, tt, c, w, p: [(Uo[:, tt, name[1] * W:name[1] * W + w], p)])
            qkt_out("odd")
            attention("diff")
            act.wait_ge(S("o_out"), span("diff")[1])
            A(hTb[:, 0:1024], OTb[:, 0:1024], ACT.Square).then_inc(S("sub_sq"), 1)
            attention("moba")
            act.wait_ge(S("res_out"), 12)
            square_sums(3, X)
            norm_out(3, hT)
            mlp(1)
            act.wait_ge(S("res_out"), 16)
            square_sums(4, X)
            norm_out(4, hT)
            act.wait_ge(S("ctx_in"), 16)
            square_sums(5, ctx_x)
            norm_out(5, hc)

            def in2_place(j, name, tt, c, w, p):
                i = name[1]
                seen = [g for g in groups("in2")[:j] if g[0] == name]
                if len(seen) >= 2:
                    return [(Uc[:, tt, CTX_AT[i]:CTX_AT[i] + w], p)]
                return [(U2[:, tt, IN2[i][0]:IN2[i][0] + w], p)]

            proj_out("in2", in2_place)
            for f in range(4):
                act.wait_ge(S("glu"), f + 1)
                if f >= 2:
                    act.wait_ge(S("glu_out"), f - 1)
                A(tmp[:, f % 2, 0:SEQ], ps[:, 4 + f % 2, SEQ:2 * SEQ], ACT.Sigmoid).then_inc(S("glu_sig"), 1)
            qkt_out("b2")
            attention("gqa")
            attention("na")
            for g in range(4):
                act.wait_ge(S("dft1"), g + 1)
                A(Z12[:, g, :], ps[:, g, :], ACT.Copy).then_inc(S("dft1_out"), 1)
            for g in range(4):
                act.wait_ge(S("dft2"), (g | 1) + 1)
                A(YF[:, g, :], ps[:, 4 + g // 2, SEQ * (g % 2):SEQ * (g % 2) + SEQ], ACT.Copy).then_inc(S("dft2_out"), 1)
            act.wait_ge(S("conv_done"), 4)
            A(convs[:, :, :], convy[:, :, :], ACT.Square).then_inc(S("conv_sq"), 1)
            act.wait_ge(S("conv_scaled"), 1)
            for k in range(4):
                A(YC[:, k, :], convs[:, k, :], ACT.Silu, scale=col("convg")[:, k:k + 1]).then_inc(S("conv_out"), 1)
            for n in range(32):
                act.wait_ge(S("merge"), n + 1)
                if n >= 2:
                    act.wait_ge(S("merge_out"), n - 1)
                A(tmp[:, n % 2, 0:SEQ], ps[:, 4 + n % 2, 0:SEQ], ACT.Sigmoid).then_inc(S("merge_act"), 1)
            act.wait_ge(S("res_out"), 20)
            square_sums(6, X)
            norm_out(6, hT)
            act.wait_ge(S("logits"), 1)
            A(moe[:, 0:32], ps[:, 6, 0:32], ACT.Sigmoid).then_inc(S("router_sig"), 1)
            with act.Fori(0, NEXP // 4) as it:
                e = it * 4
                for j in range(16):
                    act.wait_ge(S("merge"), 32 + j + 1 + e * 4)
                    act.wait_ge(S("merge_out"), 32 + j - 1 + e * 4)
                    A(tmp[:, j % 2, 0:SEQ], ps[:, 4 + j % 2, 0:SEQ], ACT.Silu).then_inc(S("merge_act"), 1)
            act.wait_ge(S("final_x"), 1)
            square_sums(7, X)

        @block.gpsimd
        def _(pool):
            pool.memset(ones[:, :], 1.0).then_inc(S("ones_set"), 1)
            pool.memset(zero[:, :], 0.0).then_inc(S("ones_set"), 1)
            pool.wait_ge(S("consts_in"), 16 * NSMALL)

            def gate_bias(l):
                for i, v in enumerate((2, 5)):
                    b = (t["ada_b"][l] if l < 2 else t["b_mod_2"][0])[v * D:(v + 1) * D]
                    pool.dma_start(G[:, 2 * (l % 2) + i, :], b.partition_broadcast(P)) \
                        .then_inc(S(f"gate_bias{l}"), 16)

            def attention(ph):
                a, b = span(ph)
                for i in range(a, b):
                    pool.wait_ge(S("recip"), i + 1)
                    sf = softmax_of(UNITS[i])
                    E = Eb[:, i % 3, :]
                    if ph == "diff":
                        n = sf[0][1]
                        for m in range(2):
                            pool.tensor_scalar(E[:, m * n:(m + 1) * n], E[:, m * n:(m + 1) * n], rc[:, i % 3, m:m + 1], 1.0,
                                               ALU.mult, ALU.mult).then_inc(S("diff_scaled"), 1)
                        pool.wait_ge(S("diff_scaled"), 2 * (i - a) + 2)
                        pool.tensor_tensor(out=E[:, 0:n], in0=E[:, 0:n], in1=E[:, n:2 * n], op=ALU.add).then_inc(S("normed"), 1)
                    else:
                        n = sf[0][1]
                        pool.tensor_scalar(E[:, 0:n], E[:, 0:n], rc[:, i % 3, 0:1], 1.0, ALU.mult, ALU.mult) \
                            .then_inc(S("normed"), 1)

            def na_bias(h):
                if h >= 2:
                    pool.wait_ge(S("masked"), span("na")[0] + 2 * (h - 1))
                pool.dma_start(nab[:, h % 2, :, 0:256], t["na_bias"][h].rearrange("(t p) n -> p t n", p=P)) \
                    .then_inc(S("nab_in"), 16)

            def na_mask(h):
                pool.wait_ge(S("nab_in"), 16 * (h + 1))
                pool.tensor_tensor(out=nab[:, h % 2, :, 0:256], in0=nab[:, h % 2, :, 0:256],
                                   in1=con("na").rearrange("p (t n) -> p t n", t=2), op=ALU.add).then_inc(S("nab"), 1)

            gate_bias(0)
            gate_bias(1)
            attention("mla")
            attention("dil")
            attention("diff")
            attention("moba")
            pool.wait_ge(S("res_out"), 8)
            gate_bias(2)
            pool.wait_ge(S("weighed"), span("moba")[1])
            pool.dma_start(ctx_x, t["ctx_2"][0].rearrange("(t p) n -> p t n", p=P)).then_inc(S("ctx_in"), 16)
            pool.wait_ge(S("roped"), 4)
            pool.memset(nab[:, :, :, 256:512], 0.0).then_inc(S("nab_zero"), 1)
            pool.wait_ge(S("nab_zero"), 1)
            pool.wait_ge(S("normed"), span("moba")[1])
            pool.dma_start(consts[:, dft_at:dft_at + NDFT], t["dft"]).then_inc(S("dft_in"), 16)
            na_bias(0)
            na_mask(0)
            na_bias(1)
            na_mask(1)
            attention("gqa")
            a, b = span("na")
            for h in range(8):
                more = 1 <= h < 7
                if more:
                    na_bias(h + 1)
                for i in (a + 2 * h, a + 2 * h + 1):
                    if i % 2 and more:
                        na_mask(h + 1)
                    pool.wait_ge(S("recip"), i + 1)
                    pool.tensor_scalar(Eb[:, i % 3, 0:512], Eb[:, i % 3, 0:512], rc[:, i % 3, 0:1], 1.0, ALU.mult, ALU.mult) \
                        .then_inc(S("normed"), 1)
            pool.wait_ge(S("res_out"), 16)
            pool.dma_start(G[:, 2, :], t["final_norm_g_2"].partition_broadcast(P)) \
                .then_inc(S("final_gain"), 16)

        @block.vector
        def _(dve):
            V = nc.vector
            chain = [0]

            def link(ins):
                chain[0] += 1
                ins.then_inc(S("dve_chain"), 1)
                dve.wait_ge(S("dve_chain"), chain[0])

            def ts(o, i, a, b=None, p=ALU.mult, q=ALU.add):
                if b is None:
                    return V.tensor_scalar(o, i, a, None, p)
                return V.tensor_scalar(o, i, a, b, p, q)

            def tt_(o, a, b, op=ALU.mult):
                return V.tensor_tensor(o, a, b, op)

            def stt(o, a, s, b, p=ALU.mult, q=ALU.add):
                return V.scalar_tensor_tensor(out=o, in0=a, scalar=s, in1=b, op0=p, op1=q)

            def rstd(y, x, inv_n, scale=None):
                n = x.shape[-1]
                v, xh = (wn[:, i, 0:n] for i in range(2))
                link(ts(v, x, inv_n, EPS))
                ts(xh, v, -0.5)
                link(ts(y.bitcast(I32), v.bitcast(I32), -0.5, 1597463007.0))
                for _ in range(3):
                    link(tt_(v, y, y))
                    link(tt_(v, v, xh))
                    link(stt(y, v, 1.5, y, ALU.add, ALU.mult))
                if scale is not None:
                    link(ts(y, y, scale))

            def norm_heads(x, h, d, scr, gain, scale, cos, sin, r0, halfw, pairs=False):
                sq = scr[:, 0:h * d].rearrange("p (h d) -> p h d", h=h)
                link(tt_(sq, x, x))
                link(V.reduce_sum(ss[:, 16:16 + h], sq, axis=AX))
                rstd(wn[:, 2, 0:h], ss[:, 16:16 + h], 1.0 / d, scale)
                link(tt_(x, x, spread(wn[:, 2, 0:h], 2, d)))
                link(tt_(x, x, spread(gain, 1, h)))
                if cos is None:
                    return
                c = spread(cos, 1, h)
                s = spread(sin, 1, h)
                if pairs:
                    v = x.rearrange("p h (m two) -> p h m two", two=2)
                    x1, x2 = v[:, :, :, 0], v[:, :, :, 1]
                else:
                    x1, x2 = x[:, :, r0:r0 + halfw], x[:, :, r0 + halfw:r0 + 2 * halfw]
                w = h * halfw
                a = scr[:, 0:w].rearrange("p (h d) -> p h d", h=h)
                b = tmp[:, 0, 0:w].rearrange("p (h d) -> p h d", h=h) if w <= W else None
                b = b if b is not None else tmp[:, :, :].rearrange("p s n -> p (s n)")[:, 0:w].rearrange("p (h d) -> p h d", h=h)
                tt_(a, x1, s)
                link(tt_(b, x2, s))
                tt_(x1, x1, c)
                link(tt_(x2, x2, c))
                tt_(x1, x1, b, ALU.subtract)
                link(tt_(x2, x2, a, ALU.add))

            def mod_acc(q):
                l, j = MODSEQ[q]
                name = ("mod", min(l, 2), j)
                w = arrived(dve, name)
                a = acc[:, q % 2, :]
                c0 = 8 * min(l, 3) if l > 1 else 0
                c0 = {0: 0, 1: 0, 2: 8, 3: 16}[l]
                link(ts(a, w[:, 0, :], cond[:, c0:c0 + 1]))
                for k in range(1, KT):
                    ins = stt(a, w[:, k, :], cond[:, c0 + k:c0 + k + 1], a)
                    if k < KT - 1:
                        link(ins)
                ins.then_inc(S("mod_acc"), 1)

            def mod_fin(q):
                l, j = MODSEQ[q]
                v, hf = j // 2, j % 2
                dve.wait_ge(S("mod_sum"), q + 1)
                p = ps[:, 6, :]
                if v in (2, 5):
                    dve.wait_ge(S(f"gate_bias{l}"), 32)
                    g = G[:, 2 * (l % 2) + v // 3, hf * W:(hf + 1) * W]
                    tt_(g, g, p, ALU.add).then_inc(S("mod_fin"), 1)
                    dve.wait_ge(S("mod_fin"), q + 1)
                    return
                w4 = mtmp.rearrange("p (c n) -> p c n", c=4)
                link(tt_(w4, p.rearrange("p (c n) -> p c n", c=4), spread(ident, 1, 4)))
                m = modc[:, l, v, 4 * hf:4 * hf + 4]
                link(V.reduce_sum(m, w4, axis=AX))
                bias = col("adab")[:, 48 * min(l, 2) + 8 * v + 4 * hf:48 * min(l, 2) + 8 * v + 4 * hf + 4]
                tt_(m, m, bias, ALU.add).then_inc(S("mod_fin"), 1)
                dve.wait_ge(S("mod_fin"), q + 1)

            def norm(i, src):
                l, v = ((0, 1), (0, 4), (1, 1), (1, 4), (2, 1), (3, 1), (2, 4))[i]
                gain = (col("nmix")[:, 0:8], col("nmlp")[:, 0:8], col("nmix")[:, 8:16], col("nmlp")[:, 8:16],
                        col("n1"), col("n1"), col("n2"))[i]
                stt(coef[:, i, :], modc[:, l, v, :], 1.0, gain, ALU.add, ALU.mult).then_inc(S("coef"), 1)
                dve.wait_ge(S("norm_sq"), 2 * i + 2)
                r = ss[:, 4:6]
                rstd(r, ss[:, 2 * (i % 2):2 * (i % 2) + 2], 1.0 / D)
                for tt in range(TT):
                    ts(xs[:, tt, :], src[:, tt, :], r[:, tt:tt + 1]).then_inc(S("norm_scaled"), 1)

            def residual(r, s):
                for n in range(2):
                    for tt in range(TT):
                        m = 2 * n + tt
                        dve.wait_ge(S("res"), 4 * r + m + 1)
                        link(tt_(xs[:, tt, n * W:(n + 1) * W], ps[:, m, :], G[:, s, n * W:(n + 1) * W]))
                        x = X[:, tt, n * W:(n + 1) * W]
                        tt_(x, x, xs[:, tt, n * W:(n + 1) * W], ALU.add).then_inc(S("res_out"), 1)
                dve.wait_ge(S("res_out"), 4 * r + 4)

            def attention(ph, filler=()):
                a, b = span(ph)
                for i in range(a, b + 3):
                    if i < b:
                        dve.wait_ge(S("scored"), i + 1)
                        if i >= 3:
                            dve.wait_ge(S("pt"), i - 2)
                        if ph == "na" and i % 2 == 0:
                            dve.wait_ge(S("nab"), (i - a) // 2 + 1)
                        for j, (c, n, mask) in enumerate(softmax_of(UNITS[i])):
                            pc = j * W
                            last = V.tensor_tensor_reduce(out=Eb[:, i % 3, c:c + n], in0=s_bank(i)[:, pc:pc + n], in1=mask[:, 0:n],
                                                          scale=-1.0, scalar=3e38, op0=ALU.add, op1=ALU.min,
                                                          accum_out=mx[:, i % 3, j:j + 1])
                        last.then_inc(S("masked"), 1)
                    if a <= i - 1 < b:
                        m = i - 1
                        dve.wait_ge(S("exped"), m + 1)
                        if ph == "diff":
                            link(V.reciprocal(rc[:, m % 3, 0:2], sm[:, m % 3, 0:2]))
                            tt_(rc[:, m % 3, 1:2], rc[:, m % 3, 1:2], lam[:, 5:6]).then_inc(S("recip"), 1)
                        else:
                            V.reciprocal(rc[:, m % 3, 0:1], sm[:, m % 3, 0:1]).then_inc(S("recip"), 1)
                    if a <= i - 3:
                        m = i - 3
                        dve.wait_ge(S("weighed"), m + 1)
                        r, w, dst = output_of(UNITS[m])
                        V.tensor_copy(dst, ps[r:r + w, 6 + m % 2, 0:P]).then_inc(S("o_out"), 1)

            mtmp = wn[:, 0:2, :].rearrange("p s n -> p (s n)")
            dve.wait_ge(S("consts_in"), 16 * NSMALL)
            dve.wait_ge(S("ones_set"), 2)
            link(V.tensor_copy(posf[:, :], posi[:, :]))
            an, kk, tm = rw[:, 0, :], rw[:, 1, :], rw[:, 2, :]
            for tt in range(TT):
                last = ts(an[:, 48 * tt:48 * tt + 48], con("invf"), posf[:, tt:tt + 1])
            link(last)
            link(ts(kk, an, 1.0 / TWO_PI, 12582912.0))
            link(ts(kk, kk, 12582912.0, None, ALU.subtract))
            c1 = 6.28125
            c2 = float(np.float32(np.round((TWO_PI - c1) * 2 ** 20) / 2 ** 20))
            c3 = TWO_PI - c1 - c2
            for c in (c1, c2, c3):
                link(stt(an, kk, -c, an))
            sn, cs = rope[:, 96:192], rope[:, 0:96]
            link(ts(sn, an, PI_LO, -PI_LO, ALU.min, ALU.max))
            link(ts(tm, sn, -1.0))
            link(tt_(tm, tm, sn, ALU.max))
            ts(cs, tm, -1.0, float(np.pi / 2)).then_inc(S("angles"), 1)
            lv = row("lam").rearrange("p (i d) -> p i d", i=4)
            for i in range(2):
                link(V.tensor_tensor_reduce(out=rw[:, 3, 0:64], in0=lv[:, 2 * i, :], in1=lv[:, 2 * i + 1, :], scale=1.0,
                                            scalar=0.0, op0=ALU.mult, op1=ALU.add, accum_out=lam[:, i:i + 1]))
            V.engine_nop().then_inc(S("angles"), 1)
            dve.wait_ge(S("cond"), 1)
            for q in range(4):
                mod_acc(q)
                if q:
                    mod_fin(q - 1)
            mod_fin(3)
            norm(0, X)
            dve.wait_ge(S("lam_exp"), 1)
            link(tt_(lam[:, 4:5], lam[:, 3:4], lam[:, 2:3], ALU.subtract))
            link(ts(lam[:, 5:6], lam[:, 4:5], LAM_INIT, None, ALU.subtract))
            for q in range(4, 12):
                mod_acc(q)
                if q > 4:
                    mod_fin(q - 1)
            mod_fin(11)
            dve.wait_ge(S("lat_sq"), 4)
            rstd(ss[:, 12:14], ss[:, 8:10], 1.0 / QR)
            rstd(ss[:, 14:16], ss[:, 10:12], 1.0 / KVR)
            for tt in range(TT):
                ts(Ue[:, tt, 0:QR], Ue[:, tt, 0:QR], ss[:, 12 + tt:13 + tt])
                last = ts(Ue[:, tt, QR:QR + KVR], Ue[:, tt, QR:QR + KVR], ss[:, 14 + tt:15 + tt])
            last.then_inc(S("lat_scaled"), 1)
            for tt in range(TT):
                V.tensor_copy(Km[:, tt, :, NOPE:QKD], spread(Ue[:, tt, QR + KVR:QR + KVR + ROPE], 1, MH)) \
                    .then_inc(S("krope"), 1)
            dve.wait_ge(S("krope"), 2)
            dve.wait_ge(S("sines"), 1)
            dve.wait_ge(S("proj_out"), g0["oin"])
            for tt in range(TT):
                norm_heads(Qm[:, tt], MH, QKD, work, row("mlaq"), QKD ** -0.5, Cos[:, tt, 0:16], Sin[:, tt, 0:16], NOPE, 16)
                norm_heads(Km[:, tt], MH, QKD, work, row("mlak"), None, Cos[:, tt, 0:16], Sin[:, tt, 0:16], NOPE, 16)
            V.engine_nop().then_inc(S("roped"), 1)
            for tt in range(TT):
                for s, (gn, sc) in enumerate((("dilq", HD ** -0.5), ("dilk", None))):
                    o = QR + KVR + ROPE + s * 768
                    norm_heads(Ue[:, tt, o:o + 768].rearrange("p (h d) -> p h d", h=12), 12, HD, work, row(gn), sc,
                               Cos[:, tt, 16:48], Sin[:, tt, 16:48], 0, 32)
            V.engine_nop().then_inc(S("roped"), 1)
            attention("mla")
            attention("dil")
            residual(0, 0)
            norm(1, X)
            for q in range(12, 24):
                mod_acc(q)
                if q > 12:
                    mod_fin(q - 1)
            mod_fin(23)
            residual(1, 1)
            norm(2, X)
            dve.wait_ge(S("proj_out"), g0["in2"])
            for tt in range(TT):
                for c, gn, sc in ((0, "diffq", 0.125), (1, "diffk", None), (3, "mobaq", 0.125), (4, "mobak", None)):
                    norm_heads(Uo[:, tt, 512 * c:512 * c + 512].rearrange("p (h d) -> p h d", h=8), 8, HD, work, row(gn), sc,
                               Cos[:, tt, 16:48], Sin[:, tt, 16:48], 0, 32)
            V.engine_nop().then_inc(S("roped"), 1)
            attention("diff")
            dve.wait_ge(S("o_out"), span("diff")[1])
            dve.wait_ge(S("sub_sum"), 1)
            for h in range(4):
                rstd(wn[:, 2, 0:256], ps[:, 6 - (h // 2) * 2, 256 * (h % 2):256 * (h % 2) + 256], 1.0 / P, 1.0 - LAM_INIT)
                link(ts(wn[:, 2, :], wn[:, 2, :], col("subln")))
                link(tt_(OT[:, h, :], OT[:, h, :], wn[:, 2, :]))
            V.engine_nop().then_inc(S("sub_done"), 1)
            attention("moba")
            residual(2, 2)
            norm(3, X)
            for q in range(24, 40):
                mod_acc(q)
                if q > 24:
                    mod_fin(q - 1)
            mod_fin(39)
            residual(3, 3)
            norm(4, X)
            dve.wait_ge(S("ctx_in"), 16)
            dve.wait_ge(S("norm_tr"), 5 * KT)
            norm(5, ctx_x)
            dve.wait_ge(S("weighed"), span("moba")[1])
            link(V.memset(zp[:, :, :], 0.0))
            for f in range(4):
                dve.wait_ge(S("glu_sig"), f + 1)
                tt_(zp[:, f, 15:15 + SEQ], tmp[:, f % 2, 0:SEQ], ps[:, 4 + f % 2, 0:SEQ]).then_inc(S("glu_out"), 1)
            dve.wait_ge(S("glu_out"), 4)
            cw = col("convw").rearrange("p (c j) -> p c j", c=4)
            for k in range(4):
                link(ts(convy[:, k, :], zp[:, k, 0:SEQ], cw[:, k, 0:1], col("convb")[:, k:k + 1]))
            for j in range(1, TAPS):
                for k in range(4):
                    last = stt(convy[:, k, :], zp[:, k, j:j + SEQ], cw[:, k, j:j + 1], convy[:, k, :])
                link(last)
            V.engine_nop().then_inc(S("conv_done"), 4)
            dve.wait_ge(S("proj_out"), g0["in2"] + len(groups("in2")))
            for tt in range(TT):
                norm_heads(U2[:, tt, 0:512].rearrange("p (h d) -> p h d", h=8), 8, HD, work2, row("gqaq"), 0.125,
                           axcs[:, tt, :], axsn[:, tt, :], 0, 32, pairs=True)
                norm_heads(U2[:, tt, 512:640].rearrange("p (h d) -> p h d", h=2), 2, HD, work2, row("gqak"), None,
                           axcs[:, tt, :], axsn[:, tt, :], 0, 32, pairs=True)
                norm_heads(Uc[:, tt, 0:128].rearrange("p (h d) -> p h d", h=2), 2, HD, work2, row("gqak"), None,
                           None, None, 0, 32)
                V.tensor_copy(gq_pairs[:, tt].rearrange("p j (g d) -> p j g d", g=2),
                              U2[:, tt, 0:512].rearrange("p (g j d) -> p j g d", g=2, j=4))
                link(ts(U2[:, tt, 768:1280], U2[:, tt, 768:1280], 0.125))
            V.engine_nop().then_inc(S("roped"), 1)
            dve.wait_ge(S("qkt"), tr0["b2"] + 4)
            attention("gqa")
            attention("na")
            dve.wait_ge(S("conv_sum"), 1)
            rstd(wn[:, 2, 0:256], ps[:, 6, 0:SEQ], 1.0 / 512)
            tt_(convs[:, :, :], convy[:, :, :], spread(wn[:, 2, :], 1, 4)).then_inc(S("conv_scaled"), 1)
            for n in range(32):
                dve.wait_ge(S("merge_act"), n + 1)
                f = n % 8
                z = ps[:, 4 + n % 2, SEQ:2 * SEQ]
                g = tmp[:, n % 2, 0:SEQ]
                if n < 8:
                    tt_(M2[:, f, :], g, z).then_inc(S("merge_out"), 1)
                else:
                    tt_(xs[:, 0, 256 * (n % 2):256 * (n % 2) + 256], g, z).then_inc(S("merge_out"), 1)
                    dve.wait_ge(S("merge_out"), n + 1)
                    link(tt_(M2[:, f, :], M2[:, f, :], xs[:, 0, 256 * (n % 2):256 * (n % 2) + 256], ALU.add))
            V.engine_nop().then_inc(S("merged"), 1)
            residual(4, 0)
            norm(6, X)
            dve.wait_ge(S("router_sig"), 1)
            sc = moe[:, 0:32]
            sel = moe[:, 32:64]
            link(tt_(sel.rearrange("p (t e) -> p t e", t=2), sc.rearrange("p (t e) -> p t e", t=2),
                     spread(row("rbias"), 1, 2), ALU.add))
            s4 = sel.rearrange("p (g e) -> p g e", e=4)
            pr = moe[:, 64:112].rearrange("p (g i) -> p g i", i=6)
            for i, (a, b) in enumerate(((0, 1), (0, 2), (0, 3), (1, 2), (1, 3), (2, 3))):
                last = tt_(pr[:, :, i:i + 1], s4[:, :, a:a + 1], s4[:, :, b:b + 1], ALU.add)
            link(last)
            gs = moe[:, 112:120]
            link(V.reduce_max(gs, pr, axis=AX))
            tri = con("tri").rearrange("p (a b) -> p a b", a=4)

            def ranks(dst, v, n, w1, w2):
                for g in range(n):
                    a = spread(v[:, g, :], 1, 4)
                    b = spread(v[:, g, :], 2, 4)
                    tt_(w1[:, g], a, b, ALU.is_gt)
                    last = tt_(w2[:, g], a, b, ALU.is_equal)
                link(last)
                link(tt_(w2, w2, spread(tri, 1, n)))
                link(tt_(w1, w1, w2, ALU.add))
                link(V.reduce_sum(dst, w1, axis=AX))

            rk = moe[:, 120:152]
            ranks(rk.rearrange("p (g e) -> p g e", e=4), s4, 8, moe[:, 152:280].rearrange("p (g a b) -> p g a b", g=8, a=4),
                  moe[:, 280:408].rearrange("p (g a b) -> p g a b", g=8, a=4))
            gk = moe[:, 408:416]
            ranks(gk.rearrange("p (g e) -> p g e", e=4), gs.rearrange("p (g e) -> p g e", e=4), 2,
                  moe[:, 416:448].rearrange("p (g a b) -> p g a b", g=2, a=4),
                  moe[:, 448:480].rearrange("p (g a b) -> p g a b", g=2, a=4))
            link(ts(rk, rk, 2.0, None, ALU.is_lt))
            link(ts(gk, gk, 1.0, None, ALU.is_lt))
            gt = moe[:, 480:512]
            link(tt_(gt, sc, rk))
            g8 = gt.rearrange("p (g e) -> p g e", e=4)
            link(tt_(g8, g8, spread(gk, 2, 4)))
            link(V.reduce_sum(moe[:, 512:514], gt.rearrange("p (t e) -> p t e", t=2), axis=AX))
            link(V.reciprocal(moe[:, 514:516], moe[:, 512:514]))
            link(tt_(gt.rearrange("p (t e) -> p t e", t=2), gt.rearrange("p (t e) -> p t e", t=2),
                     spread(moe[:, 514:516], 2, 16)))
            link(V.memset(accY[:, :, :], 0.0))
            with dve.Fori(0, NEXP // 4) as it:
                e = it * 4
                for j in range(4):
                    for f in range(4):
                        dve.wait_ge(S("merge_act"), 32 + 4 * j + f + 1 + e * 4)
                        if f == 0:
                            dve.wait_ge(S("res"), 20 + 4 * j - 4 + e * 4)
                        tt_(HT[:, j % 2, f, :], tmp[:, f % 2, 0:SEQ], ps[:, 4 + f % 2, SEQ:2 * SEQ]) \
                            .then_inc(S("merge_out"), 1)
                    for n in range(2):
                        for tt in range(TT):
                            m = 2 * n + tt
                            dve.wait_ge(S("res"), 20 + 4 * j + m + 1 + e * 4)
                            if m == 0:
                                dve.wait_ge(S("res_out"), 20 + 4 * j + e * 4)
                            y = accY[:, tt, n * W:(n + 1) * W]
                            stt(y, ps[:, m, :], gt[:, bass.ds(16 * tt + e + j, 1)], y).then_inc(S("res_out"), 1)
            dve.wait_ge(S("res_out"), 20 + 4 * NEXP)
            for tt in range(TT):
                link(tt_(accY[:, tt, :], accY[:, tt, :], G[:, 1, :]))
                last = tt_(X[:, tt, :], X[:, tt, :], accY[:, tt, :], ALU.add)
            last.then_inc(S("final_x"), 1)
            dve.wait_ge(S("norm_sq"), 16)
            rstd(ss[:, 4:6], ss[:, 2:4], 1.0 / D)
            dve.wait_ge(S("final_gain"), 16)
            for tt in range(TT):
                stt(xs[:, tt, :], X[:, tt, :], ss[:, 4 + tt:5 + tt], G[:, 2, :], ALU.mult, ALU.mult).then_inc(S("final_done"), 1)


def kernel(**inputs):
    import concourse.bacc as _bacc
    from concourse.bass_utils import run_bass_kernel_spmd as _run

    a = {n: np.asarray(v) for n, v in inputs.items()}
    nc = _bacc.Bacc("TRN2", target_bir_lowering=False, num_devices=1)

    def col(v):
        return v.reshape(-1, P).T

    whole = ("x", "ctx_2", "ada_w", "ada_b", "mlp_w1", "mlp_w2", "even_w_in", "even_w_out", "mla_w_uq", "mla_w_ukv",
             "odd_w_in", "odd_w_out", "w_mod_2", "b_mod_2", "w_in_2", "w_branch_2", "w_out_2", "w_router_2",
             "w_expert_gu_2", "w_expert_down_2", "final_norm_g_2")
    arr = {n: np.ascontiguousarray(a[n]) for n in whole}
    arr["positions"] = np.ascontiguousarray(a["positions"].reshape(TT, P).T)
    arr["cols"] = np.ascontiguousarray(np.concatenate(
        [col(a["c"]), col(a["c_2"]), col(a["c_ctx_2"]), col(a["ada_b"]), col(a["b_mod_2"]), col(a["norm_mix"]),
         col(a["norm_mlp"]), col(a["norm1_g_2"]), col(a["norm2_g_2"]), col(a["mla_q_lat_norm"]), col(a["mla_kv_lat_norm"]),
         col(a["diff_subln"]), a["conv_w_2"][0].reshape(TAPS, 4, P).transpose(2, 1, 0).reshape(P, -1), col(a["conv_b_2"]),
         col(a["conv_norm_g_2"])], 1))
    arr["rows"] = np.ascontiguousarray(np.concatenate(
        [a[n].reshape(-1) for n in ("mla_q_norm", "mla_k_norm", "dil_q_norm", "dil_k_norm", "diff_q_norm", "diff_k_norm",
                                    "moba_q_norm", "moba_k_norm", "q_norm_g_2", "k_norm_g_2", "diff_lambda",
                                    "router_bias_2")]))
    rpb = np.ascontiguousarray(a["na_rpb_2"][0])
    i = rpb.itemsize
    flat = np.lib.stride_tricks.as_strided(rpb.reshape(-1)[7 * 31 + 15:], shape=(8, 4, 64, 4, 64),
                                           strides=(15 * 31 * i, -31 * i, -i, 31 * i, i))
    arr["na_bias"] = np.ascontiguousarray(flat).reshape(8, SEQ, SEQ)
    arr["consts"], arr["dft"] = shape_constants()
    aps = {n: nc.dram_tensor("in_" + n, v.shape, mybir.dt.from_np(v.dtype), kind="ExternalInput").ap() for n, v in arr.items()}
    out = nc.dram_tensor("out_0", (1, SEQ, D), F32, kind="ExternalOutput").ap()
    program(nc, aps, out)
    r = _run(nc, [{"in_" + n: v for n, v in arr.items()}], core_ids=[0])
    return r.results[0]["out_0"]
```

```python
from contextlib import ExitStack

import numpy as np

import concourse.bass as bass
from concourse import mybir

F32 = mybir.dt.float32
I32 = mybir.dt.int32
ALU = mybir.AluOpType
ACT = mybir.ActivationFunctionType
AX = mybir.AxisListType.X

P = 128
D = 1024
SEQ = 256
KT = D // P
TT = SEQ // P
W = 512
FF = 4 * D
HD = 64
EPS = 1e-6
NEG = -1e30
QR, KVR, NOPE, ROPE, MH = 384, 256, 64, 32, 8
QKD = NOPE + ROPE
DIL = ((128, 1), (512, 4), (2048, 16))
DG, DH = 3, 4
E_IN = QR + KVR + ROPE + 3 * DG * DH * HD
E_OUT = MH * HD + DH * HD
O_IN = 6 * 512
NEXP, EFF = 16, 512
GATE0 = 3840
TAPS = 31
PADT = SEQ + TAPS - 1
LAM_INIT = 0.8 - 0.6 * float(np.exp(-0.3))
RING = 4
SLOT = KT * W
NST = 8
TWO_PI = 2.0 * float(np.pi)
PI_LO = 3.1415925

CONSTS = (("ident", 128), ("c0", 128), ("c1", 256), ("d0", 384), ("d1", 768), ("na", 512), ("ax", 128),
          ("invf", 48), ("tri", 16))
DFT = (("CL", 512), ("SL", 512), ("CD", 128), ("SD", 128))
COLS = (("c", 24), ("adab", 144), ("nmix", 16), ("nmlp", 16), ("n1", 8), ("n2", 8), ("qlat", 3), ("kvlat", 2),
        ("subln", 1), ("convw", 124), ("convb", 4), ("convg", 4))
ROWS = (("mlaq", 96), ("mlak", 96), ("dilq", 64), ("dilk", 64), ("diffq", 64), ("diffk", 64), ("mobaq", 64),
        ("mobak", 64), ("gqaq", 64), ("gqak", 64), ("lam", 256), ("rbias", 16))


def offsets(parts):
    at, out = 0, {}
    for name, n in parts:
        out[name] = (at, at + n)
        at += n
    return out, at


def shape_constants():
    out = {"ident": np.eye(P)}
    q, k = np.arange(SEQ)[:, None], np.arange(SEQ)[None, :]
    neg = lambda keep: np.where(keep, 0.0, NEG)
    causal = neg(q >= k)
    out["c0"], out["c1"] = causal[:P, :P], causal[P:]
    dil = [neg((q >= k) & ((q - k) % r == 0) & (q - k <= w)) for w, r in DIL]
    out["d0"] = np.concatenate([m[:P, :P] for m in dil], 1)
    out["d1"] = np.concatenate([m[P:] for m in dil], 1)
    qc, kc = q % 64, k % 64
    start = np.clip(qc - 8, 0, 48)
    na = neg((kc >= start) & (kc < start + 16))
    out["na"] = np.concatenate([na[:P], na[P:]], 1)
    t = np.arange(SEQ)
    f = np.float32(10000.0) ** (-np.arange(16, dtype=np.float32) / np.float32(16))
    f32_ = np.float32(10000.0) ** (-np.arange(32, dtype=np.float32) / np.float32(32))
    ang = np.concatenate([(t // 64).astype(np.float32)[:, None] * f, (t % 64).astype(np.float32)[:, None] * f], 1)
    cs, sn = np.cos(ang.astype(np.float64)), np.sin(ang.astype(np.float64))
    out["ax"] = np.concatenate([cs[:P], cs[P:], sn[:P], sn[P:]], 1)
    out["invf"] = np.tile(np.concatenate([f, f32_])[None], (P, 1))
    out["tri"] = np.tile((np.arange(4)[None, :] < np.arange(4)[:, None]).astype(np.float32).reshape(1, 16), (P, 1))
    al = 2 * np.pi * ((q * k) % SEQ) / SEQ
    tiles = lambda m: m.reshape(TT, P, SEQ).transpose(1, 0, 2).reshape(P, -1)
    out["CL"], out["SL"] = tiles(np.cos(al)), tiles(np.sin(al))
    d = np.arange(P)
    ad = 2 * np.pi * ((d[:, None] * d[None, :]) % P) / P
    norm = 1.0 / np.sqrt(SEQ * P)
    out["CD"], out["SD"] = np.cos(ad) * norm, -np.sin(ad) * norm
    return [np.ascontiguousarray(np.concatenate([out[n] for n, _ in part], 1).astype(np.float32)) for part in (CONSTS, DFT)]


def weight_stream(t):
    S = []

    def add(name, src, k, n):
        S.append((name, src.rearrange("(k p) n -> p k n", p=P), k, n))

    def mod(l, j):
        w = t["ada_w"][l] if l < 2 else t["w_mod_2"][0]
        add(("mod", l, j), w[:, j * W:(j + 1) * W], KT, W)

    for j in range(4):
        mod(0, j)
    for i in range(6):
        n = min(W, E_IN - i * W)
        add(("ein", i), t["even_w_in"][0][:, i * W:i * W + n], KT, n)
        mod(0, 4 + i)
    mod(0, 10)
    mod(0, 11)
    add(("uq",), t["mla_w_uq"][0].rearrange("r h d -> r (h d)"), 3, 768)
    add(("ukv",), t["mla_w_ukv"][0].rearrange("r h d -> r (h d)"), 2, 1024)
    for n in range(2):
        add(("eout", n), t["even_w_out"][0][:, n * W:(n + 1) * W], 6, W)

    def mlp(l):
        for j in range(FF // W):
            add(("w1", l, j), t["mlp_w1"][l][:, j * W:(j + 1) * W], KT, W)
            for m in mod_in_mlp(j):
                mod(l + 1, m)
            add(("w2", l, j), t["mlp_w2"][l][j * W:(j + 1) * W, :], 4, D)

    mlp(0)
    for i in range(6):
        add(("oin", i), t["odd_w_in"][0][:, i * W:(i + 1) * W], KT, W)
    for n in range(2):
        add(("oout", n), t["odd_w_out"][0][:, n * W:(n + 1) * W], KT, W)
    mlp(1)
    for i, (a, n) in enumerate(IN2):
        add(("in2", i), t["w_in_2"][0][:, a:a + n], KT, n)
    for b in range(4):
        add(("gate", 2 * b), t["w_in_2"][0][:, GATE0 + 2 * b * W:GATE0 + (2 * b + 1) * W], KT, W)
        add(("branch", b), t["w_branch_2"][0, b], 4, D)
        add(("gate", 2 * b + 1), t["w_in_2"][0][:, GATE0 + (2 * b + 1) * W:GATE0 + (2 * b + 2) * W], KT, W)
    for n in range(2):
        add(("out2", n), t["w_out_2"][0][:, n * W:(n + 1) * W], KT, W)
    return S


def mod_in_mlp(j):
    return (j,) if j < 4 else (2 * j - 4, 2 * j - 3)


IN2 = ((0, 512), (512, 256), (768, 512), (1280, 512), (1792, 512), (2304, 512), (2816, 512), (3328, 512))
CTX_AT = {1: 0, 3: 256, 4: 768}
MODSEQ = [(0, j) for j in range(12)] + [(1, j) for j in range(12)]
for _j in range(12):
    MODSEQ += [(2, _j)] + ([(3, _j)] if _j < 4 else [])


def spread(ap, dim, n):
    ap = ap.unsqueeze(dim)
    shape = list(ap.shape)
    shape[dim] = n
    return ap.broadcast_to(shape)


def units():
    out = []
    for ph, heads in (("dil", DH), ("mla", MH), ("diff", 4), ("moba", 8), ("gqa", 8), ("na", 8)):
        out += [(ph, h, t) for h in range(heads) for t in range(TT)]
    return out


def program(nc, t, out):
    stream = weight_stream(t)
    number = {s[0]: n for n, s in enumerate(stream)}
    NSTREAM = len(stream)
    CO, NCO = offsets(CONSTS)
    CC, NCC = offsets(COLS)
    CR, NCR = offsets(ROWS)
    UNITS = units()
    ctx = ExitStack()
    with ctx:
        def sb(name, n, dt=F32):
            return ctx.enter_context(nc.sbuf_tensor(name, [P, n], dt))

        sems = {}

        def S(name):
            if name not in sems:
                sems[name] = ctx.enter_context(nc.semaphore(name))
            return sems[name]

        ring = sb("ring", RING * SLOT)
        consts = sb("consts", NCO)
        cols = sb("cols", NCC)
        rows = sb("rows", NCR)
        X = sb("X", TT * D)[:, :].rearrange("p (t n) -> p t n", t=TT)
        hTb = sb("hT", KT * SEQ)
        hT = hTb[:, :].rearrange("p (k n) -> p k n", k=KT)
        U = sb("U", 6144)
        AUX = sb("AUX", 4608)
        QK = sb("QK", 4608)
        OTb = sb("OT", KT * SEQ)
        OT = OTb[:, :].rearrange("p (k n) -> p k n", k=KT)
        G = sb("G", 4 * D)[:, :].rearrange("p (s n) -> p s n", s=4)
        Eb = sb("E", 3 * 768)[:, :].rearrange("p (s n) -> p s n", s=3)
        PTb = sb("PT", 2 * 768)[:, :].rearrange("p (s n) -> p s n", s=2)
        scratch = sb("scratch", 4 * W)
        acc = scratch[:, 0:2 * W].rearrange("p (s n) -> p s n", s=2)
        tmp = scratch[:, 2 * W:4 * W].rearrange("p (s n) -> p s n", s=2)
        nab = scratch[:, :].rearrange("p (s t n) -> p s t n", s=2, t=2)
        ones = sb("ones", P)
        zero = sb("zero", 1)
        cond = sb("cond", 24)
        modc = sb("modc", 4 * 48)[:, :].rearrange("p (l v k) -> p l v k", l=4, v=6)
        coef = sb("coef", 8 * 8)[:, :].rearrange("p (i k) -> p i k", i=8)
        ss = sb("ss", 32)
        wn = sb("wn", 3 * 256)[:, :].rearrange("p (s n) -> p s n", s=3)
        rope = sb("rope", 2 * 2 * 48)
        posi = sb("posi", 2, I32)
        posf = sb("posf", 2)
        mx = sb("mx", NST * 2)[:, :].rearrange("p (s n) -> p s n", s=NST)
        sm = sb("sm", NST * 2)[:, :].rearrange("p (s n) -> p s n", s=NST)
        rc = sb("rc", NST * 2)[:, :].rearrange("p (s n) -> p s n", s=NST)
        lam = sb("lam", 8)
        moe = QK[:, 0:640]
        rw = moe[:, 0:480].rearrange("p (s n) -> p s n", s=5)
        wrt = sb("wrt", KT * NEXP)
        ps = ctx.enter_context(nc.psum_tensor("ps", [P, 8, W], F32))

        DF, NDFT = offsets(DFT)
        dft_at = CO["c0"][0]
        assert CO["d1"][1] - dft_at >= NDFT
        dft = lambda n: consts[:, dft_at + DF[n][0]:dft_at + DF[n][1]]
        con = lambda n: consts[:, CO[n][0]:CO[n][1]]
        col = lambda n: cols[:, CC[n][0]:CC[n][1]]
        row = lambda n: rows[:, CR[n][0]:CR[n][1]]
        ident = con("ident")
        Cos = rope[:, 0:96].rearrange("p (t n) -> p t n", t=2)
        Sin = rope[:, 96:192].rearrange("p (t n) -> p t n", t=2)
        axcs = con("ax")[:, 0:64].rearrange("p (t n) -> p t n", t=2)
        axsn = con("ax")[:, 64:128].rearrange("p (t n) -> p t n", t=2)

        Ue = U[:, 0:2 * E_IN].rearrange("p (t n) -> p t n", t=2)
        Uo = U[:, :].rearrange("p (t n) -> p t n", t=2)
        U2 = U[:, 0:2 * 2816].rearrange("p (t n) -> p t n", t=2)
        Qm = AUX[:, 0:1536].rearrange("p (t h d) -> p t h d", t=2, h=MH)
        Km = AUX[:, 1536:3072].rearrange("p (t h d) -> p t h d", t=2, h=MH)
        Vm = AUX[:, 3072:4096].rearrange("p (t h d) -> p t h d", t=2, h=MH)
        sqb = PTb
        cT = hTb[:, 0:5 * SEQ].rearrange("p (k n) -> p k n", k=5)
        hc = AUX[:, 0:2048].rearrange("p (k n) -> p k n", k=KT)
        ctx_x = QK[:, 0:2048].rearrange("p (t n) -> p t n", t=2)
        xs = Eb.rearrange("p s n -> p (s n)")[:, 0:2048].rearrange("p (t n) -> p t n", t=2)
        Uc = AUX[:, 2048:4608].rearrange("p (t n) -> p t n", t=2)
        HT = U[:, 0:2048].rearrange("p (s k n) -> p s k n", s=2, k=4)
        M2 = U[:, 0:2048].rearrange("p (k n) -> p k n", k=KT)
        YF = AUX[:, 0:1024].rearrange("p (k n) -> p k n", k=4)
        Z = YF
        YC = AUX[:, 1024:2048].rearrange("p (k n) -> p k n", k=4)
        Z12 = QK[:, 0:2048].rearrange("p (g n) -> p g n", g=4)
        convy = YC
        convs = QK[:, 2048:3072].rearrange("p (k n) -> p k n", k=4)
        accY = AUX[:, 0:2048].rearrange("p (t n) -> p t n", t=2)

        def chunk(name):
            n = number[name]
            _, _, k, w = stream[n]
            s = n % RING
            return ring[:, s * SLOT:s * SLOT + k * w].rearrange("p (k n) -> p k n", k=k)

        def arrived(eng, name):
            n = number[name]
            eng.wait_ge(S(f"loaded{n % RING}"), 16 * (n // RING + 1))
            return chunk(name)

        def last_use(name):
            kind = name[0]
            if kind == "mod":
                return S("mod_acc"), 1 + max(q for q, (l, j) in enumerate(MODSEQ) if (min(l, 2), j) == name[1:])
            if kind in ("eout", "oout", "out2"):
                return S("res"), 4 * {"eout": 0, "oout": 2, "out2": 4}[kind] + 2 * name[1] + 2
            if kind == "w1":
                return S("hid"), 32 * name[1] + 4 * name[2] + 4
            if kind == "w2":
                l, j = name[1:]
                return (S("res"), 8 * l + 8) if j == 7 else (S("w2_used"), 7 * l + j + 1)
            if kind == "gate":
                return S("merge"), 4 * name[1] + 4
            if kind == "branch":
                return S("merge"), 8 * name[1] + 8
            if kind == "in2" and name[1] >= 6:
                return S("glu"), 4
            ph = {"uq": "lat", "ukv": "lat"}.get(kind, kind)
            return S("proj"), g0[ph] + 1 + max(j for j, g in enumerate(groups(ph)) if g[0] == name)

        loads_of = [len(range(s, NSTREAM, RING)) for s in range(RING)]

        def last_in(s):
            return stream[max(range(s, NSTREAM, RING))][0]

        def qkt(off, tiles):
            return QK[:, off:off + tiles * SEQ].rearrange("p (k n) -> p k n", k=tiles)

        mlaQ, mlaK = qkt(0, 8), qkt(2048, 8)
        dilQ, dilK = qkt(0, 6), qkt(1536, 6)
        diffQ, diffK, mobaQ, mobaK = qkt(0, 4), qkt(1024, 4), qkt(2048, 4), qkt(3072, 4)
        gqaQ, gqaK, gqaC = qkt(0, 4), qkt(1024, 1), qkt(1280, 1)
        naQ, naK, naC = qkt(1536, 4), qkt(2560, 4), qkt(3584, 4)

        def half(ap, h, a, n):
            return ap[64 * (h % 2):64 * (h % 2) + 64, h // 2, a:a + n]

        def scores_of(u):
            ph, h, t = u
            nk = P * (t + 1)
            q0 = P * t
            if ph == "mla":
                return [(0, mlaQ[0:QKD, h, q0:q0 + P], mlaK[0:QKD, h, 0:nk], nk)]
            if ph == "dil":
                return [(g * nk, half(dilQ, g * DH + h, q0, P), half(dilK, g * DH + h, 0, nk), nk) for g in range(DG)]
            if ph == "diff":
                return [(m * W, half(diffQ, 2 * h + m, q0, P), half(diffK, 2 * h + m, 0, nk), nk) for m in range(2)]
            if ph == "moba":
                return [(0, half(mobaQ, h, q0, P), half(mobaK, h, 0, nk), nk)]
            if ph == "gqa":
                r = 64 * (h // 4)
                q = gqaQ[r:r + 64, h % 4, q0:q0 + P]
                return [(0, q, gqaK[r:r + 64, 0, :], SEQ), (SEQ, q, gqaC[r:r + 64, 0, :], SEQ)]
            q = half(naQ, h, q0, P)
            return [(0, q, half(naK, h, 0, SEQ), SEQ), (SEQ, q, half(naC, h, 0, SEQ), SEQ)]

        def softmax_of(u):
            ph, h, t = u
            nk = P * (t + 1)
            if ph == "dil":
                return [(0, DG * nk, con(f"d{t}"))]
            if ph == "diff":
                return [(m * nk, nk, con(f"c{t}")) for m in range(2)]
            if ph in ("mla", "moba"):
                return [(0, nk, con(f"c{t}"))]
            if ph == "gqa":
                return [(0, 2 * SEQ, zero[:, :].broadcast_to([P, W]))]
            return [(0, 2 * SEQ, nab[:, h % 2, t, :])]

        def values_of(u):
            ph, h, t = u
            kb = range(t + 1)
            if ph == "mla":
                return [((0, 64), [Vm[:, b, h, :] for b in kb])]
            if ph == "dil":
                v0 = QR + KVR + ROPE + 2 * DG * DH * HD
                return [((0, 64), [Ue[:, b, v0 + (g * DH + h) * HD:v0 + (g * DH + h + 1) * HD] for g in range(DG) for b in kb])]
            if ph == "diff":
                return [((m * P, (m + 1) * P), [Uo[:, b, 1024 + h * P:1024 + (h + 1) * P] for b in kb]) for m in range(2)]
            if ph == "moba":
                return [((0, 64), [Uo[:, b, 2560 + h * HD:2560 + (h + 1) * HD] for b in kb])]
            if ph == "gqa":
                g = h // 4
                return [((0, 64), [U2[:, b, 640 + g * HD:640 + (g + 1) * HD] for b in range(2)]
                         + [Uc[:, b, 128 + g * HD:128 + (g + 1) * HD] for b in range(2)])]
            return [((0, 64), [U2[:, b, 1792 + h * HD:1792 + (h + 1) * HD] for b in range(2)]
                     + [Uc[:, b, 768 + h * HD:768 + (h + 1) * HD] for b in range(2)])]

        def blocks_of(u):
            return sum(len(v) for _, v in values_of(u))

        OkE = hTb[:, 0:1536].rearrange("p (t n) -> p t n", t=2)
        OkO = AUX[:, 0:2048].rearrange("p (t n) -> p t n", t=2)
        OkB = U2[:, :, 768:1792]

        def output_of(u):
            ph, h, t = u
            if ph == "diff":
                return OkO[:, t, h * P:(h + 1) * P]
            ok = {"mla": OkE, "dil": OkE, "moba": OkO, "gqa": OkB, "na": OkB}[ph]
            c = (0 if ph in ("mla", "gqa") else 512) + h * HD
            return ok[:, t, c:c + HD]

        def wide(u):
            return u[0] == "dil"

        def pt_bank(i):
            b = 4 if wide(UNITS[i]) else 4 + i % 2
            return ps[:, b:b + 2, :].rearrange("p b n -> p (b n)") if wide(UNITS[i]) else ps[:, b, :]

        def s_bank(i):
            return ps[:, 2 * (i % 2):2 * (i % 2) + 2, :].rearrange("p b n -> p (b n)")

        def span(ph):
            ids = [i for i, u in enumerate(UNITS) if u[0] == ph]
            return ids[0], ids[-1] + 1

        def tr_list(ph):
            o = QR + KVR + ROPE
            if ph == "mla":
                return [(lambda t, h=h: Qm[:, t, h, :], mlaQ[0:QKD, h, :]) for h in range(MH)] \
                    + [(lambda t, h=h: Km[:, t, h, :], mlaK[0:QKD, h, :]) for h in range(MH)]
            if ph == "dil":
                return [(lambda t, k=k: Ue[:, t, o + k * P:o + (k + 1) * P],
                         (dilQ[:, k, :] if k < 6 else dilK[:, k - 6, :])) for k in range(12)]
            if ph == "odd":
                dst = [diffQ, diffK, None, mobaQ, mobaK]
                return [(lambda t, c=c, k=k: Uo[:, t, c * 512 + k * P:c * 512 + (k + 1) * P], dst[c][:, k, :])
                        for c in (0, 1, 3, 4) for k in range(4)]
            if ph in ("otE", "otO", "otB"):
                ok, n = {"otE": (OkE, 6), "otO": (OkO, 8), "otB": (OkB, 8)}[ph]
                return [(lambda t, k=k: ok[:, t, k * P:(k + 1) * P], OT[:, k, :]) for k in range(n)]
            out_ = []
            for j in range(4):
                out_.append((lambda t, j=j: U2[:, t, j * P:(j + 1) * P], gqaQ[:, j, :]))
            out_.append((lambda t: U2[:, t, 512:640], gqaK[:, 0, :]))
            out_.append((lambda t: Uc[:, t, 0:128], gqaC[:, 0, :]))
            for k in range(4):
                out_.append((lambda t, k=k: U2[:, t, 768 + k * P:768 + (k + 1) * P], naQ[:, k, :]))
                out_.append((lambda t, k=k: U2[:, t, 1280 + k * P:1280 + (k + 1) * P], naK[:, k, :]))
                out_.append((lambda t, k=k: Uc[:, t, 256 + k * P:256 + (k + 1) * P], naC[:, k, :]))
            return out_

        TRPH = ("dil", "mla", "otE", "odd", "otO", "b2", "otB")
        tr0 = {}
        at = 0
        for ph in TRPH:
            tr0[ph] = at
            at += len(tr_list(ph))

        def head_calls(ph):
            out_ = []
            o = QR + KVR + ROPE
            for tt in range(TT):
                r64 = (Cos[:, tt, 16:48], Sin[:, tt, 16:48], 0, False)
                r16 = (Cos[:, tt, 0:16], Sin[:, tt, 0:16], NOPE, False)
                ax = (axcs[:, tt, :], axsn[:, tt, :], 0, True)
                h64 = lambda ap: ap.rearrange("p (h d) -> p h d", d=HD)
                if ph == "dilq":
                    out_.append((h64(Ue[:, tt, o:o + 768]), row("dilq"), HD ** -0.5) + r64)
                if ph == "dilk":
                    out_.append((h64(Ue[:, tt, o + 768:o + 1536]), row("dilk"), None) + r64)
                if ph == "mla":
                    out_.append((Qm[:, tt], row("mlaq"), QKD ** -0.5) + r16)
                    out_.append((Km[:, tt], row("mlak"), None) + r16)
                if ph[:3] == "odd":
                    c = int(ph[3])
                    gn, sc = {0: ("diffq", 0.125), 1: ("diffk", None), 3: ("mobaq", 0.125), 4: ("mobak", None)}[c]
                    out_.append((h64(Uo[:, tt, 512 * c:512 * c + 512]), row(gn), sc) + r64)
                if ph == "gq":
                    out_.append((h64(U2[:, tt, 0:512]), row("gqaq"), 0.125) + ax)
                if ph == "gk":
                    out_.append((h64(U2[:, tt, 512:640]), row("gqak"), None) + ax)
                    out_.append((h64(Uc[:, tt, 0:128]), row("gqak"), None) + (None, None, 0, False))
            return out_

        HPH = ("dilq", "dilk", "mla", "odd0", "odd1", "odd3", "odd4", "gq", "gk")
        hc0 = {}
        at = 0
        for ph in HPH:
            hc0[ph] = at
            at += len(head_calls(ph))

        def calls_until(ph):
            return hc0[ph] + len(head_calls(ph))

        def groups(ph):
            if ph == "ein":
                return [(("ein", i), hT, KT, tt, 0, min(W, E_IN - i * W)) for i in range(6) for tt in range(TT)]
            if ph == "lat":
                return ([(("uq",), cT, 3, tt, c, w) for tt in range(TT) for c, w in ((0, 512), (512, 256))]
                        + [(("ukv",), cT[:, 3:5, :], 2, tt, c, 512) for tt in range(TT) for c in (0, 512)])
            if ph == "oin":
                return [(("oin", i), hT, KT, tt, 0, W) for i in range(6) for tt in range(TT)]
            g = []
            for i in range(6):
                g += [(("in2", i), hT, KT, tt, 0, IN2[i][1]) for tt in range(TT)]
                if i in CTX_AT:
                    g += [(("in2", i), hc, KT, tt, 0, IN2[i][1]) for tt in range(TT)]
            return g

        g0 = {}
        at = 0
        for ph in ("ein", "lat", "oin", "in2"):
            g0[ph] = at
            at += len(groups(ph))

        def small_loads():
            return [(X, t["x"][0].rearrange("(t p) n -> p t n", p=P)), (consts[:, :], t["consts"]), (cols[:, :], t["cols"]),
                    (rows[:, :], t["rows"].partition_broadcast(P)), (posi[:, :], t["positions"]),
                    (wrt[:, :].rearrange("p (k n) -> p k n", k=KT), t["w_router_2"].rearrange("(k p) n -> p k n", p=P))]

        NSMALL = len(small_loads())
        RES = ("eout", "mlp0", "oout", "mlp1", "out2")
        NORMS = ("mix0", "mlp0", "mix1", "mlp1", "mix2", "ctx2", "mlp2")
        block = ctx.enter_context(nc.Block())

        @block.sync
        def _(sp):
            for n, (name, src, k, w) in enumerate(stream):
                if n >= RING:
                    sp.wait_ge(*last_use(stream[n - RING][0]))
                sp.dma_start(chunk(name), src).then_inc(S(f"loaded{n % RING}"), 16)
            def expert_loads(e, first):
                for m in range(12):
                    j, c, s = m // 3, m % 3, m % RING
                    if first and m < RING:
                        sp.wait_ge(*last_use(last_in(s)))
                    else:
                        jj, cc = (m - RING) // 3, (m - RING) % 3
                        if cc < 2:
                            sp.wait_ge(S("merge"), 32 + 4 * jj + 4 + e * 4)
                        else:
                            sp.wait_ge(S("res"), 20 + 4 * jj + 4 + e * 4)
                    if c < 2:
                        src = t["w_expert_gu_2"][0][bass.ds(e + j, 1), :, c * EFF:(c + 1) * EFF]
                        dst = ring[:, s * SLOT:s * SLOT + KT * EFF].rearrange("p (k n) -> p k n", k=KT)
                    else:
                        src = t["w_expert_down_2"][0][bass.ds(e + j, 1), :, :]
                        dst = ring[:, s * SLOT:(s + 1) * SLOT].rearrange("p (k n) -> p k n", k=4)
                    sp.dma_start(dst, src.rearrange("o (k p) n -> p (o k) n", p=P)).then_inc(S(f"loaded{s}"), 16)

            expert_loads(0, True)
            with sp.Fori(1, NEXP // 4) as it:
                expert_loads(it * 4, False)
            sp.wait_ge(S("final_done"), 2)
            sp.dma_start(out[0].rearrange("(t p) n -> p t n", p=P), xs).then_inc(S("stored"), 16)
            sp.wait_ge(S("stored"), 16)

        @block.tensor
        def _(pe):
            mm = nc.tensor.matmul
            pe.wait_ge(S("consts_in"), 16 * NSMALL)
            pe.wait_ge(S("ones_set"), 2)

            def mod_sum(q):
                pe.wait_ge(S("mod_acc"), q + 1)
                if q:
                    pe.wait_ge(S("mod_fin"), q)
                mm(ps[:, 6, :], ones[:, :], acc[:, q % 2, :], start=True, stop=True).then_inc(S("mod_sum"), 1)

            def norm_transposes(i):
                pe.wait_ge(S("norm_scaled"), 2 * (i + 1))
                for k in range(KT):
                    n = KT * i + k
                    if n >= 4 and k % 2 == 0:
                        pe.wait_ge(S("norm_out"), n - 2)
                    for tt in range(TT):
                        last = nc.tensor.transpose(ps[:, 4 + (k // 2) % 2, 256 * (k % 2) + P * tt:256 * (k % 2) + P * tt + P],
                                                   xs[:, tt, k * P:(k + 1) * P], ident)
                    last.then_inc(S("norm_tr"), 1)

            def projections(ph, after=None):
                gs = groups(ph)
                for j, (name, src, nk, tt, c, w) in enumerate(gs):
                    g = g0[ph] + j
                    wt = arrived(pe, name)
                    if g >= 4:
                        pe.wait_ge(S("proj_out"), g - 3)
                    for k in range(nk):
                        last = mm(ps[:, g % 4, 0:w], src[:, k, P * tt:P * tt + P], wt[:, k, c:c + w],
                                  start=(k == 0), stop=(k == nk - 1))
                    last.then_inc(S("proj"), 1)
                    if after and (j + 1 == len(gs) or gs[j + 1][0] != name):
                        after(name)

            def head_transposes(ph, j0=0, j1=None):
                for j, (src, dst) in list(enumerate(tr_list(ph)))[j0:j1]:
                    n = tr0[ph] + j
                    if n >= 4 and n % 2 == 0:
                        pe.wait_ge(S("qkt_out"), n - 2)
                    for tt in range(TT):
                        s = src(tt)
                        d = s.shape[-1]
                        last = nc.tensor.transpose(ps[0:d, 4 + (n // 2) % 2, 256 * (n % 2) + P * tt:256 * (n % 2) + P * tt + P],
                                                   s, ident)
                    last.then_inc(S("qkt"), 1)

            def attention(ph):
                a, b = span(ph)

                def score(i):
                    if i >= 2:
                        pe.wait_ge(S("masked"), i - 1)
                    for c, q, k, n in scores_of(UNITS[i]):
                        last = mm(s_bank(i)[:, c:c + n], q, k, start=True, stop=True)
                    last.then_inc(S("scored"), 1)

                def transposes(i):
                    pe.wait_ge(S("exped"), i + 1)
                    lag = 1 if wide(UNITS[i]) else 2
                    if i >= lag:
                        pe.wait_ge(S("pt_out"), i - lag + 1)
                    for j in range(blocks_of(UNITS[i])):
                        last = nc.tensor.transpose(pt_bank(i)[:, j * P:(j + 1) * P], Eb[:, i % 3, j * P:(j + 1) * P], ident)
                    last.then_inc(S("pt"), 1)

                def weigh(i):
                    pe.wait_ge(S("pt_out"), i + 1)
                    if i >= 2:
                        pe.wait_ge(S("o_out"), i - 1)
                    n = 0
                    for (c0, c1), vs in values_of(UNITS[i]):
                        for j, v in enumerate(vs):
                            last = mm(ps[:, 6 + i % 2, c0:c1], PTb[:, i % 2, n * P:(n + 1) * P], v,
                                      start=(j == 0), stop=(j == len(vs) - 1))
                            n += 1
                    last.then_inc(S("weighed"), 1)

                for i in range(a, b + 3):
                    if i < b:
                        score(i)
                    if a <= i - 2 < b:
                        transposes(i - 2)
                    if a <= i - 3:
                        weigh(i - 3)

            def out_projection(name, nk, r):
                for n in range(2):
                    wt = arrived(pe, (name, n))
                    for tt in range(TT):
                        for k in range(nk):
                            last = mm(ps[:, 2 * n + tt, :], (M2 if name == "out2" else OT)[:, k, P * tt:P * tt + P],
                                      wt[:, k, :], start=(k == 0), stop=(k == nk - 1))
                        last.then_inc(S("res"), 1)

            def mlp(l, q0, r):
                qd = [q0]
                for j in range(FF // W):
                    w1 = arrived(pe, ("w1", l, j))
                    for f in range(4):
                        n = 32 * l + 4 * j + f
                        if n >= 2:
                            pe.wait_ge(S("hid_read"), n - 1)
                        for k in range(KT):
                            last = mm(ps[:, 4 + n % 2, 0:SEQ], w1[:, k, f * P:(f + 1) * P], hT[:, k, :],
                                      start=(k == 0), stop=(k == KT - 1))
                        last.then_inc(S("hid"), 1)
                    w2 = arrived(pe, ("w2", l, j))
                    for k in range(4):
                        pe.wait_ge(S("hid_out"), 32 * l + 4 * j + k + 1)
                        for n in range(2):
                            for tt in range(TT):
                                last = mm(ps[:, 2 * n + tt, :], HT[:, j % 2, k, P * tt:P * tt + P],
                                          w2[:, k, n * W:(n + 1) * W],
                                          start=(j == 0 and k == 0), stop=(j == 7 and k == 3))
                                if j == 7 and k == 3:
                                    last.then_inc(S("res"), 1)
                    if j < 7:
                        last.then_inc(S("w2_used"), 1)
                    for m in mod_in_mlp(j):
                        mod_sum(qd[0])
                        qd[0] += 1
                        if l == 1 and m < 4:
                            mod_sum(qd[0])
                            qd[0] += 1

            for q in range(4):
                mod_sum(q)
            norm_transposes(0)
            pe.wait_ge(S("norm_out"), KT)
            projections("ein", after=lambda name: mod_sum(4 + name[1]) if name[0] == "ein" else None)
            pe.wait_ge(S("lat_scaled"), 1)
            for k in range(5):
                if k == 4:
                    pe.wait_ge(S("lat_out"), 2)
                for tt in range(TT):
                    last = nc.tensor.transpose(ps[:, 4 + (k // 2) % 2, 256 * (k % 2) + P * tt:256 * (k % 2) + P * tt + P],
                                               Ue[:, tt, k * P:(k + 1) * P], ident)
                last.then_inc(S("lat_tr"), 1)
            pe.wait_ge(S("lat_out"), 5)
            projections("lat")
            mod_sum(10)
            mod_sum(11)
            pe.wait_ge(S("roped"), calls_until("dilk"))
            head_transposes("dil")
            pe.wait_ge(S("qkt_out"), tr0["mla"])
            pe.wait_ge(S("proj_out"), g0["oin"])
            pe.wait_ge(S("mod_fin"), 12)
            attention("dil")
            pe.wait_ge(S("roped"), calls_until("mla"))
            head_transposes("mla")
            pe.wait_ge(S("qkt_out"), tr0["otE"])
            attention("mla")
            pe.wait_ge(S("o_out"), span("mla")[1])
            head_transposes("otE")
            pe.wait_ge(S("qkt_out"), tr0["odd"])
            out_projection("eout", 6, 0)
            norm_transposes(1)
            pe.wait_ge(S("norm_out"), 2 * KT)
            mlp(0, 12, 1)
            norm_transposes(2)
            pe.wait_ge(S("norm_out"), 3 * KT)
            def after_odd(name):
                if name[1] == 4:
                    pe.wait_ge(S("roped"), calls_until("odd1"))
                    head_transposes("odd", 0, 8)

            projections("oin", after_odd)
            pe.wait_ge(S("qkt_out"), tr0["odd"] + 8)
            pe.wait_ge(S("proj_out"), g0["in2"])
            attention("diff")
            pe.wait_ge(S("roped"), calls_until("odd4"))
            head_transposes("odd", 8, 16)
            pe.wait_ge(S("qkt_out"), tr0["otO"])
            attention("moba")
            pe.wait_ge(S("sub_done"), 1)
            pe.wait_ge(S("o_out"), span("moba")[1])
            head_transposes("otO")
            pe.wait_ge(S("qkt_out"), tr0["b2"])
            out_projection("oout", 8, 2)
            norm_transposes(3)
            pe.wait_ge(S("norm_out"), 4 * KT)
            mlp(1, 24, 3)
            norm_transposes(4)
            norm_transposes(5)
            pe.wait_ge(S("norm_out"), 6 * KT)
            def after_b2(name):
                if name[1] == 3:
                    pe.wait_ge(S("roped"), calls_until("gk"))
                    head_transposes("b2", 0, 6)
                if name[1] == 5:
                    head_transposes("b2", 6, None)

            projections("in2", after_b2)
            pe.wait_ge(S("qkt_out"), tr0["otB"])
            wa = arrived(pe, ("in2", 6))
            wb = arrived(pe, ("in2", 7))
            for f in range(4):
                if f >= 2:
                    pe.wait_ge(S("glu_out"), f - 1)
                for wt, c in ((wa, 0), (wb, SEQ)):
                    for k in range(KT):
                        last = mm(ps[:, 4 + f % 2, c:c + SEQ], wt[:, k, f * P:(f + 1) * P], hT[:, k, :],
                                  start=(k == 0), stop=(k == KT - 1))
                last.then_inc(S("glu"), 1)
            pe.wait_ge(S("glu_out"), 4)
            pe.wait_ge(S("proj_out"), g0["in2"] + len(groups("in2")))
            attention("gqa")
            attention("na")
            pe.wait_ge(S("pt_out"), len(UNITS))
            pe.wait_ge(S("o_out"), len(UNITS))
            pe.wait_ge(S("dft_in"), 16)
            CL = dft("CL").rearrange("p (t n) -> p t n", t=2)
            SL = dft("SL").rearrange("p (t n) -> p t n", t=2)
            for g in range(4):
                for m, c in ((CL, 0), (SL, SEQ)):
                    for tt in range(TT):
                        last = mm(ps[:, g, c:c + SEQ], U2[:, tt, 2304 + g * P:2304 + (g + 1) * P], m[:, tt, :],
                                  start=(tt == 0), stop=(tt == TT - 1))
                last.then_inc(S("dft1"), 1)
            for g in range(4):
                pe.wait_ge(S("dft1_out"), g + 1)
                b, c = 4 + g // 2, SEQ * (g % 2)
                mm(ps[:, b, c:c + SEQ], dft("CD"), Z12[:, g, 0:SEQ], start=True, stop=False)
                mm(ps[:, b, c:c + SEQ], dft("SD"), Z12[:, g, SEQ:2 * SEQ], start=False, stop=True).then_inc(S("dft2"), 1)
            pe.wait_ge(S("dft2_out"), 4)
            pe.wait_ge(S("conv_sq"), 1)
            for k in range(4):
                last = mm(ps[:, 6, 0:SEQ], ones[:, :], convs[:, k, :], start=(k == 0), stop=(k == 3))
            last.then_inc(S("conv_sum"), 1)
            head_transposes("otB")
            pe.wait_ge(S("dft2_out"), 4)
            pe.wait_ge(S("conv_out"), 4)
            pe.wait_ge(S("qkt_out"), tr0["otB"] + 8)
            for b in range(4):
                wb = None
                for hf in range(2):
                    wg = arrived(pe, ("gate", 2 * b + hf))
                    if wb is None:
                        wb = arrived(pe, ("branch", b))
                    y = (OT[:, 0:4, :], OT[:, 4:8, :], YF, YC)[b]
                    for f in range(4):
                        n = 8 * b + 4 * hf + f
                        if n >= 2:
                            pe.wait_ge(S("merge_out"), n - 1)
                        for k in range(KT):
                            mm(ps[:, 4 + n % 2, 0:SEQ], wg[:, k, f * P:(f + 1) * P], hT[:, k, :],
                               start=(k == 0), stop=(k == KT - 1))
                        for k in range(4):
                            last = mm(ps[:, 4 + n % 2, SEQ:2 * SEQ], wb[:, k, (4 * hf + f) * P:(4 * hf + f + 1) * P], y[:, k, :],
                                      start=(k == 0), stop=(k == 3))
                        last.then_inc(S("merge"), 1)
            pe.wait_ge(S("merged"), 1)
            out_projection("out2", 8, 4)
            norm_transposes(6)
            pe.wait_ge(S("norm_out"), 7 * KT)
            wr = wrt[:, :].rearrange("p (k n) -> p k n", k=KT)
            for tt in range(TT):
                for k in range(KT):
                    last = mm(ps[:, 6, 16 * tt:16 * tt + 16], hT[:, k, P * tt:P * tt + P], wr[:, k, :],
                              start=(k == 0), stop=(k == KT - 1))
            last.then_inc(S("logits"), 1)
            def loaded(e, m):
                s = m % RING
                pe.wait_ge(S(f"loaded{s}"), 16 * (loads_of[s] + m // RING + 1) + e * 12)

            with pe.Fori(0, NEXP // 4) as it:
                e = it * 4
                for j in range(4):
                    sl = [(3 * j + c) % RING for c in range(3)]
                    wa, wb = (ring[:, s * SLOT:(s + 1) * SLOT].rearrange("p (k n) -> p k n", k=KT) for s in sl[0:2])
                    wd = ring[:, sl[2] * SLOT:(sl[2] + 1) * SLOT].rearrange("p (k n) -> p k n", k=4)
                    loaded(e, 3 * j)
                    loaded(e, 3 * j + 1)
                    for f in range(4):
                        pe.wait_ge(S("merge_out"), 32 + 4 * j + f - 1 + e * 4)
                        for wt, c in ((wa, 0), (wb, SEQ)):
                            for k in range(KT):
                                last = mm(ps[:, 4 + f % 2, c:c + SEQ], wt[:, k, f * P:(f + 1) * P], hT[:, k, :],
                                          start=(k == 0), stop=(k == KT - 1))
                        last.then_inc(S("merge"), 1)
                    loaded(e, 3 * j + 2)
                    pe.wait_ge(S("res_out"), 20 + 4 * j + e * 4)
                    for k in range(4):
                        pe.wait_ge(S("merge_out"), 32 + 4 * j + k + 1 + e * 4)
                        for n in range(2):
                            for tt in range(TT):
                                last = mm(ps[:, 2 * n + tt, :], HT[:, j % 2, k, P * tt:P * tt + P],
                                          wd[:, k, n * W:(n + 1) * W], start=(k == 0), stop=(k == 3))
                                if k == 3:
                                    last.then_inc(S("res"), 1)

        @block.scalar
        def _(act):
            A = nc.scalar.activation
            for dst, src in small_loads():
                act.dma_start(dst, src).then_inc(S("consts_in"), 16)
            act.wait_ge(S("consts_in"), 16 * NSMALL)
            A(cond[:, :], col("c"), ACT.Silu).then_inc(S("cond"), 1)
            act.wait_ge(S("angles"), 2)
            A(rope[:, 0:192], rope[:, 0:192], ACT.Sin).then_inc(S("sines"), 1)
            A(lam[:, 2:4], lam[:, 0:2], ACT.Exp).then_inc(S("lam_exp"), 1)

            def square_sums(i, src):
                for tt in range(TT):
                    A(xs[:, tt, :], src[:, tt, :], ACT.Square, accum_out=ss[:, 2 * (i % 2) + tt:2 * (i % 2) + tt + 1]) \
                        .then_inc(S("norm_sq"), 1)

            def norm_out(i, dst):
                l, v = ((0, 0), (0, 3), (1, 0), (1, 3), (2, 0), (3, 0), (2, 3))[i]
                act.wait_ge(S("coef"), i + 1)
                for k in range(KT):
                    act.wait_ge(S("norm_tr"), KT * i + (k | 1) + 1)
                    A(dst[:, k, :], ps[:, 4 + (k // 2) % 2, 256 * (k % 2):256 * (k % 2) + 256], ACT.Identity,
                      bias=modc[:, l, v, k:k + 1], scale=coef[:, i, k:k + 1]).then_inc(S("norm_out"), 1)

            def proj_out(ph, place, only=None):
                for j, (name, _, nk, tt, c, w) in enumerate(groups(ph)):
                    if only is not None and name[1] not in only:
                        continue
                    g = g0[ph] + j
                    act.wait_ge(S("proj"), g + 1)
                    cps = place(j, name, tt, c, w, ps[:, g % 4, 0:w])
                    for dst, src, *scale in cps:
                        last = A(dst, src, ACT.Copy, scale=scale[0] if scale else 1.0)
                    last.then_inc(S("proj_out"), 1)

            def qkt_out(ph, j0=0, j1=None):
                for j, (src, dst) in list(enumerate(tr_list(ph)))[j0:j1]:
                    n = tr0[ph] + j
                    act.wait_ge(S("qkt"), (n | 1) + 1)
                    d = dst.shape[0]
                    gain = col("subln")[:, 0:1] if ph == "otO" and j < 4 else 1.0
                    A(dst, ps[0:d, 4 + (n // 2) % 2, 256 * (n % 2):256 * (n % 2) + 256], ACT.Copy, scale=gain) \
                        .then_inc(S("qkt_out"), 1)

            def head_squares(ph, projected):
                act.wait_ge(S("proj_out"), projected)
                for n, (x, *_) in enumerate(head_calls(ph)):
                    c = hc0[ph] + n
                    if c >= 2:
                        act.wait_ge(S("heads_summed"), c - 1)
                    h, d = x.shape[1], x.shape[2]
                    A(sqb[:, c % 2, 0:h * d].rearrange("p (h d) -> p h d", h=h), x, ACT.Square).then_inc(S("heads_sq"), 1)

            def attention(ph):
                a, b = span(ph)
                for i in range(a, b + 2):
                    if i < b:
                        act.wait_ge(S("masked"), i + 1)
                        for j, (c, n, _) in enumerate(softmax_of(UNITS[i])):
                            last = A(Eb[:, i % 3, c:c + n], Eb[:, i % 3, c:c + n], ACT.Exp, bias=mx[:, i % NST, j:j + 1],
                                     scale=-1.0, accum_out=sm[:, i % NST, j:j + 1])
                        last.then_inc(S("exped"), 1)
                    if i - 2 >= a:
                        m = i - 2
                        n = P * blocks_of(UNITS[m])
                        act.wait_ge(S("pt"), m + 1)
                        if m >= 2:
                            act.wait_ge(S("weighed"), m - 1)
                        A(PTb[:, m % 2, 0:n], pt_bank(m)[:, 0:n], ACT.Copy).then_inc(S("pt_out"), 1)

            def mlp(l):
                for n in range(32):
                    m = 32 * l + n
                    act.wait_ge(S("hid"), m + 1)
                    if m >= 2:
                        act.wait_ge(S("hid_out"), m - 1)
                    A(tmp[:, m % 2, 0:SEQ], ps[:, 4 + m % 2, 0:SEQ], ACT.Relu).then_inc(S("hid_read"), 1)
                    act.wait_ge(S("hid_read"), m + 1)
                    if n >= 8 and n % 4 == 0:
                        act.wait_ge(S("w2_used"), 7 * l + n // 4 - 1)
                    A(HT[:, (n // 4) % 2, n % 4, :], tmp[:, m % 2, 0:SEQ], ACT.Square).then_inc(S("hid_out"), 1)

            square_sums(0, X)
            norm_out(0, hT)
            ein = lambda j, name, tt, c, w, p: [(Ue[:, tt, name[1] * W:name[1] * W + w], p)]
            proj_out("ein", ein, (0, 1))
            act.wait_ge(S("proj_out"), 4)
            for tt in range(TT):
                A(xs[:, 0, 0:QR], Ue[:, tt, 0:QR], ACT.Square, accum_out=ss[:, 8 + tt:9 + tt]).then_inc(S("lat_sq"), 1)
                A(xs[:, 1, 0:KVR], Ue[:, tt, QR:QR + KVR], ACT.Square, accum_out=ss[:, 10 + tt:11 + tt]).then_inc(S("lat_sq"), 1)
                act.wait_ge(S("lat_sq"), 2 * tt + 2)
            proj_out("ein", ein, (2,))
            head_squares("dilq", 6)
            proj_out("ein", ein, (3, 4))
            head_squares("dilk", 10)
            proj_out("ein", ein, (5,))
            for k in range(5):
                act.wait_ge(S("lat_tr"), min((k | 1) + 1, 5))
                gain = col("qlat")[:, k:k + 1] if k < 3 else col("kvlat")[:, k - 3:k - 2]
                A(cT[:, k, :], ps[:, 4 + (k // 2) % 2, 256 * (k % 2):256 * (k % 2) + 256], ACT.Copy, scale=gain) \
                    .then_inc(S("lat_out"), 1)

            def lat_place(j, name, tt, c, w, p):
                if name[0] == "uq":
                    return [(AUX[:, 768 * tt + c:768 * tt + c + w], p)]
                h0 = c // P
                v = p.rearrange("p (h d) -> p h d", d=P)
                return [(Km[:, tt, h0:h0 + 4, 0:NOPE], v[:, :, 0:NOPE]), (Vm[:, tt, h0:h0 + 4, :], v[:, :, NOPE:])]

            proj_out("lat", lat_place)
            act.wait_ge(S("krope"), 2)
            head_squares("mla", g0["oin"])
            qkt_out("dil")
            attention("dil")
            qkt_out("mla")
            attention("mla")
            qkt_out("otE")
            act.wait_ge(S("res_out"), 4)
            square_sums(1, X)
            norm_out(1, hT)
            mlp(0)
            act.wait_ge(S("res_out"), 8)
            square_sums(2, X)
            norm_out(2, hT)
            oin = lambda j, name, tt, c, w, p: [(Uo[:, tt, name[1] * W:name[1] * W + w], p)]
            for c in range(6):
                proj_out("oin", oin, (c,))
                if c in (0, 1, 3, 4):
                    head_squares(f"odd{c}", g0["oin"] + 2 * c + 2)
                if c == 4:
                    qkt_out("odd", 0, 8)
            attention("diff")
            qkt_out("odd", 8, 16)
            attention("moba")
            qkt_out("otO")
            act.wait_ge(S("res_out"), 12)
            square_sums(3, X)
            norm_out(3, hT)
            mlp(1)
            act.wait_ge(S("res_out"), 16)
            square_sums(4, X)
            norm_out(4, hT)
            act.wait_ge(S("ctx_in"), 16)
            square_sums(5, ctx_x)
            norm_out(5, hc)

            def in2_place(j, name, tt, c, w, p):
                i = name[1]
                seen = [g for g in groups("in2")[:j] if g[0] == name]
                if len(seen) >= 2:
                    return [(Uc[:, tt, CTX_AT[i]:CTX_AT[i] + w], p)]
                dst = U2[:, tt, IN2[i][0]:IN2[i][0] + w]
                if i == 0:
                    return [(dst.rearrange("p (j g d) -> p g j d", g=2, d=HD), p.rearrange("p (g j d) -> p g j d", g=2, d=HD))]
                return [(dst, p, HD ** -0.5) if i == 2 else (dst, p)]

            proj_out("in2", in2_place, (0,))
            head_squares("gq", g0["in2"] + 2)
            proj_out("in2", in2_place, (1,))
            head_squares("gk", g0["in2"] + 6)
            proj_out("in2", in2_place, (2, 3))
            qkt_out("b2", 0, 6)
            proj_out("in2", in2_place, (4, 5))
            qkt_out("b2", 6, None)
            for f in range(4):
                act.wait_ge(S("glu"), f + 1)
                if f >= 2:
                    act.wait_ge(S("glu_out"), f - 1)
                A(tmp[:, f % 2, 0:SEQ], ps[:, 4 + f % 2, SEQ:2 * SEQ], ACT.Sigmoid).then_inc(S("glu_sig"), 1)
            attention("gqa")
            attention("na")
            for g in range(4):
                act.wait_ge(S("dft1"), g + 1)
                A(Z12[:, g, :], ps[:, g, :], ACT.Copy).then_inc(S("dft1_out"), 1)
            for g in range(4):
                act.wait_ge(S("dft2"), (g | 1) + 1)
                A(YF[:, g, :], ps[:, 4 + g // 2, SEQ * (g % 2):SEQ * (g % 2) + SEQ], ACT.Copy).then_inc(S("dft2_out"), 1)
            act.wait_ge(S("conv_tap"), TAPS)
            A(convs[:, :, :], convy[:, :, :], ACT.Square).then_inc(S("conv_sq"), 1)
            qkt_out("otB")
            act.wait_ge(S("conv_scaled"), 1)
            for k in range(4):
                A(YC[:, k, :], convs[:, k, :], ACT.Silu, scale=col("convg")[:, k:k + 1]).then_inc(S("conv_out"), 1)
            for n in range(32):
                act.wait_ge(S("merge"), n + 1)
                if n >= 2:
                    act.wait_ge(S("merge_out"), n - 1)
                A(tmp[:, n % 2, 0:SEQ], ps[:, 4 + n % 2, 0:SEQ], ACT.Sigmoid).then_inc(S("merge_act"), 1)
            act.wait_ge(S("res_out"), 20)
            square_sums(6, X)
            norm_out(6, hT)
            act.wait_ge(S("logits"), 1)
            A(moe[:, 0:32], ps[:, 6, 0:32], ACT.Sigmoid).then_inc(S("router_sig"), 1)
            with act.Fori(0, NEXP // 4) as it:
                e = it * 4
                for j in range(16):
                    act.wait_ge(S("merge"), 32 + j + 1 + e * 4)
                    act.wait_ge(S("merge_out"), 32 + j - 1 + e * 4)
                    A(tmp[:, j % 2, 0:SEQ], ps[:, 4 + j % 2, 0:SEQ], ACT.Silu).then_inc(S("merge_act"), 1)
            act.wait_ge(S("final_x"), 1)
            square_sums(7, X)

        @block.gpsimd
        def _(pool):
            pool.memset(ones[:, :], 1.0).then_inc(S("ones_set"), 1)
            pool.memset(zero[:, :], 0.0).then_inc(S("ones_set"), 1)
            pool.wait_ge(S("consts_in"), 16 * NSMALL)

            def gate_bias(l):
                for i, v in enumerate((2, 5)):
                    b = (t["ada_b"][l] if l < 2 else t["b_mod_2"][0])[v * D:(v + 1) * D]
                    pool.dma_start(G[:, 2 * (l % 2) + i, :], b.partition_broadcast(P)) \
                        .then_inc(S(f"gate_bias{l}"), 16)

            links = [0]

            def link(ins):
                links[0] += 1
                ins.then_inc(S("pool_chain"), 1)
                pool.wait_ge(S("pool_chain"), links[0])

            def rotate(ph):
                for n, (x, _, _, cos, sin, r0, pairs) in enumerate(head_calls(ph)):
                    pool.wait_ge(S("heads_scaled"), hc0[ph] + n + 1)
                    h = x.shape[1]
                    if cos is None:
                        pool.sem_inc(S("roped"), 1)
                        continue
                    hw = cos.shape[-1]
                    if pairs:
                        v = x.rearrange("p h (m two) -> p h m two", two=2)
                        x1, x2 = v[:, :, :, 0], v[:, :, :, 1]
                    else:
                        x1, x2 = x[:, :, r0:r0 + hw], x[:, :, r0 + hw:r0 + 2 * hw]
                    cb, sb_ = spread(cos, 1, h), spread(sin, 1, h)
                    flat = tmp.rearrange("p s n -> p (s n)")
                    a, b = (flat[:, 512 * i:512 * i + h * hw].rearrange("p (h d) -> p h d", h=h) for i in range(2))
                    tt_ = lambda o, i0, i1, op: pool.tensor_tensor(out=o, in0=i0, in1=i1, op=op)
                    tt_(a, x1, sb_, ALU.mult)
                    link(tt_(b, x2, sb_, ALU.mult))
                    tt_(x1, x1, cb, ALU.mult)
                    link(tt_(x2, x2, cb, ALU.mult))
                    link(tt_(x1, x1, b, ALU.subtract))
                    tt_(x2, x2, a, ALU.add).then_inc(S("roped"), 1)
                    pool.wait_ge(S("roped"), hc0[ph] + n + 1)

            def na_bias(h):
                if h >= 2:
                    pool.wait_ge(S("masked"), span("na")[0] + 2 * (h - 1))
                pool.dma_start(nab[:, h % 2, :, 0:256], t["na_bias"][h].rearrange("(t p) n -> p t n", p=P)) \
                    .then_inc(S("nab_in"), 16)

            def na_mask(h):
                pool.wait_ge(S("nab_in"), 16 * (h + 1))
                pool.tensor_tensor(out=nab[:, h % 2, :, 0:256], in0=nab[:, h % 2, :, 0:256],
                                   in1=con("na").rearrange("p (t n) -> p t n", t=2), op=ALU.add).then_inc(S("nab"), 1)

            gate_bias(0)
            gate_bias(1)
            pool.wait_ge(S("sines"), 1)
            for ph in ("dilq", "dilk", "mla", "odd0", "odd1", "odd3", "odd4"):
                rotate(ph)
            pool.wait_ge(S("res_out"), 8)
            gate_bias(2)
            pool.wait_ge(S("weighed"), span("moba")[1])
            pool.dma_start(ctx_x, t["ctx_2"][0].rearrange("(t p) n -> p t n", p=P)).then_inc(S("ctx_in"), 16)
            rotate("gq")
            rotate("gk")
            pool.wait_ge(S("glu_out"), 4)
            pool.memset(nab[:, :, :, 256:512], 0.0).then_inc(S("nab_zero"), 1)
            pool.wait_ge(S("nab_zero"), 1)
            pool.dma_start(consts[:, dft_at:dft_at + NDFT], t["dft"]).then_inc(S("dft_in"), 16)
            for h in range(8):
                na_bias(h)
                na_mask(h)
            pool.wait_ge(S("res_out"), 16)
            pool.dma_start(G[:, 2, :], t["final_norm_g_2"].partition_broadcast(P)) \
                .then_inc(S("final_gain"), 16)

        @block.vector
        def _(dve):
            V = nc.vector
            chain = [0]

            def link(ins):
                chain[0] += 1
                ins.then_inc(S("dve_chain"), 1)
                dve.wait_ge(S("dve_chain"), chain[0])

            def ts(o, i, a, b=None, p=ALU.mult, q=ALU.add):
                if b is None:
                    return V.tensor_scalar(o, i, a, None, p)
                return V.tensor_scalar(o, i, a, b, p, q)

            def tt_(o, a, b, op=ALU.mult):
                return V.tensor_tensor(o, a, b, op)

            def stt(o, a, s, b, p=ALU.mult, q=ALU.add):
                return V.scalar_tensor_tensor(out=o, in0=a, scalar=s, in1=b, op0=p, op1=q)

            def rstd(y, x, inv_n, scale=None):
                n = x.shape[-1]
                v, xh = (wn[:, i, 0:n] for i in range(2))
                link(ts(v, x, inv_n, EPS))
                ts(xh, v, -0.5)
                link(ts(y.bitcast(I32), v.bitcast(I32), -0.5, 1597463007.0))
                for _ in range(3):
                    link(tt_(v, y, y))
                    link(tt_(v, v, xh))
                    link(stt(y, v, 1.5, y, ALU.add, ALU.mult))
                if scale is not None:
                    link(ts(y, y, scale))

            def norm_heads(ph):
                for n, (x, gain, scale, *_) in enumerate(head_calls(ph)):
                    c = hc0[ph] + n
                    h, d = x.shape[1], x.shape[2]
                    dve.wait_ge(S("heads_sq"), c + 1)
                    V.reduce_sum(ss[:, 16:16 + h], sqb[:, c % 2, 0:h * d].rearrange("p (h d) -> p h d", h=h), axis=AX) \
                        .then_inc(S("heads_summed"), 1)
                    dve.wait_ge(S("heads_summed"), c + 1)
                    rstd(wn[:, 2, 0:h], ss[:, 16:16 + h], 1.0 / d, scale)
                    link(tt_(x, x, spread(wn[:, 2, 0:h], 2, d)))
                    tt_(x, x, spread(gain, 1, h)).then_inc(S("heads_scaled"), 1)

            def mod_acc(q):
                l, j = MODSEQ[q]
                name = ("mod", min(l, 2), j)
                w = arrived(dve, name)
                a = acc[:, q % 2, :]
                c0 = 8 * min(l, 3) if l > 1 else 0
                c0 = {0: 0, 1: 0, 2: 8, 3: 16}[l]
                link(ts(a, w[:, 0, :], cond[:, c0:c0 + 1]))
                for k in range(1, KT):
                    ins = stt(a, w[:, k, :], cond[:, c0 + k:c0 + k + 1], a)
                    if k < KT - 1:
                        link(ins)
                ins.then_inc(S("mod_acc"), 1)

            def mod_fin(q):
                l, j = MODSEQ[q]
                v, hf = j // 2, j % 2
                dve.wait_ge(S("mod_sum"), q + 1)
                p = ps[:, 6, :]
                if v in (2, 5):
                    dve.wait_ge(S(f"gate_bias{l}"), 32)
                    g = G[:, 2 * (l % 2) + v // 3, hf * W:(hf + 1) * W]
                    tt_(g, g, p, ALU.add).then_inc(S("mod_fin"), 1)
                    dve.wait_ge(S("mod_fin"), q + 1)
                    return
                w4 = mtmp.rearrange("p (c n) -> p c n", c=4)
                link(tt_(w4, p.rearrange("p (c n) -> p c n", c=4), spread(ident, 1, 4)))
                m = modc[:, l, v, 4 * hf:4 * hf + 4]
                link(V.reduce_sum(m, w4, axis=AX))
                bias = col("adab")[:, 48 * min(l, 2) + 8 * v + 4 * hf:48 * min(l, 2) + 8 * v + 4 * hf + 4]
                tt_(m, m, bias, ALU.add).then_inc(S("mod_fin"), 1)
                dve.wait_ge(S("mod_fin"), q + 1)

            def norm(i, src):
                l, v = ((0, 1), (0, 4), (1, 1), (1, 4), (2, 1), (3, 1), (2, 4))[i]
                gain = (col("nmix")[:, 0:8], col("nmlp")[:, 0:8], col("nmix")[:, 8:16], col("nmlp")[:, 8:16],
                        col("n1"), col("n1"), col("n2"))[i]
                stt(coef[:, i, :], modc[:, l, v, :], 1.0, gain, ALU.add, ALU.mult).then_inc(S("coef"), 1)
                dve.wait_ge(S("norm_sq"), 2 * i + 2)
                r = ss[:, 4:6]
                rstd(r, ss[:, 2 * (i % 2):2 * (i % 2) + 2], 1.0 / D)
                for tt in range(TT):
                    ts(xs[:, tt, :], src[:, tt, :], r[:, tt:tt + 1]).then_inc(S("norm_scaled"), 1)

            def residual(r, s):
                for n in range(2):
                    for tt in range(TT):
                        m = 2 * n + tt
                        dve.wait_ge(S("res"), 4 * r + m + 1)
                        link(tt_(xs[:, tt, n * W:(n + 1) * W], ps[:, m, :], G[:, s, n * W:(n + 1) * W]))
                        x = X[:, tt, n * W:(n + 1) * W]
                        tt_(x, x, xs[:, tt, n * W:(n + 1) * W], ALU.add).then_inc(S("res_out"), 1)
                dve.wait_ge(S("res_out"), 4 * r + 4)

            def attention(ph, between=None):
                a, b = span(ph)
                for i in range(a, b + 4):
                    if i < b:
                        dve.wait_ge(S("scored"), i + 1)
                        if i >= 3:
                            dve.wait_ge(S("pt"), i - 2)
                        if ph == "na" and i % 2 == 0:
                            dve.wait_ge(S("nab"), (i - a) // 2 + 1)
                        for j, (c, n, mask) in enumerate(softmax_of(UNITS[i])):
                            pc = j * W
                            last = V.tensor_tensor_reduce(out=Eb[:, i % 3, c:c + n], in0=s_bank(i)[:, pc:pc + n], in1=mask[:, 0:n],
                                                          scale=-1.0, scalar=3e38, op0=ALU.add, op1=ALU.min,
                                                          accum_out=mx[:, i % NST, j:j + 1])
                        last.then_inc(S("masked"), 1)
                    if a <= i - 4:
                        m = i - 4
                        dve.wait_ge(S("weighed"), m + 1)
                        o = ps[:, 6 + m % 2, :]
                        n = 2 if ph == "diff" else 1
                        link(V.reciprocal(rc[:, m % NST, 0:n], sm[:, m % NST, 0:n]))
                        if ph == "diff":
                            t2 = wn[:, 2, 0:P]
                            link(stt(t2, o[:, P:2 * P], rc[:, m % NST, 1:2], spread(lam[:, 5], 1, P), ALU.mult, ALU.mult))
                            stt(output_of(UNITS[m]), o[:, 0:P], rc[:, m % NST, 0:1], t2).then_inc(S("o_out"), 1)
                        else:
                            ts(output_of(UNITS[m]), o[:, 0:HD], rc[:, m % NST, 0:1]).then_inc(S("o_out"), 1)
                    if between:
                        between(i)

            def sub_norm():
                dve.wait_ge(S("o_out"), span("diff")[1])
                sq = hTb[:, 0:1024].rearrange("p (t h d) -> p t h d", t=2, h=4)
                o = OkO[:, :, 0:512].rearrange("p t (h d) -> p t h d", h=4)
                for tt in range(TT):
                    last = tt_(sq[:, tt], o[:, tt], o[:, tt])
                link(last)
                link(V.reduce_sum(ss[:, 16:24], hTb[:, 0:1024].rearrange("p (g d) -> p g d", d=P), axis=AX))
                rstd(wn[:, 2, 0:8], ss[:, 16:24], 1.0 / P, 1.0 - LAM_INIT)
                for tt in range(TT):
                    last = tt_(o[:, tt], o[:, tt], spread(wn[:, 2, 4 * tt:4 * tt + 4], 2, P))
                last.then_inc(S("sub_done"), 1)

            cw = col("convw").rearrange("p (c j) -> p c j", c=4)
            TAP_ORDER = [TAPS // 2] + [j for j in range(TAPS) if j != TAPS // 2]

            def conv_tap(n):
                if n >= TAPS:
                    return
                j = TAP_ORDER[n]
                if n:
                    dve.wait_ge(S("conv_tap"), n)
                lo, hi = max(0, TAPS // 2 - j), min(SEQ, SEQ + TAPS // 2 - j)
                for k in range(4):
                    z = Z[:, k, lo + j - TAPS // 2:hi + j - TAPS // 2]
                    if n == 0:
                        last = ts(convy[:, k, :], z, cw[:, k, j:j + 1], col("convb")[:, k:k + 1])
                    else:
                        last = stt(convy[:, k, lo:hi], z, cw[:, k, j:j + 1], convy[:, k, lo:hi])
                last.then_inc(S("conv_tap"), 1)

            mtmp = wn[:, 0:2, :].rearrange("p s n -> p (s n)")
            dve.wait_ge(S("consts_in"), 16 * NSMALL)
            dve.wait_ge(S("ones_set"), 2)
            link(V.tensor_copy(posf[:, :], posi[:, :]))
            an, kk, tm = rw[:, 0, :], rw[:, 1, :], rw[:, 2, :]
            for tt in range(TT):
                last = ts(an[:, 48 * tt:48 * tt + 48], con("invf"), posf[:, tt:tt + 1])
            link(last)
            link(ts(kk, an, 1.0 / TWO_PI, 12582912.0))
            link(ts(kk, kk, 12582912.0, None, ALU.subtract))
            c1 = 6.28125
            c2 = float(np.float32(np.round((TWO_PI - c1) * 2 ** 20) / 2 ** 20))
            c3 = TWO_PI - c1 - c2
            for c in (c1, c2, c3):
                link(stt(an, kk, -c, an))
            sn, cs = rope[:, 96:192], rope[:, 0:96]
            link(ts(sn, an, PI_LO, -PI_LO, ALU.min, ALU.max))
            link(ts(tm, sn, -1.0))
            link(tt_(tm, tm, sn, ALU.max))
            ts(cs, tm, -1.0, float(np.pi / 2)).then_inc(S("angles"), 1)
            lv = row("lam").rearrange("p (i d) -> p i d", i=4)
            for i in range(2):
                link(V.tensor_tensor_reduce(out=rw[:, 3, 0:64], in0=lv[:, 2 * i, :], in1=lv[:, 2 * i + 1, :], scale=1.0,
                                            scalar=0.0, op0=ALU.mult, op1=ALU.add, accum_out=lam[:, i:i + 1]))
            V.engine_nop().then_inc(S("angles"), 1)
            dve.wait_ge(S("cond"), 1)
            for q in range(4):
                mod_acc(q)
                if q:
                    mod_fin(q - 1)
            mod_fin(3)
            norm(0, X)
            dve.wait_ge(S("lam_exp"), 1)
            link(tt_(lam[:, 4:5], lam[:, 3:4], lam[:, 2:3], ALU.subtract))
            link(ts(lam[:, 5:6], lam[:, 4:5], LAM_INIT, None, ALU.subtract))
            for q in (4, 5):
                mod_acc(q)
                if q > 4:
                    mod_fin(q - 1)
            dve.wait_ge(S("lat_sq"), 4)
            rstd(ss[:, 12:14], ss[:, 8:10], 1.0 / QR)
            rstd(ss[:, 14:16], ss[:, 10:12], 1.0 / KVR)
            for tt in range(TT):
                ts(Ue[:, tt, 0:QR], Ue[:, tt, 0:QR], ss[:, 12 + tt:13 + tt])
                last = ts(Ue[:, tt, QR:QR + KVR], Ue[:, tt, QR:QR + KVR], ss[:, 14 + tt:15 + tt])
            last.then_inc(S("lat_scaled"), 1)
            for tt in range(TT):
                V.tensor_copy(Km[:, tt, :, NOPE:QKD], spread(Ue[:, tt, QR + KVR:QR + KVR + ROPE], 1, MH)) \
                    .then_inc(S("krope"), 1)
            mod_acc(6)
            mod_fin(5)
            norm_heads("dilq")
            for q in (7, 8):
                mod_acc(q)
                mod_fin(q - 1)
            norm_heads("dilk")
            for q in (9, 10, 11):
                mod_acc(q)
                mod_fin(q - 1)
            mod_fin(11)
            norm_heads("mla")
            attention("dil")
            attention("mla")
            residual(0, 0)
            norm(1, X)
            for q in range(12, 24):
                mod_acc(q)
                if q > 12:
                    mod_fin(q - 1)
            mod_fin(23)
            residual(1, 1)
            norm(2, X)
            for c in (0, 1, 3, 4):
                norm_heads(f"odd{c}")
            attention("diff")
            attention("moba", between=lambda i: sub_norm() if i == span("moba")[0] + 4 else None)
            residual(2, 2)
            norm(3, X)
            for q in range(24, 40):
                mod_acc(q)
                if q > 24:
                    mod_fin(q - 1)
            mod_fin(39)
            residual(3, 3)
            norm(4, X)
            dve.wait_ge(S("ctx_in"), 16)
            dve.wait_ge(S("norm_tr"), 5 * KT)
            norm(5, ctx_x)
            norm_heads("gq")
            norm_heads("gk")
            for f in range(4):
                dve.wait_ge(S("glu_sig"), f + 1)
                tt_(Z[:, f, :], tmp[:, f % 2, 0:SEQ], ps[:, 4 + f % 2, 0:SEQ]).then_inc(S("glu_out"), 1)
            dve.wait_ge(S("glu_out"), 4)
            attention("gqa", between=lambda i: conv_tap(i - span("gqa")[0]) if i < span("gqa")[1] else None)
            attention("na", between=lambda i: conv_tap(i - span("gqa")[0]) if i < span("na")[1] else None)
            dve.wait_ge(S("conv_sum"), 1)
            rstd(wn[:, 2, 0:256], ps[:, 6, 0:SEQ], 1.0 / 512)
            tt_(convs[:, :, :], convy[:, :, :], spread(wn[:, 2, :], 1, 4)).then_inc(S("conv_scaled"), 1)
            for n in range(32):
                dve.wait_ge(S("merge_act"), n + 1)
                f = n % 8
                z = ps[:, 4 + n % 2, SEQ:2 * SEQ]
                g = tmp[:, n % 2, 0:SEQ]
                if n < 8:
                    tt_(M2[:, f, :], g, z).then_inc(S("merge_out"), 1)
                else:
                    tt_(xs[:, 0, 256 * (n % 2):256 * (n % 2) + 256], g, z).then_inc(S("merge_out"), 1)
                    dve.wait_ge(S("merge_out"), n + 1)
                    link(tt_(M2[:, f, :], M2[:, f, :], xs[:, 0, 256 * (n % 2):256 * (n % 2) + 256], ALU.add))
            V.engine_nop().then_inc(S("merged"), 1)
            residual(4, 0)
            norm(6, X)
            dve.wait_ge(S("router_sig"), 1)
            sc = moe[:, 0:32]
            sel = moe[:, 32:64]
            link(tt_(sel.rearrange("p (t e) -> p t e", t=2), sc.rearrange("p (t e) -> p t e", t=2),
                     spread(row("rbias"), 1, 2), ALU.add))
            s4 = sel.rearrange("p (g e) -> p g e", e=4)
            pr = moe[:, 64:112].rearrange("p (g i) -> p g i", i=6)
            for i, (a, b) in enumerate(((0, 1), (0, 2), (0, 3), (1, 2), (1, 3), (2, 3))):
                last = tt_(pr[:, :, i:i + 1], s4[:, :, a:a + 1], s4[:, :, b:b + 1], ALU.add)
            link(last)
            gs = moe[:, 112:120]
            link(V.reduce_max(gs, pr, axis=AX))
            tri = con("tri").rearrange("p (a b) -> p a b", a=4)

            def ranks(dst, v, n, w1, w2):
                for g in range(n):
                    a = spread(v[:, g, :], 1, 4)
                    b = spread(v[:, g, :], 2, 4)
                    tt_(w1[:, g], a, b, ALU.is_gt)
                    last = tt_(w2[:, g], a, b, ALU.is_equal)
                link(last)
                link(tt_(w2, w2, spread(tri, 1, n)))
                link(tt_(w1, w1, w2, ALU.add))
                link(V.reduce_sum(dst, w1, axis=AX))

            rk = moe[:, 120:152]
            ranks(rk.rearrange("p (g e) -> p g e", e=4), s4, 8, moe[:, 152:280].rearrange("p (g a b) -> p g a b", g=8, a=4),
                  moe[:, 280:408].rearrange("p (g a b) -> p g a b", g=8, a=4))
            gk = moe[:, 408:416]
            ranks(gk.rearrange("p (g e) -> p g e", e=4), gs.rearrange("p (g e) -> p g e", e=4), 2,
                  moe[:, 416:448].rearrange("p (g a b) -> p g a b", g=2, a=4),
                  moe[:, 448:480].rearrange("p (g a b) -> p g a b", g=2, a=4))
            link(ts(rk, rk, 2.0, None, ALU.is_lt))
            link(ts(gk, gk, 1.0, None, ALU.is_lt))
            gt = moe[:, 480:512]
            link(tt_(gt, sc, rk))
            g8 = gt.rearrange("p (g e) -> p g e", e=4)
            link(tt_(g8, g8, spread(gk, 2, 4)))
            link(V.reduce_sum(moe[:, 512:514], gt.rearrange("p (t e) -> p t e", t=2), axis=AX))
            link(V.reciprocal(moe[:, 514:516], moe[:, 512:514]))
            link(tt_(gt.rearrange("p (t e) -> p t e", t=2), gt.rearrange("p (t e) -> p t e", t=2),
                     spread(moe[:, 514:516], 2, 16)))
            link(V.memset(accY[:, :, :], 0.0))
            with dve.Fori(0, NEXP // 4) as it:
                e = it * 4
                for j in range(4):
                    for f in range(4):
                        dve.wait_ge(S("merge_act"), 32 + 4 * j + f + 1 + e * 4)
                        if f == 0:
                            dve.wait_ge(S("res"), 20 + 4 * j - 4 + e * 4)
                        tt_(HT[:, j % 2, f, :], tmp[:, f % 2, 0:SEQ], ps[:, 4 + f % 2, SEQ:2 * SEQ]) \
                            .then_inc(S("merge_out"), 1)
                    for n in range(2):
                        for tt in range(TT):
                            m = 2 * n + tt
                            dve.wait_ge(S("res"), 20 + 4 * j + m + 1 + e * 4)
                            if m == 0:
                                dve.wait_ge(S("res_out"), 20 + 4 * j + e * 4)
                            y = accY[:, tt, n * W:(n + 1) * W]
                            stt(y, ps[:, m, :], gt[:, bass.ds(16 * tt + e + j, 1)], y).then_inc(S("res_out"), 1)
            dve.wait_ge(S("res_out"), 20 + 4 * NEXP)
            for tt in range(TT):
                link(tt_(accY[:, tt, :], accY[:, tt, :], G[:, 1, :]))
                last = tt_(X[:, tt, :], X[:, tt, :], accY[:, tt, :], ALU.add)
            last.then_inc(S("final_x"), 1)
            dve.wait_ge(S("norm_sq"), 16)
            rstd(ss[:, 4:6], ss[:, 2:4], 1.0 / D)
            dve.wait_ge(S("final_gain"), 16)
            for tt in range(TT):
                stt(xs[:, tt, :], X[:, tt, :], ss[:, 4 + tt:5 + tt], G[:, 2, :], ALU.mult, ALU.mult).then_inc(S("final_done"), 1)


def kernel(**inputs):
    import concourse.bacc as _bacc
    from concourse.bass_utils import run_bass_kernel_spmd as _run

    a = {n: np.asarray(v) for n, v in inputs.items()}
    nc = _bacc.Bacc("TRN2", target_bir_lowering=False, num_devices=1)

    def col(v):
        return v.reshape(-1, P).T

    whole = ("x", "ctx_2", "ada_w", "ada_b", "mlp_w1", "mlp_w2", "even_w_in", "even_w_out", "mla_w_uq", "mla_w_ukv",
             "odd_w_in", "odd_w_out", "w_mod_2", "b_mod_2", "w_in_2", "w_branch_2", "w_out_2", "w_router_2",
             "w_expert_gu_2", "w_expert_down_2", "final_norm_g_2")
    arr = {n: np.ascontiguousarray(a[n]) for n in whole}
    arr["positions"] = np.ascontiguousarray(a["positions"].reshape(TT, P).T)
    arr["cols"] = np.ascontiguousarray(np.concatenate(
        [col(a["c"]), col(a["c_2"]), col(a["c_ctx_2"]), col(a["ada_b"]), col(a["b_mod_2"]), col(a["norm_mix"]),
         col(a["norm_mlp"]), col(a["norm1_g_2"]), col(a["norm2_g_2"]), col(a["mla_q_lat_norm"]), col(a["mla_kv_lat_norm"]),
         col(a["diff_subln"]), a["conv_w_2"][0].reshape(TAPS, 4, P).transpose(2, 1, 0).reshape(P, -1), col(a["conv_b_2"]),
         col(a["conv_norm_g_2"])], 1))
    arr["rows"] = np.ascontiguousarray(np.concatenate(
        [a[n].reshape(-1) for n in ("mla_q_norm", "mla_k_norm", "dil_q_norm", "dil_k_norm", "diff_q_norm", "diff_k_norm",
                                    "moba_q_norm", "moba_k_norm", "q_norm_g_2", "k_norm_g_2", "diff_lambda",
                                    "router_bias_2")]))
    rpb = np.ascontiguousarray(a["na_rpb_2"][0])
    i = rpb.itemsize
    flat = np.lib.stride_tricks.as_strided(rpb.reshape(-1)[7 * 31 + 15:], shape=(8, 4, 64, 4, 64),
                                           strides=(15 * 31 * i, -31 * i, -i, 31 * i, i))
    arr["na_bias"] = np.ascontiguousarray(flat).reshape(8, SEQ, SEQ)
    arr["consts"], arr["dft"] = shape_constants()
    aps = {n: nc.dram_tensor("in_" + n, v.shape, mybir.dt.from_np(v.dtype), kind="ExternalInput").ap() for n, v in arr.items()}
    out = nc.dram_tensor("out_0", (1, SEQ, D), F32, kind="ExternalOutput").ap()
    program(nc, aps, out)
    r = _run(nc, [{"in_" + n: v for n, v in arr.items()}], core_ids=[0])
    return r.results[0]["out_0"]
```

```python
from contextlib import ExitStack

import numpy as np

import concourse.bass as bass
from concourse import mybir

F32 = mybir.dt.float32
I32 = mybir.dt.int32
R32 = mybir.dt.float32r
ALU = mybir.AluOpType
ACT = mybir.ActivationFunctionType
AX = mybir.AxisListType.X

P = 128
D = 1024
SEQ = 256
KT = D // P
TT = SEQ // P
W = 512
FF = 4 * D
HD = 64
EPS = 1e-6
NEG = -1e30
QR, KVR, NOPE, ROPE, MH = 384, 256, 64, 32, 8
QKD = NOPE + ROPE
DIL = ((128, 1), (512, 4), (2048, 16))
DG, DH = 3, 4
E_IN = QR + KVR + ROPE + 3 * DG * DH * HD
E_OUT = MH * HD + DH * HD
O_IN = 6 * 512
NEXP, EFF = 16, 512
GATE0 = 3840
TAPS = 31
PADT = SEQ + TAPS - 1
LAM_INIT = 0.8 - 0.6 * float(np.exp(-0.3))
RING = 4
SLOT = KT * W
NST = 8
TWO_PI = 2.0 * float(np.pi)
PI_LO = 3.1415925

CONSTS = (("ident", 128), ("c0", 128), ("c1", 256), ("d0", 384), ("d1", 768), ("na", 512), ("ax", 128),
          ("invf", 48), ("tri", 16))
DFT = (("CL", 512), ("SL", 512), ("CD", 128), ("SD", 128))
COLS = (("c", 24), ("adab", 144), ("nmix", 16), ("nmlp", 16), ("n1", 8), ("n2", 8), ("qlat", 3), ("kvlat", 2),
        ("subln", 1), ("convw", 124), ("convb", 4), ("convg", 4))
ROWS = (("mlaq", 96), ("mlak", 96), ("dilq", 64), ("dilk", 64), ("diffq", 64), ("diffk", 64), ("mobaq", 64),
        ("mobak", 64), ("gqaq", 64), ("gqak", 64), ("lam", 256), ("rbias", 16))


def offsets(parts):
    at, out = 0, {}
    for name, n in parts:
        out[name] = (at, at + n)
        at += n
    return out, at


def shape_constants():
    out = {"ident": np.eye(P)}
    q, k = np.arange(SEQ)[:, None], np.arange(SEQ)[None, :]
    neg = lambda keep: np.where(keep, 0.0, NEG)
    causal = neg(q >= k)
    out["c0"], out["c1"] = causal[:P, :P], causal[P:]
    dil = [neg((q >= k) & ((q - k) % r == 0) & (q - k <= w)) for w, r in DIL]
    out["d0"] = np.concatenate([m[:P, :P] for m in dil], 1)
    out["d1"] = np.concatenate([m[P:] for m in dil], 1)
    qc, kc = q % 64, k % 64
    start = np.clip(qc - 8, 0, 48)
    na = neg((kc >= start) & (kc < start + 16))
    out["na"] = np.concatenate([na[:P], na[P:]], 1)
    t = np.arange(SEQ)
    f = np.float32(10000.0) ** (-np.arange(16, dtype=np.float32) / np.float32(16))
    f32_ = np.float32(10000.0) ** (-np.arange(32, dtype=np.float32) / np.float32(32))
    ang = np.concatenate([(t // 64).astype(np.float32)[:, None] * f, (t % 64).astype(np.float32)[:, None] * f], 1)
    cs, sn = np.cos(ang.astype(np.float64)), np.sin(ang.astype(np.float64))
    out["ax"] = np.concatenate([cs[:P], cs[P:], sn[:P], sn[P:]], 1)
    out["invf"] = np.tile(np.concatenate([f, f32_])[None], (P, 1))
    out["tri"] = np.tile((np.arange(4)[None, :] < np.arange(4)[:, None]).astype(np.float32).reshape(1, 16), (P, 1))
    al = 2 * np.pi * ((q * k) % SEQ) / SEQ
    tiles = lambda m: m.reshape(TT, P, SEQ).transpose(1, 0, 2).reshape(P, -1)
    out["CL"], out["SL"] = tiles(np.cos(al)), tiles(np.sin(al))
    d = np.arange(P)
    ad = 2 * np.pi * ((d[:, None] * d[None, :]) % P) / P
    norm = 1.0 / np.sqrt(SEQ * P)
    out["CD"], out["SD"] = np.cos(ad) * norm, -np.sin(ad) * norm
    return [np.ascontiguousarray(np.concatenate([out[n] for n, _ in part], 1).astype(np.float32)) for part in (CONSTS, DFT)]


def weight_stream(t):
    S = []

    def add(name, src, k, n):
        S.append((name, src.rearrange("(k p) n -> p k n", p=P), k, n))

    def mod(l, j):
        w = t["ada_w"][l] if l < 2 else t["w_mod_2"][0]
        add(("mod", l, j), w[:, j * W:(j + 1) * W], KT, W)

    for j in range(4):
        mod(0, j)
    for i in range(6):
        n = min(W, E_IN - i * W)
        add(("ein", i), t["even_w_in"][0][:, i * W:i * W + n], KT, n)
        mod(0, 4 + i)
    mod(0, 10)
    mod(0, 11)
    add(("uq",), t["mla_w_uq"][0].rearrange("r h d -> r (h d)"), 3, 768)
    add(("ukv",), t["mla_w_ukv"][0].rearrange("r h d -> r (h d)"), 2, 1024)
    for j in MOD_IN_ATT["mla"][0][1]:
        mod(1, j)
    for n in range(2):
        add(("eout", n), t["even_w_out"][0][:, n * W:(n + 1) * W], 6, W)

    def mlp(l):
        for j in range(FF // W):
            add(("w1", l, j), t["mlp_w1"][l][:, j * W:(j + 1) * W], KT, W)
            add(("w2", l, j), t["mlp_w2"][l][j * W:(j + 1) * W, :], 4, D)
            for m in mod_in_mlp(l, j):
                mod(l + 1, m)

    mlp(0)
    for i in range(6):
        add(("oin", i), t["odd_w_in"][0][:, i * W:(i + 1) * W], KT, W)
    for j in MOD_IN_ATT["moba"][0][1]:
        mod(2, j)
    for n in range(2):
        add(("oout", n), t["odd_w_out"][0][:, n * W:(n + 1) * W], KT, W)
    mlp(1)
    for i, (a, n) in enumerate(IN2):
        add(("in2", i), t["w_in_2"][0][:, a:a + n], KT, n)
    for b in range(4):
        add(("gate", 2 * b), t["w_in_2"][0][:, GATE0 + 2 * b * W:GATE0 + (2 * b + 1) * W], KT, W)
        add(("branch", b), t["w_branch_2"][0, b], 4, D)
        add(("gate", 2 * b + 1), t["w_in_2"][0][:, GATE0 + (2 * b + 1) * W:GATE0 + (2 * b + 2) * W], KT, W)
    for n in range(2):
        add(("out2", n), t["w_out_2"][0][:, n * W:(n + 1) * W], KT, W)
    return S


def mod_in_mlp(l, j):
    if l == 0:
        return (4 + j,)
    return (2 + j,) if j < 6 else (2 * j - 4, 2 * j - 3)


MOD_IN_ATT = {"mla": ((1, (0, 1, 2, 3)), 12, 4), "moba": ((2, (0, 1)), 24, 4)}


IN2 = ((0, 512), (512, 256), (768, 512), (1280, 512), (1792, 512), (2304, 512), (2816, 512), (3328, 512))
CTX_AT = {1: 0, 3: 256, 4: 768}
MODSEQ = [(0, j) for j in range(12)] + [(1, j) for j in range(12)]
for _j in range(12):
    MODSEQ += [(2, _j)] + ([(3, _j)] if _j < 4 else [])


def spread(ap, dim, n):
    ap = ap.unsqueeze(dim)
    shape = list(ap.shape)
    shape[dim] = n
    return ap.broadcast_to(shape)


def units():
    out = []
    for ph, heads in (("dil", DH), ("mla", MH), ("diff", 4), ("moba", 8), ("gqa", 8), ("na", 8)):
        out += [(ph, h, t) for h in range(heads) for t in range(TT)]
    return out


def program(nc, t, out):
    stream = weight_stream(t)
    number = {s[0]: n for n, s in enumerate(stream)}
    NSTREAM = len(stream)
    CO, NCO = offsets(CONSTS)
    CC, NCC = offsets(COLS)
    CR, NCR = offsets(ROWS)
    UNITS = units()
    ctx = ExitStack()
    with ctx:
        def sb(name, n, dt=F32):
            return ctx.enter_context(nc.sbuf_tensor(name, [P, n], dt))

        sems = {}

        def S(name):
            if name not in sems:
                sems[name] = ctx.enter_context(nc.semaphore(name))
            return sems[name]

        ring = sb("ring", RING * SLOT)
        consts = sb("consts", NCO)
        cols = sb("cols", NCC)
        rows = sb("rows", NCR)
        X = sb("X", TT * D)[:, :].rearrange("p (t n) -> p t n", t=TT)
        hTb = sb("hT", KT * SEQ)
        hT = hTb[:, :].rearrange("p (k n) -> p k n", k=KT)
        arena = nc.sbuf_base
        U = sb("U", 6144)
        AUX = sb("AUX", 4608)
        QK = sb("QK", 4608)

        def at(name, first, n):
            return nc.alloc_sbuf_tensor_at(name, [P, n], R32, offset=arena + 4 * first)

        WH = at("WH", 0, 4096)[:, :].rearrange("p (s n) -> p s n", s=4)
        WL = at("WL", 4096, 4096)[:, :].rearrange("p (s n) -> p s n", s=4)
        HH = at("HH", 8192, 1024)[:, :].rearrange("p (k n) -> p k n", k=4)
        HL = at("HL", 9216, 1024)[:, :].rearrange("p (k n) -> p k n", k=4)
        XH = at("XH", 10240, 2048)[:, :].rearrange("p (k n) -> p k n", k=KT)
        XL = at("XL", 12288, 2048)[:, :].rearrange("p (k n) -> p k n", k=KT)
        GH = at("GH", 2048, 2048)[:, :].rearrange("p (s k n) -> p s k n", s=4, k=4)
        GL = at("GL", 4096, 2048)[:, :].rearrange("p (s k n) -> p s k n", s=4, k=4)
        OTb = sb("OT", KT * SEQ)
        OT = OTb[:, :].rearrange("p (k n) -> p k n", k=KT)
        G = sb("G", 4 * D)[:, :].rearrange("p (s n) -> p s n", s=4)
        e_at = nc.sbuf_base
        Eb = sb("E", 3 * 768)[:, :].rearrange("p (s n) -> p s n", s=3)
        PTb = sb("PT", 2 * 768)[:, :].rearrange("p (s n) -> p s n", s=2)
        EH, EL = (nc.alloc_sbuf_tensor_at(name, [P, 1024], R32, offset=e_at + 4 * first)[:, :]
                  .rearrange("p (k n) -> p k n", k=4) for name, first in (("EH", 512), ("EL", 1536)))
        scratch = sb("scratch", 4 * W)
        acc = scratch[:, 0:2 * W].rearrange("p (s n) -> p s n", s=2)
        tmp = scratch[:, 2 * W:4 * W].rearrange("p (s n) -> p s n", s=2)
        nab = scratch[:, :].rearrange("p (s t n) -> p s t n", s=2, t=2)
        ones = sb("ones", P)
        zero = sb("zero", 1)
        cond = sb("cond", 24)
        modc = sb("modc", 4 * 48)[:, :].rearrange("p (l v k) -> p l v k", l=4, v=6)
        coef = sb("coef", 8 * 8)[:, :].rearrange("p (i k) -> p i k", i=8)
        ss = sb("ss", 32)
        wn = sb("wn", 3 * 256)[:, :].rearrange("p (s n) -> p s n", s=3)
        rope = sb("rope", 2 * 2 * 48)
        posi = sb("posi", 2, I32)
        posf = sb("posf", 2)
        mx = sb("mx", NST * 2)[:, :].rearrange("p (s n) -> p s n", s=NST)
        sm = sb("sm", NST * 2)[:, :].rearrange("p (s n) -> p s n", s=NST)
        rc = sb("rc", NST * 2)[:, :].rearrange("p (s n) -> p s n", s=NST)
        lam = sb("lam", 8)
        moe = QK[:, 3584:4224]
        rw = moe[:, 0:480].rearrange("p (s n) -> p s n", s=5)
        wrt = sb("wrt", KT * NEXP)
        ps = ctx.enter_context(nc.psum_tensor("ps", [P, 8, W], F32))

        DF, NDFT = offsets(DFT)
        dft_at = CO["c0"][0]
        assert CO["d1"][1] - dft_at >= NDFT
        dft = lambda n: consts[:, dft_at + DF[n][0]:dft_at + DF[n][1]]
        con = lambda n: consts[:, CO[n][0]:CO[n][1]]
        col = lambda n: cols[:, CC[n][0]:CC[n][1]]
        row = lambda n: rows[:, CR[n][0]:CR[n][1]]
        ident = con("ident")
        Cos = rope[:, 0:96].rearrange("p (t n) -> p t n", t=2)
        Sin = rope[:, 96:192].rearrange("p (t n) -> p t n", t=2)
        axcs = con("ax")[:, 0:64].rearrange("p (t n) -> p t n", t=2)
        axsn = con("ax")[:, 64:128].rearrange("p (t n) -> p t n", t=2)

        Ue = U[:, 0:2 * E_IN].rearrange("p (t n) -> p t n", t=2)
        Uo = U[:, :].rearrange("p (t n) -> p t n", t=2)
        U2 = U[:, 0:2 * 2816].rearrange("p (t n) -> p t n", t=2)
        Qm = AUX[:, 0:1536].rearrange("p (t h d) -> p t h d", t=2, h=MH)
        Km = AUX[:, 1536:3072].rearrange("p (t h d) -> p t h d", t=2, h=MH)
        Vm = AUX[:, 3072:4096].rearrange("p (t h d) -> p t h d", t=2, h=MH)
        sqb = PTb
        cT = hTb[:, 0:5 * SEQ].rearrange("p (k n) -> p k n", k=5)
        hc = AUX[:, 0:2048].rearrange("p (k n) -> p k n", k=KT)
        ctx_x = QK[:, 0:2048].rearrange("p (t n) -> p t n", t=2)
        xs = Eb.rearrange("p s n -> p (s n)")[:, 0:2048].rearrange("p (t n) -> p t n", t=2)
        Uc = AUX[:, 2048:4608].rearrange("p (t n) -> p t n", t=2)
        M2 = U[:, 0:2048].rearrange("p (k n) -> p k n", k=KT)
        YF = AUX[:, 0:1024].rearrange("p (k n) -> p k n", k=4)
        Z = YF
        YC = AUX[:, 1024:2048].rearrange("p (k n) -> p k n", k=4)
        Z12 = QK[:, 0:2048].rearrange("p (g n) -> p g n", g=4)
        convy = YC
        convs = QK[:, 2048:3072].rearrange("p (k n) -> p k n", k=4)
        accY = OTb[:, :].rearrange("p (t n) -> p t n", t=2)

        def branch_split(b):
            return (EH, EL) if b % 2 else (HH, HL)

        branch_out = (OT[:, 0:4, :], OT[:, 4:8, :], YF, YC)

        def chunk(name):
            n = number[name]
            _, _, k, w = stream[n]
            s = n % RING
            return ring[:, s * SLOT:s * SLOT + k * w].rearrange("p (k n) -> p k n", k=k)

        def arrived(eng, name):
            n = number[name]
            eng.wait_ge(S(f"loaded{n % RING}"), 16 * (n // RING + 1))
            return chunk(name)

        def last_use(name):
            kind = name[0]
            if kind == "mod":
                return S("mod_acc"), 1 + max(q for q, (l, j) in enumerate(MODSEQ) if (min(l, 2), j) == name[1:])
            if kind in ("eout", "oout", "out2"):
                return S("res"), 4 * {"eout": 0, "oout": 2, "out2": 4}[kind] + 2 * name[1] + 2
            if kind in ("w1", "w2"):
                return S("lo_done"), 64 * name[1] + 8 * name[2] + (4 if kind == "w1" else 8)
            if kind == "gate":
                return S("gate_lo"), 12 * name[1] + 11
            if kind == "branch":
                return S("gate_lo"), 24 * name[1] + 24
            if kind == "in2" and name[1] >= 6:
                return S("glu"), 4
            ph = {"uq": "lat", "ukv": "lat"}.get(kind, kind)
            return S("proj"), g0[ph] + 1 + max(j for j, g in enumerate(groups(ph)) if g[0] == name)

        loads_of = [len(range(s, NSTREAM, RING)) for s in range(RING)]

        def last_in(s):
            return stream[max(range(s, NSTREAM, RING))][0]

        def quarter(w, i):
            return w[:, :, i * P:(i + 1) * P] if w.shape[1] == KT else w[:, i:i + 1, :]

        def split_slot(cu, k):
            return [w[:, cu % 4, :].rearrange("p (k n) -> p k n", k=k) for w in (WH, WL)]

        def expert_unit(e, j, i):
            c, q = (i % 2, i // 2) if i < 8 else (2, i - 8)
            m = 3 * j + c
            s, k = m % RING, KT if c < 2 else 4
            w = ring[:, s * SLOT:(s + 1) * SLOT].rearrange("p (k n) -> p k n", k=k)
            return s, 16 * (loads_of[s] + m // RING + 1) + e * 12, quarter(w, q), KT if c < 2 else 1

        def merge_piece(get, m):
            n, c = m // 3, m % 3
            if c < 2:
                w = get(("gate", n // 4))
                return w[:, 4 * c:4 * c + 4, n % 4 * P:(n % 4 + 1) * P]
            return get(("branch", n // 8))[:, :, n % 8 * P:(n % 8 + 1) * P]

        def mod_bank(q):
            return 1 if any(q0 <= q < q0 + n for _, q0, n in MOD_IN_ATT.values()) else 6

        def qkt(off, tiles):
            return QK[:, off:off + tiles * SEQ].rearrange("p (k n) -> p k n", k=tiles)

        mlaQ, mlaK = qkt(0, 8), qkt(2048, 8)
        dilQ, dilK = qkt(0, 6), qkt(1536, 6)
        diffQ, diffK, mobaQ, mobaK = qkt(0, 4), qkt(1024, 4), qkt(2048, 4), qkt(3072, 4)
        gqaQ, gqaK, gqaC = qkt(0, 4), qkt(1024, 1), qkt(1280, 1)
        naQ, naK, naC = qkt(1536, 4), qkt(2560, 4), qkt(3584, 4)

        def half(ap, h, a, n):
            return ap[64 * (h % 2):64 * (h % 2) + 64, h // 2, a:a + n]

        def scores_of(u):
            ph, h, t = u
            nk = P * (t + 1)
            q0 = P * t
            if ph == "mla":
                return [(0, mlaQ[0:QKD, h, q0:q0 + P], mlaK[0:QKD, h, 0:nk], nk)]
            if ph == "dil":
                return [(g * nk, half(dilQ, g * DH + h, q0, P), half(dilK, g * DH + h, 0, nk), nk) for g in range(DG)]
            if ph == "diff":
                return [(m * W, half(diffQ, 2 * h + m, q0, P), half(diffK, 2 * h + m, 0, nk), nk) for m in range(2)]
            if ph == "moba":
                return [(0, half(mobaQ, h, q0, P), half(mobaK, h, 0, nk), nk)]
            if ph == "gqa":
                r = 64 * (h // 4)
                q = gqaQ[r:r + 64, h % 4, q0:q0 + P]
                return [(0, q, gqaK[r:r + 64, 0, :], SEQ), (SEQ, q, gqaC[r:r + 64, 0, :], SEQ)]
            q = half(naQ, h, q0, P)
            return [(0, q, half(naK, h, 0, SEQ), SEQ), (SEQ, q, half(naC, h, 0, SEQ), SEQ)]

        def softmax_of(u):
            ph, h, t = u
            nk = P * (t + 1)
            if ph == "dil":
                return [(0, DG * nk, con(f"d{t}"))]
            if ph == "diff":
                return [(m * nk, nk, con(f"c{t}")) for m in range(2)]
            if ph in ("mla", "moba"):
                return [(0, nk, con(f"c{t}"))]
            if ph == "gqa":
                return [(0, 2 * SEQ, zero[:, :].broadcast_to([P, W]))]
            return [(0, 2 * SEQ, nab[:, h % 2, t, :])]

        def values_of(u):
            ph, h, t = u
            kb = range(t + 1)
            if ph == "mla":
                return [((0, 64), [Vm[:, b, h, :] for b in kb])]
            if ph == "dil":
                v0 = QR + KVR + ROPE + 2 * DG * DH * HD
                return [((0, 64), [Ue[:, b, v0 + (g * DH + h) * HD:v0 + (g * DH + h + 1) * HD] for g in range(DG) for b in kb])]
            if ph == "diff":
                return [((m * P, (m + 1) * P), [Uo[:, b, 1024 + h * P:1024 + (h + 1) * P] for b in kb]) for m in range(2)]
            if ph == "moba":
                return [((0, 64), [Uo[:, b, 2560 + h * HD:2560 + (h + 1) * HD] for b in kb])]
            if ph == "gqa":
                g = h // 4
                return [((0, 64), [U2[:, b, 640 + g * HD:640 + (g + 1) * HD] for b in range(2)]
                         + [Uc[:, b, 128 + g * HD:128 + (g + 1) * HD] for b in range(2)])]
            return [((0, 64), [U2[:, b, 1792 + h * HD:1792 + (h + 1) * HD] for b in range(2)]
                     + [Uc[:, b, 768 + h * HD:768 + (h + 1) * HD] for b in range(2)])]

        def blocks_of(u):
            return sum(len(v) for _, v in values_of(u))

        OkE = hTb[:, 0:1536].rearrange("p (t n) -> p t n", t=2)
        OkO = AUX[:, 0:2048].rearrange("p (t n) -> p t n", t=2)
        OkB = U2[:, :, 768:1792]

        def output_of(u):
            ph, h, t = u
            if ph == "diff":
                return OkO[:, t, h * P:(h + 1) * P]
            ok = {"mla": OkE, "dil": OkE, "moba": OkO, "gqa": OkB, "na": OkB}[ph]
            c = (0 if ph in ("mla", "gqa") else 512) + h * HD
            return ok[:, t, c:c + HD]

        def wide(u):
            return u[0] == "dil"

        def pt_bank(i):
            b = 4 if wide(UNITS[i]) else 4 + i % 2
            return ps[:, b:b + 2, :].rearrange("p b n -> p (b n)") if wide(UNITS[i]) else ps[:, b, :]

        def s_bank(i):
            return ps[:, 2 * (i % 2):2 * (i % 2) + 2, :].rearrange("p b n -> p (b n)")

        def span(ph):
            ids = [i for i, u in enumerate(UNITS) if u[0] == ph]
            return ids[0], ids[-1] + 1

        def tr_list(ph):
            o = QR + KVR + ROPE
            if ph == "mla":
                return [(lambda t, h=h: Qm[:, t, h, :], mlaQ[0:QKD, h, :]) for h in range(MH)] \
                    + [(lambda t, h=h: Km[:, t, h, :], mlaK[0:QKD, h, :]) for h in range(MH)]
            if ph == "dil":
                return [(lambda t, k=k: Ue[:, t, o + k * P:o + (k + 1) * P],
                         (dilQ[:, k, :] if k < 6 else dilK[:, k - 6, :])) for k in range(12)]
            if ph == "odd":
                dst = [diffQ, diffK, None, mobaQ, mobaK]
                return [(lambda t, c=c, k=k: Uo[:, t, c * 512 + k * P:c * 512 + (k + 1) * P], dst[c][:, k, :])
                        for c in (0, 1, 3, 4) for k in range(4)]
            if ph in ("otE", "otO", "otB"):
                ok, n = {"otE": (OkE, 6), "otO": (OkO, 8), "otB": (OkB, 8)}[ph]
                return [(lambda t, k=k: ok[:, t, k * P:(k + 1) * P], OT[:, k, :]) for k in range(n)]
            out_ = []
            for j in range(4):
                out_.append((lambda t, j=j: U2[:, t, j * P:(j + 1) * P], gqaQ[:, j, :]))
            out_.append((lambda t: U2[:, t, 512:640], gqaK[:, 0, :]))
            out_.append((lambda t: Uc[:, t, 0:128], gqaC[:, 0, :]))
            for k in range(4):
                out_.append((lambda t, k=k: U2[:, t, 768 + k * P:768 + (k + 1) * P], naQ[:, k, :]))
                out_.append((lambda t, k=k: U2[:, t, 1280 + k * P:1280 + (k + 1) * P], naK[:, k, :]))
                out_.append((lambda t, k=k: Uc[:, t, 256 + k * P:256 + (k + 1) * P], naC[:, k, :]))
            return out_

        TRPH = ("dil", "mla", "otE", "odd", "otO", "b2", "otB")
        tr0 = {}
        at = 0
        for ph in TRPH:
            tr0[ph] = at
            at += len(tr_list(ph))

        def head_calls(ph):
            out_ = []
            o = QR + KVR + ROPE
            for tt in range(TT):
                r64 = (Cos[:, tt, 16:48], Sin[:, tt, 16:48], 0, False)
                r16 = (Cos[:, tt, 0:16], Sin[:, tt, 0:16], NOPE, False)
                ax = (axcs[:, tt, :], axsn[:, tt, :], 0, True)
                h64 = lambda ap: ap.rearrange("p (h d) -> p h d", d=HD)
                if ph == "dilq":
                    out_.append((h64(Ue[:, tt, o:o + 768]), row("dilq"), HD ** -0.5) + r64)
                if ph == "dilk":
                    out_.append((h64(Ue[:, tt, o + 768:o + 1536]), row("dilk"), None) + r64)
                if ph == "mla":
                    out_.append((Qm[:, tt], row("mlaq"), QKD ** -0.5) + r16)
                    out_.append((Km[:, tt], row("mlak"), None) + r16)
                if ph[:3] == "odd":
                    c = int(ph[3])
                    gn, sc = {0: ("diffq", 0.125), 1: ("diffk", None), 3: ("mobaq", 0.125), 4: ("mobak", None)}[c]
                    out_.append((h64(Uo[:, tt, 512 * c:512 * c + 512]), row(gn), sc) + r64)
                if ph == "gq":
                    out_.append((h64(U2[:, tt, 0:512]), row("gqaq"), 0.125) + ax)
                if ph == "gk":
                    out_.append((h64(U2[:, tt, 512:640]), row("gqak"), None) + ax)
                    out_.append((h64(Uc[:, tt, 0:128]), row("gqak"), None) + (None, None, 0, False))
            return out_

        HPH = ("dilq", "dilk", "mla", "odd0", "odd1", "odd3", "odd4", "gq", "gk")
        hc0 = {}
        at = 0
        for ph in HPH:
            hc0[ph] = at
            at += len(head_calls(ph))

        def calls_until(ph):
            return hc0[ph] + len(head_calls(ph))

        def groups(ph):
            if ph == "ein":
                return [(("ein", i), hT, KT, tt, 0, min(W, E_IN - i * W)) for i in range(6) for tt in range(TT)]
            if ph == "lat":
                return ([(("uq",), cT, 3, tt, c, w) for tt in range(TT) for c, w in ((0, 512), (512, 256))]
                        + [(("ukv",), cT[:, 3:5, :], 2, tt, c, 512) for tt in range(TT) for c in (0, 512)])
            if ph == "oin":
                return [(("oin", i), hT, KT, tt, 0, W) for i in range(6) for tt in range(TT)]
            g = []
            for i in range(6):
                g += [(("in2", i), hT, KT, tt, 0, IN2[i][1]) for tt in range(TT)]
                if i in CTX_AT:
                    g += [(("in2", i), hc, KT, tt, 0, IN2[i][1]) for tt in range(TT)]
            return g

        g0 = {}
        at = 0
        for ph in ("ein", "lat", "oin", "in2"):
            g0[ph] = at
            at += len(groups(ph))

        def small_loads():
            return [(X, t["x"][0].rearrange("(t p) n -> p t n", p=P)),
                    (rows[:, :], t["rows"].partition_broadcast(P)), (posi[:, :], t["positions"]),
                    (wrt[:, :].rearrange("p (k n) -> p k n", k=KT), t["w_router_2"].rearrange("(k p) n -> p k n", p=P))]

        NSMALL = len(small_loads())
        RES = ("eout", "mlp0", "oout", "mlp1", "out2")
        NORMS = ("mix0", "mlp0", "mix1", "mlp1", "mix2", "ctx2", "mlp2")
        block = ctx.enter_context(nc.Block())

        @block.sync
        def _(sp):
            for n, (name, src, k, w) in enumerate(stream):
                if n >= RING:
                    sp.wait_ge(*last_use(stream[n - RING][0]))
                sp.dma_start(chunk(name), src).then_inc(S(f"loaded{n % RING}"), 16)
            def expert_loads(e, first):
                for m in range(12):
                    j, c, s = m // 3, m % 3, m % RING
                    if first and m < RING:
                        sp.wait_ge(*last_use(last_in(s)))
                    else:
                        jj, cc = (m - RING) // 3, (m - RING) % 3
                        sp.wait_ge(S("lo_done"), 128 + 12 * jj + (7, 8, 12)[cc] + e * 12)
                    if c < 2:
                        src = t["w_expert_gu_2"][0][bass.ds(e + j, 1), :, c * EFF:(c + 1) * EFF]
                        dst = ring[:, s * SLOT:s * SLOT + KT * EFF].rearrange("p (k n) -> p k n", k=KT)
                    else:
                        src = t["w_expert_down_2"][0][bass.ds(e + j, 1), :, :]
                        dst = ring[:, s * SLOT:(s + 1) * SLOT].rearrange("p (k n) -> p k n", k=4)
                    sp.dma_start(dst, src.rearrange("o (k p) n -> p (o k) n", p=P)).then_inc(S(f"loaded{s}"), 16)

            expert_loads(0, True)
            with sp.Fori(1, NEXP // 4) as it:
                expert_loads(it * 4, False)
            sp.wait_ge(S("final_done"), 2)
            sp.dma_start(out[0].rearrange("(t p) n -> p t n", p=P), xs).then_inc(S("stored"), 16)
            sp.wait_ge(S("stored"), 16)

        @block.tensor
        def _(pe):
            mm = nc.tensor.matmul
            pe.wait_ge(S("ones_set"), 2)

            def mm3(o, lh, ll, rh, rl, start, stop):
                mm(o, lh, rh, start=start, stop=False)
                mm(o, lh, rl, start=False, stop=False)
                return mm(o, ll, rh, start=False, stop=stop)

            def mod_sum(q):
                pe.wait_ge(S("mod_acc"), q + 1)
                if q:
                    pe.wait_ge(S("mod_fin"), q)
                mm(ps[:, mod_bank(q), :], ones[:, :], acc[:, q % 2, :], start=True, stop=True).then_inc(S("mod_sum"), 1)

            def norm_transposes(i):
                pe.wait_ge(S("norm_scaled"), 2 * (i + 1))
                for k in range(KT):
                    n = KT * i + k
                    if n >= 4 and k % 2 == 0:
                        pe.wait_ge(S("norm_out"), n - 2)
                    for tt in range(TT):
                        last = nc.tensor.transpose(ps[:, 4 + (k // 2) % 2, 256 * (k % 2) + P * tt:256 * (k % 2) + P * tt + P],
                                                   xs[:, tt, k * P:(k + 1) * P], ident)
                    last.then_inc(S("norm_tr"), 1)

            def projections(ph, after=None):
                gs = groups(ph)
                for j, (name, src, nk, tt, c, w) in enumerate(gs):
                    g = g0[ph] + j
                    wt = arrived(pe, name)
                    if g >= 4:
                        pe.wait_ge(S("proj_out"), g - 3)
                    for k in range(nk):
                        last = mm(ps[:, g % 4, 0:w], src[:, k, P * tt:P * tt + P], wt[:, k, c:c + w],
                                  start=(k == 0), stop=(k == nk - 1))
                    last.then_inc(S("proj"), 1)
                    if after and (j + 1 == len(gs) or gs[j + 1][0] != name):
                        after(name)

            def head_transposes(ph, j0=0, j1=None):
                for j, (src, dst) in list(enumerate(tr_list(ph)))[j0:j1]:
                    n = tr0[ph] + j
                    if n >= 4 and n % 2 == 0:
                        pe.wait_ge(S("qkt_out"), n - 2)
                    for tt in range(TT):
                        s = src(tt)
                        d = s.shape[-1]
                        last = nc.tensor.transpose(ps[0:d, 4 + (n // 2) % 2, 256 * (n % 2) + P * tt:256 * (n % 2) + P * tt + P],
                                                   s, ident)
                    last.then_inc(S("qkt"), 1)

            def attention(ph):
                a, b = span(ph)

                def score(i):
                    if i >= 2:
                        pe.wait_ge(S("masked"), i - 1)
                    for c, q, k, n in scores_of(UNITS[i]):
                        last = mm(s_bank(i)[:, c:c + n], q, k, start=True, stop=True)
                    last.then_inc(S("scored"), 1)

                def transposes(i):
                    pe.wait_ge(S("exped"), i + 1)
                    lag = 1 if wide(UNITS[i]) else 2
                    if i >= lag:
                        pe.wait_ge(S("pt_out"), i - lag + 1)
                    for j in range(blocks_of(UNITS[i])):
                        last = nc.tensor.transpose(pt_bank(i)[:, j * P:(j + 1) * P], Eb[:, i % 3, j * P:(j + 1) * P], ident)
                    last.then_inc(S("pt"), 1)

                def weigh(i):
                    pe.wait_ge(S("pt_out"), i + 1)
                    if i >= 2:
                        pe.wait_ge(S("o_out"), i - 1)
                    n = 0
                    for (c0, c1), vs in values_of(UNITS[i]):
                        for j, v in enumerate(vs):
                            last = mm(ps[:, 6 + i % 2, c0:c1], PTb[:, i % 2, n * P:(n + 1) * P], v,
                                      start=(j == 0), stop=(j == len(vs) - 1))
                            n += 1
                    last.then_inc(S("weighed"), 1)

                for i in range(a, b + 3):
                    if i < b:
                        score(i)
                    if a <= i - 2 < b:
                        transposes(i - 2)
                    if a <= i - 3:
                        weigh(i - 3)
                    if ph in MOD_IN_ATT and (i - a) % 4 == 1 and i - a >= 5:
                        mod_sum(MOD_IN_ATT[ph][1] + (i - a) // 4 - 1)

            def out_projection(name, nk, r):
                for n in range(2):
                    wt = arrived(pe, (name, n))
                    for tt in range(TT):
                        for k in range(nk):
                            last = mm(ps[:, 2 * n + tt, :], (M2 if name == "out2" else OT)[:, k, P * tt:P * tt + P],
                                      wt[:, k, :], start=(k == 0), stop=(k == nk - 1))
                        last.then_inc(S("res"), 1)

            def mlp(l, q0, r):
                qd = [q0]
                for j in range(FF // W):
                    for f in range(4):
                        cu, n = 64 * l + 8 * j + f, 32 * l + 4 * j + f
                        wh, wl = split_slot(cu, KT)
                        pe.wait_ge(S("lo_done"), cu + 1)
                        if n >= 2:
                            pe.wait_ge(S("hid_read"), 3 * (n - 1))
                        for k in range(KT):
                            last = mm3(ps[:, 4 + n % 2, 0:SEQ], wh[:, k, :], wl[:, k, :], XH[:, k, :], XL[:, k, :],
                                       start=(k == 0), stop=(k == KT - 1))
                        last.then_inc(S("hid"), 1)
                    for k in range(4):
                        cu = 64 * l + 8 * j + 4 + k
                        wh, wl = split_slot(cu, 1)
                        pe.wait_ge(S("lo_done"), cu + 1)
                        pe.wait_ge(S("hid_out"), 32 * l + 4 * j + k + 1)
                        for n in range(2):
                            for tt in range(TT):
                                c, cn = slice(P * tt, P * tt + P), slice(n * W, (n + 1) * W)
                                last = mm3(ps[:, 2 * n + tt, :], HH[:, k, c], HL[:, k, c], wh[:, 0, cn], wl[:, 0, cn],
                                           start=(j == 0 and k == 0), stop=(j == 7 and k == 3))
                                if j == 7 and k == 3:
                                    last.then_inc(S("res"), 1)
                        if not (j == 7 and k == 3):
                            last.then_inc(S("w2_used"), 1)
                    for m in mod_in_mlp(l, j):
                        mod_sum(qd[0])
                        qd[0] += 1
                        if l == 1 and m < 4:
                            mod_sum(qd[0])
                            qd[0] += 1

            for q in range(4):
                mod_sum(q)
            pe.wait_ge(S("ident_in"), 16)
            pe.wait_ge(S("consts_in"), 16 * NSMALL)
            norm_transposes(0)
            pe.wait_ge(S("norm_out"), KT)
            projections("ein", after=lambda name: mod_sum(4 + name[1]) if name[0] == "ein" else None)
            pe.wait_ge(S("lat_scaled"), 1)
            for k in range(5):
                if k == 4:
                    pe.wait_ge(S("lat_out"), 2)
                for tt in range(TT):
                    last = nc.tensor.transpose(ps[:, 4 + (k // 2) % 2, 256 * (k % 2) + P * tt:256 * (k % 2) + P * tt + P],
                                               Ue[:, tt, k * P:(k + 1) * P], ident)
                last.then_inc(S("lat_tr"), 1)
            pe.wait_ge(S("lat_out"), 5)
            projections("lat")
            mod_sum(10)
            mod_sum(11)
            pe.wait_ge(S("roped"), calls_until("dilk"))
            head_transposes("dil")
            pe.wait_ge(S("qkt_out"), tr0["mla"])
            pe.wait_ge(S("proj_out"), g0["oin"])
            pe.wait_ge(S("mod_fin"), 12)
            attention("dil")
            pe.wait_ge(S("roped"), calls_until("mla"))
            head_transposes("mla")
            pe.wait_ge(S("qkt_out"), tr0["otE"])
            attention("mla")
            pe.wait_ge(S("o_out"), span("mla")[1])
            head_transposes("otE")
            pe.wait_ge(S("qkt_out"), tr0["odd"])
            pe.wait_ge(S("mod_fin"), 16)
            out_projection("eout", 6, 0)
            norm_transposes(1)
            pe.wait_ge(S("split_x"), 1)
            mlp(0, 16, 1)
            norm_transposes(2)
            pe.wait_ge(S("norm_out"), 3 * KT)
            def after_odd(name):
                if name[1] == 4:
                    pe.wait_ge(S("roped"), calls_until("odd1"))
                    head_transposes("odd", 0, 8)

            projections("oin", after_odd)
            pe.wait_ge(S("qkt_out"), tr0["odd"] + 8)
            pe.wait_ge(S("proj_out"), g0["in2"])
            attention("diff")
            pe.wait_ge(S("roped"), calls_until("odd4"))
            head_transposes("odd", 8, 16)
            pe.wait_ge(S("qkt_out"), tr0["otO"])
            attention("moba")
            pe.wait_ge(S("sub_done"), 1)
            pe.wait_ge(S("o_out"), span("moba")[1])
            head_transposes("otO")
            pe.wait_ge(S("qkt_out"), tr0["b2"])
            pe.wait_ge(S("mod_fin"), 28)
            out_projection("oout", 8, 2)
            norm_transposes(3)
            pe.wait_ge(S("split_x"), 2)
            mlp(1, 28, 3)
            norm_transposes(4)
            norm_transposes(5)
            pe.wait_ge(S("norm_out"), 6 * KT)
            def after_b2(name):
                if name[1] == 3:
                    pe.wait_ge(S("roped"), calls_until("gk"))
                    head_transposes("b2", 0, 6)
                if name[1] == 5:
                    head_transposes("b2", 6, None)

            projections("in2", after_b2)
            pe.wait_ge(S("qkt_out"), tr0["otB"])
            wa = arrived(pe, ("in2", 6))
            wb = arrived(pe, ("in2", 7))
            for f in range(4):
                if f >= 2:
                    pe.wait_ge(S("glu_out"), f - 1)
                for wt, c in ((wa, 0), (wb, SEQ)):
                    for k in range(KT):
                        last = mm(ps[:, 4 + f % 2, c:c + SEQ], wt[:, k, f * P:(f + 1) * P], hT[:, k, :],
                                  start=(k == 0), stop=(k == KT - 1))
                last.then_inc(S("glu"), 1)
            pe.wait_ge(S("glu_out"), 4)
            pe.wait_ge(S("proj_out"), g0["in2"] + len(groups("in2")))
            attention("gqa")
            attention("na")
            pe.wait_ge(S("pt_out"), len(UNITS))
            pe.wait_ge(S("o_out"), len(UNITS))
            pe.wait_ge(S("dft_in"), 16)
            CL = dft("CL").rearrange("p (t n) -> p t n", t=2)
            SL = dft("SL").rearrange("p (t n) -> p t n", t=2)
            for g in range(4):
                for m, c in ((CL, 0), (SL, SEQ)):
                    for tt in range(TT):
                        last = mm(ps[:, g, c:c + SEQ], U2[:, tt, 2304 + g * P:2304 + (g + 1) * P], m[:, tt, :],
                                  start=(tt == 0), stop=(tt == TT - 1))
                last.then_inc(S("dft1"), 1)
            for g in range(4):
                pe.wait_ge(S("dft1_out"), g + 1)
                b, c = 4 + g // 2, SEQ * (g % 2)
                mm(ps[:, b, c:c + SEQ], dft("CD"), Z12[:, g, 0:SEQ], start=True, stop=False)
                mm(ps[:, b, c:c + SEQ], dft("SD"), Z12[:, g, SEQ:2 * SEQ], start=False, stop=True).then_inc(S("dft2"), 1)
            pe.wait_ge(S("dft2_out"), 4)
            pe.wait_ge(S("conv_sq"), 1)
            for k in range(4):
                last = mm(ps[:, 6, 0:SEQ], ones[:, :], convs[:, k, :], start=(k == 0), stop=(k == 3))
            last.then_inc(S("conv_sum"), 1)
            head_transposes("otB")
            pe.wait_ge(S("dft2_out"), 4)
            pe.wait_ge(S("conv_out"), 4)
            pe.wait_ge(S("qkt_out"), tr0["otB"] + 8)
            pe.wait_ge(S("mx_lo"), 1)
            for n in range(32):
                b = n // 8
                yh, yl = branch_split(b)
                if n >= 2:
                    pe.wait_ge(S("merge_out"), n - 1)
                for c in range(3):
                    m = 3 * n + c
                    pe.wait_ge(S("gate_lo"), m + 1)
                    if c == 2 and n % 8 == 0:
                        pe.wait_ge(S("y_lo"), b + 1)
                    for k in range(4):
                        if c < 2:
                            last = mm3(ps[:, 4 + n % 2, 0:SEQ], GH[:, m % 4, k, :], GL[:, 3 - m % 4, k, :],
                                       XH[:, 4 * c + k, :], XL[:, 4 * c + k, :], start=(c + k == 0), stop=(c + k == 4))
                        else:
                            last = mm3(ps[:, 4 + n % 2, SEQ:2 * SEQ], GH[:, m % 4, k, :], GL[:, 3 - m % 4, k, :],
                                       yh[:, k, :], yl[:, k, :], start=(k == 0), stop=(k == 3))
                    last.then_inc(S("merge" if c == 2 else "gate_free"), 1)
            pe.wait_ge(S("merged"), 1)
            out_projection("out2", 8, 4)
            norm_transposes(6)
            pe.wait_ge(S("norm_out"), 7 * KT)
            wr = wrt[:, :].rearrange("p (k n) -> p k n", k=KT)
            for tt in range(TT):
                for k in range(KT):
                    last = mm(ps[:, 6, 16 * tt:16 * tt + 16], hT[:, k, P * tt:P * tt + P], wr[:, k, :],
                              start=(k == 0), stop=(k == KT - 1))
            last.then_inc(S("logits"), 1)
            def expert(e, j):
                for f in range(4):
                    pe.wait_ge(S("merge_out"), 32 + 4 * j + f - 1 + e * 4)
                    for part in range(2):
                        i = 2 * f + part
                        wh, wl = split_slot(i, KT)
                        pe.wait_ge(S("lo_done"), 128 + 12 * j + i + 1 + e * 12)
                        for k in range(KT):
                            last = mm3(ps[:, 4 + f % 2, part * SEQ:(part + 1) * SEQ], wh[:, k, :], wl[:, k, :],
                                       XH[:, k, :], XL[:, k, :], start=(k == 0), stop=(k == KT - 1))
                        last.then_inc(S("merge" if part else "gate_used"), 1)
                pe.wait_ge(S("res_out"), 20 + 4 * j + e * 4)
                for k in range(4):
                    wh, wl = split_slot(8 + k, 1)
                    pe.wait_ge(S("lo_done"), 128 + 12 * j + 8 + k + 1 + e * 12)
                    pe.wait_ge(S("merge_out"), 32 + 4 * j + k + 1 + e * 4)
                    for n in range(2):
                        for tt in range(TT):
                            c, cn = slice(P * tt, P * tt + P), slice(n * W, (n + 1) * W)
                            last = mm3(ps[:, 2 * n + tt, :], HH[:, k, c], HL[:, k, c], wh[:, 0, cn], wl[:, 0, cn],
                                       start=(k == 0), stop=(k == 3))
                            if k == 3:
                                last.then_inc(S("res"), 1)
                    if k < 3:
                        last.then_inc(S("w2_used"), 1)

            pe.wait_ge(S("split_x"), 3)
            with pe.Fori(0, NEXP // 4 - 1) as it:
                for j in range(4):
                    expert(it * 4, j)
            for j in range(4):
                expert(NEXP - 4, j)

        @block.scalar
        def _(act):
            A = nc.scalar.activation
            act.dma_start(cols[:, :], t["cols"]).then_inc(S("cols_in"), 16)
            act.dma_start(consts[:, :], t["consts"]).then_inc(S("ident_in"), 16)
            for dst, src in small_loads():
                act.dma_start(dst, src).then_inc(S("consts_in"), 16)
            act.wait_ge(S("cols_in"), 16)
            A(cond[:, :], col("c"), ACT.Silu).then_inc(S("cond"), 1)
            act.wait_ge(S("ident_in"), 16)
            act.wait_ge(S("consts_in"), 16 * NSMALL)

            def square_sums(i, src):
                for tt in range(TT):
                    A(xs[:, tt, :], src[:, tt, :], ACT.Square, accum_out=ss[:, 2 * (i % 2) + tt:2 * (i % 2) + tt + 1]) \
                        .then_inc(S("norm_sq"), 1)

            def norm_out(i, dst):
                l, v = ((0, 0), (0, 3), (1, 0), (1, 3), (2, 0), (3, 0), (2, 3))[i]
                act.wait_ge(S("coef"), i + 1)
                for k in range(KT):
                    act.wait_ge(S("norm_tr"), KT * i + (k | 1) + 1)
                    p = ps[:, 4 + (k // 2) % 2, 256 * (k % 2):256 * (k % 2) + 256]
                    ins = A(dst[:, k, :], p, ACT.Identity, bias=modc[:, l, v, k:k + 1], scale=coef[:, i, k:k + 1])
                    if i in (1, 3, 6):
                        ins = A(XH[:, k, :], p, ACT.Identity, bias=modc[:, l, v, k:k + 1], scale=coef[:, i, k:k + 1])
                    ins.then_inc(S("norm_out"), 1)

            def proj_out(ph, place, only=None):
                for j, (name, _, nk, tt, c, w) in enumerate(groups(ph)):
                    if only is not None and name[1] not in only:
                        continue
                    g = g0[ph] + j
                    act.wait_ge(S("proj"), g + 1)
                    cps = place(j, name, tt, c, w, ps[:, g % 4, 0:w])
                    for dst, src, *scale in cps:
                        last = A(dst, src, ACT.Copy, scale=scale[0] if scale else 1.0)
                    last.then_inc(S("proj_out"), 1)

            def qkt_out(ph, j0=0, j1=None):
                for j, (src, dst) in list(enumerate(tr_list(ph)))[j0:j1]:
                    n = tr0[ph] + j
                    act.wait_ge(S("qkt"), (n | 1) + 1)
                    d = dst.shape[0]
                    gain = col("subln")[:, 0:1] if ph == "otO" and j < 4 else 1.0
                    A(dst, ps[0:d, 4 + (n // 2) % 2, 256 * (n % 2):256 * (n % 2) + 256], ACT.Copy, scale=gain) \
                        .then_inc(S("qkt_out"), 1)

            def head_squares(ph, projected):
                act.wait_ge(S("proj_out"), projected)
                for n, (x, *_) in enumerate(head_calls(ph)):
                    c = hc0[ph] + n
                    if c >= 2:
                        act.wait_ge(S("heads_summed"), c - 1)
                    h, d = x.shape[1], x.shape[2]
                    A(sqb[:, c % 2, 0:h * d].rearrange("p (h d) -> p h d", h=h), x, ACT.Square).then_inc(S("heads_sq"), 1)

            def attention(ph):
                a, b = span(ph)
                for i in range(a, b + 2):
                    if i < b:
                        act.wait_ge(S("masked"), i + 1)
                        for j, (c, n, _) in enumerate(softmax_of(UNITS[i])):
                            last = A(Eb[:, i % 3, c:c + n], Eb[:, i % 3, c:c + n], ACT.Exp, bias=mx[:, i % NST, j:j + 1],
                                     scale=-1.0, accum_out=sm[:, i % NST, j:j + 1])
                        last.then_inc(S("exped"), 1)
                    if i - 2 >= a:
                        m = i - 2
                        n = P * blocks_of(UNITS[m])
                        act.wait_ge(S("pt"), m + 1)
                        if m >= 2:
                            act.wait_ge(S("weighed"), m - 1)
                        A(PTb[:, m % 2, 0:n], pt_bank(m)[:, 0:n], ACT.Copy).then_inc(S("pt_out"), 1)

            def mlp_hi(l, u):
                j, i = u // 8, u % 8
                cu = 64 * l + u
                w = arrived(act, ("w1", l, j) if i < 4 else ("w2", l, j))
                if u >= 4:
                    if i < 4:
                        act.wait_ge(S("w2_used"), 31 * l + 4 * (j - 1) + i + 1)
                    else:
                        act.wait_ge(S("hid"), 32 * l + 4 * j + i - 4 + 1)
                A(split_slot(cu, KT if i < 4 else 1)[0], quarter(w, i % 4), ACT.Copy).then_inc(S("hi_done"), 1)

            def mlp(l):
                for n in range(32):
                    m = 32 * l + n
                    act.wait_ge(S("hid"), m + 1)
                    if m >= 2:
                        act.wait_ge(S("hid_out"), m - 1)
                    r, sq = tmp[:, m % 2, 0:SEQ], tmp[:, m % 2, SEQ:2 * SEQ]
                    A(r, ps[:, 4 + m % 2, 0:SEQ], ACT.Relu).then_inc(S("hid_read"), 1)
                    act.wait_ge(S("hid_read"), 3 * m + 1)
                    A(HH[:, n % 4, :], r, ACT.Square).then_inc(S("hid_read"), 1)
                    A(sq, r, ACT.Square).then_inc(S("hid_read"), 1)
                    mlp_hi(l, 8 * (n // 4) + 4 + n % 4)
                    if n % 4 == 3 and n < 31:
                        for f in range(4):
                            mlp_hi(l, 8 * (n // 4 + 1) + f)

            square_sums(0, X)
            norm_out(0, hT)
            act.wait_ge(S("angles"), 2)
            A(rope[:, 0:192], rope[:, 0:192], ACT.Sin).then_inc(S("sines"), 1)
            A(lam[:, 2:4], lam[:, 0:2], ACT.Exp).then_inc(S("lam_exp"), 1)
            ein = lambda j, name, tt, c, w, p: [(Ue[:, tt, name[1] * W:name[1] * W + w], p)]
            proj_out("ein", ein, (0, 1))
            act.wait_ge(S("proj_out"), 4)
            for tt in range(TT):
                A(xs[:, 0, 0:QR], Ue[:, tt, 0:QR], ACT.Square, accum_out=ss[:, 8 + tt:9 + tt]).then_inc(S("lat_sq"), 1)
                A(xs[:, 1, 0:KVR], Ue[:, tt, QR:QR + KVR], ACT.Square, accum_out=ss[:, 10 + tt:11 + tt]).then_inc(S("lat_sq"), 1)
                act.wait_ge(S("lat_sq"), 2 * tt + 2)
            proj_out("ein", ein, (2,))
            head_squares("dilq", 6)
            proj_out("ein", ein, (3, 4))
            head_squares("dilk", 10)
            proj_out("ein", ein, (5,))
            for k in range(5):
                act.wait_ge(S("lat_tr"), min((k | 1) + 1, 5))
                gain = col("qlat")[:, k:k + 1] if k < 3 else col("kvlat")[:, k - 3:k - 2]
                A(cT[:, k, :], ps[:, 4 + (k // 2) % 2, 256 * (k % 2):256 * (k % 2) + 256], ACT.Copy, scale=gain) \
                    .then_inc(S("lat_out"), 1)

            def lat_place(j, name, tt, c, w, p):
                if name[0] == "uq":
                    return [(AUX[:, 768 * tt + c:768 * tt + c + w], p)]
                h0 = c // P
                v = p.rearrange("p (h d) -> p h d", d=P)
                return [(Km[:, tt, h0:h0 + 4, 0:NOPE], v[:, :, 0:NOPE]), (Vm[:, tt, h0:h0 + 4, :], v[:, :, NOPE:])]

            proj_out("lat", lat_place)
            act.wait_ge(S("krope"), 2)
            head_squares("mla", g0["oin"])
            qkt_out("dil")
            attention("dil")
            qkt_out("mla")
            attention("mla")
            qkt_out("otE")
            act.wait_ge(S("res_out"), 4)
            square_sums(1, X)
            for f in range(4):
                mlp_hi(0, f)
            norm_out(1, hT)
            mlp(0)
            act.wait_ge(S("res_out"), 8)
            square_sums(2, X)
            norm_out(2, hT)
            oin = lambda j, name, tt, c, w, p: [(Uo[:, tt, name[1] * W:name[1] * W + w], p)]
            for c in range(6):
                proj_out("oin", oin, (c,))
                if c in (0, 1, 3, 4):
                    head_squares(f"odd{c}", g0["oin"] + 2 * c + 2)
                if c == 4:
                    qkt_out("odd", 0, 8)
            attention("diff")
            qkt_out("odd", 8, 16)
            attention("moba")
            qkt_out("otO")
            act.wait_ge(S("res_out"), 12)
            square_sums(3, X)
            for f in range(4):
                mlp_hi(1, f)
            norm_out(3, hT)
            mlp(1)
            act.wait_ge(S("res_out"), 16)
            square_sums(4, X)
            norm_out(4, hT)
            act.wait_ge(S("ctx_in"), 16)
            square_sums(5, ctx_x)
            norm_out(5, hc)

            def in2_place(j, name, tt, c, w, p):
                i = name[1]
                seen = [g for g in groups("in2")[:j] if g[0] == name]
                if len(seen) >= 2:
                    return [(Uc[:, tt, CTX_AT[i]:CTX_AT[i] + w], p)]
                dst = U2[:, tt, IN2[i][0]:IN2[i][0] + w]
                if i == 0:
                    return [(dst.rearrange("p (j g d) -> p g j d", g=2, d=HD), p.rearrange("p (g j d) -> p g j d", g=2, d=HD))]
                return [(dst, p, HD ** -0.5) if i == 2 else (dst, p)]

            proj_out("in2", in2_place, (0,))
            head_squares("gq", g0["in2"] + 2)
            proj_out("in2", in2_place, (1,))
            head_squares("gk", g0["in2"] + 6)
            proj_out("in2", in2_place, (2, 3))
            qkt_out("b2", 0, 6)
            proj_out("in2", in2_place, (4, 5))
            qkt_out("b2", 6, None)
            for f in range(4):
                act.wait_ge(S("glu"), f + 1)
                if f >= 2:
                    act.wait_ge(S("glu_out"), f - 1)
                A(tmp[:, f % 2, 0:SEQ], ps[:, 4 + f % 2, SEQ:2 * SEQ], ACT.Sigmoid).then_inc(S("glu_sig"), 1)
            attention("gqa")
            attention("na")
            for g in range(4):
                act.wait_ge(S("dft1"), g + 1)
                A(Z12[:, g, :], ps[:, g, :], ACT.Copy).then_inc(S("dft1_out"), 1)
            for g in range(4):
                act.wait_ge(S("dft2"), (g | 1) + 1)
                A(YF[:, g, :], ps[:, 4 + g // 2, SEQ * (g % 2):SEQ * (g % 2) + SEQ], ACT.Copy).then_inc(S("dft2_out"), 1)
            act.wait_ge(S("conv_tap"), TAPS)
            A(convs[:, :, :], convy[:, :, :], ACT.Square).then_inc(S("conv_sq"), 1)

            def piece_hi(m):
                w = merge_piece(lambda name: arrived(act, name), m)
                n, c = m // 3, m % 3
                if m >= 4:
                    if c == 0:
                        act.wait_ge(S("merge"), n - 1)
                    else:
                        act.wait_ge(S("gate_free"), 2 * n - 2 + c)
                A(GH[:, m % 4, :, :], w, ACT.Copy).then_inc(S("gate_hi"), 1)

            def branch_hi(b):
                A(branch_split(b)[0], branch_out[b], ACT.Copy).then_inc(S("y_hi"), 1)

            for c in range(2):
                A(XH[:, 4 * c:4 * c + 4, :], hT[:, 4 * c:4 * c + 4, :], ACT.Copy).then_inc(S("mx_hi"), 1)
            piece_hi(0)
            piece_hi(1)
            qkt_out("otB")
            act.wait_ge(S("qkt_out"), tr0["otB"] + 8)
            branch_hi(0)
            piece_hi(2)
            piece_hi(3)
            act.wait_ge(S("conv_scaled"), 1)
            for k in range(4):
                A(YC[:, k, :], convs[:, k, :], ACT.Silu, scale=col("convg")[:, k:k + 1]).then_inc(S("conv_out"), 1)
            for n in range(32):
                for m in range(3 * n + 4, min(3 * n + 7, 96)):
                    piece_hi(m)
                act.wait_ge(S("merge"), n + 1)
                if n >= 2:
                    act.wait_ge(S("merge_out"), n - 1)
                A(tmp[:, n % 2, 0:SEQ], ps[:, 4 + n % 2, 0:SEQ], ACT.Sigmoid).then_inc(S("merge_act"), 1)
                if n % 8 == 2 and n < 24:
                    if n == 18:
                        act.wait_ge(S("conv_out"), 4)
                    branch_hi(n // 8 + 1)
            act.wait_ge(S("res_out"), 20)
            square_sums(6, X)

            def expert_hi(e, j, i):
                s, load, w, k = expert_unit(e, j, i)
                act.wait_ge(S(f"loaded{s}"), load)
                if i < 3:
                    act.wait_ge(S("w2_used"), 62 + 3 * j - 2 + i + e * 3)
                elif i == 3:
                    act.wait_ge(S("res"), 20 + 4 * j + e * 4)
                elif i % 2 == 0:
                    act.wait_ge(S("gate_used"), 4 * j + (i - 4) // 2 + 1 + e * 4)
                else:
                    act.wait_ge(S("merge"), 32 + 4 * j + (i - 4) // 2 + 1 + e * 4)
                A(split_slot(i, k)[0], w, ACT.Copy).then_inc(S("hi_done"), 1)

            for i in range(4):
                expert_hi(0, 0, i)
            norm_out(6, hT)
            act.wait_ge(S("logits"), 1)
            A(moe[:, 0:32], ps[:, 6, 0:32], ACT.Sigmoid).then_inc(S("router_sig"), 1)
            def expert(e, j, last=False):
                def silu(f):
                    act.wait_ge(S("merge"), 32 + 4 * j + f + 1 + e * 4)
                    act.wait_ge(S("merge_out"), 32 + 4 * j + f - 1 + e * 4)
                    A(tmp[:, f % 2, 0:SEQ], ps[:, 4 + f % 2, 0:SEQ], ACT.Silu).then_inc(S("merge_act"), 1)

                for f in range(4):
                    expert_hi(e, j, 4 + 2 * f)
                    expert_hi(e, j, 5 + 2 * f)
                    silu(f)
                if not last:
                    for i in range(4):
                        expert_hi(e, j + 1, i)

            with act.Fori(0, NEXP // 4 - 1) as it:
                for j in range(4):
                    expert(it * 4, j)
            for j in range(4):
                expert(NEXP - 4, j, last=(j == 3))
            act.wait_ge(S("final_x"), 1)
            square_sums(7, X)

        @block.gpsimd
        def _(pool):
            pool.memset(ones[:, :], 1.0).then_inc(S("ones_set"), 1)
            pool.memset(zero[:, :], 0.0).then_inc(S("ones_set"), 1)
            pool.wait_ge(S("ident_in"), 16)
            pool.wait_ge(S("consts_in"), 16 * NSMALL)

            def gate_bias(l):
                for i, v in enumerate((2, 5)):
                    b = (t["ada_b"][l] if l < 2 else t["b_mod_2"][0])[v * D:(v + 1) * D]
                    pool.dma_start(G[:, 2 * (l % 2) + i, :], b.partition_broadcast(P)) \
                        .then_inc(S(f"gate_bias{l}"), 16)

            links = [0]

            def link(ins):
                links[0] += 1
                ins.then_inc(S("pool_chain"), 1)
                pool.wait_ge(S("pool_chain"), links[0])

            def rotate(ph):
                for n, (x, _, _, cos, sin, r0, pairs) in enumerate(head_calls(ph)):
                    pool.wait_ge(S("heads_scaled"), hc0[ph] + n + 1)
                    h = x.shape[1]
                    if cos is None:
                        pool.sem_inc(S("roped"), 1)
                        continue
                    hw = cos.shape[-1]
                    if pairs:
                        v = x.rearrange("p h (m two) -> p h m two", two=2)
                        x1, x2 = v[:, :, :, 0], v[:, :, :, 1]
                    else:
                        x1, x2 = x[:, :, r0:r0 + hw], x[:, :, r0 + hw:r0 + 2 * hw]
                    cb, sb_ = spread(cos, 1, h), spread(sin, 1, h)
                    flat = tmp.rearrange("p s n -> p (s n)")
                    a, b = (flat[:, 512 * i:512 * i + h * hw].rearrange("p (h d) -> p h d", h=h) for i in range(2))
                    tt_ = lambda o, i0, i1, op: pool.tensor_tensor(out=o, in0=i0, in1=i1, op=op)
                    tt_(a, x1, sb_, ALU.mult)
                    link(tt_(b, x2, sb_, ALU.mult))
                    tt_(x1, x1, cb, ALU.mult)
                    link(tt_(x2, x2, cb, ALU.mult))
                    link(tt_(x1, x1, b, ALU.subtract))
                    tt_(x2, x2, a, ALU.add).then_inc(S("roped"), 1)
                    pool.wait_ge(S("roped"), hc0[ph] + n + 1)

            def mlp(l):
                for j in range(FF // W):
                    for i in range(8):
                        cu = 64 * l + 8 * j + i
                        hi, lo = split_slot(cu, KT if i < 4 else 1)
                        src = quarter(chunk(("w1", l, j) if i < 4 else ("w2", l, j)), i % 4)
                        pool.wait_ge(S("hi_done"), cu + 1)
                        pool.tensor_tensor(out=lo, in0=src, in1=hi.bitcast(F32), op=ALU.subtract).then_inc(S("lo_done"), 1)

            def expert(e, j):
                for i in range(12):
                    _, _, src, k = expert_unit(e, j, i)
                    hi, lo = split_slot(i, k)
                    pool.wait_ge(S("hi_done"), 128 + 12 * j + i + 1 + e * 12)
                    pool.tensor_tensor(out=lo, in0=src, in1=hi.bitcast(F32), op=ALU.subtract).then_inc(S("lo_done"), 1)

            def na_bias(h):
                if h >= 2:
                    pool.wait_ge(S("masked"), span("na")[0] + 2 * (h - 1))
                pool.dma_start(nab[:, h % 2, :, 0:256], t["na_bias"][h].rearrange("(t p) n -> p t n", p=P)) \
                    .then_inc(S("nab_in"), 16)

            def na_mask(h):
                pool.wait_ge(S("nab_in"), 16 * (h + 1))
                pool.tensor_tensor(out=nab[:, h % 2, :, 0:256], in0=nab[:, h % 2, :, 0:256],
                                   in1=con("na").rearrange("p (t n) -> p t n", t=2), op=ALU.add).then_inc(S("nab"), 1)

            gate_bias(0)
            gate_bias(1)
            pool.wait_ge(S("sines"), 1)
            for ph in ("dilq", "dilk", "mla"):
                rotate(ph)
            mlp(0)
            for ph in ("odd0", "odd1", "odd3", "odd4"):
                rotate(ph)
            pool.wait_ge(S("res_out"), 8)
            gate_bias(2)
            mlp(1)
            pool.wait_ge(S("res_out"), 16)
            pool.dma_start(ctx_x, t["ctx_2"][0].rearrange("(t p) n -> p t n", p=P)).then_inc(S("ctx_in"), 16)
            rotate("gq")
            rotate("gk")
            pool.wait_ge(S("glu_out"), 4)
            pool.memset(nab[:, :, :, 256:512], 0.0).then_inc(S("nab_zero"), 1)
            pool.wait_ge(S("nab_zero"), 1)
            pool.dma_start(consts[:, dft_at:dft_at + NDFT], t["dft"]).then_inc(S("dft_in"), 16)
            for h in range(8):
                na_bias(h)
                na_mask(h)
            pool.wait_ge(S("res_out"), 16)
            pool.dma_start(G[:, 2, :], t["final_norm_g_2"].partition_broadcast(P)) \
                .then_inc(S("final_gain"), 16)
            for m in range(96):
                pool.wait_ge(S("gate_hi"), m + 1)
                pool.tensor_tensor(out=GL[:, 3 - m % 4, :, :], in0=merge_piece(chunk, m), in1=GH[:, m % 4, :, :].bitcast(F32),
                                   op=ALU.subtract).then_inc(S("gate_lo"), 1)
            with pool.Fori(0, NEXP // 4) as it:
                for j in range(4):
                    expert(it * 4, j)

        @block.vector
        def _(dve):
            V = nc.vector
            chain = [0]

            def link(ins):
                chain[0] += 1
                ins.then_inc(S("dve_chain"), 1)
                dve.wait_ge(S("dve_chain"), chain[0])

            def ts(o, i, a, b=None, p=ALU.mult, q=ALU.add):
                if b is None:
                    return V.tensor_scalar(o, i, a, None, p)
                return V.tensor_scalar(o, i, a, b, p, q)

            def tt_(o, a, b, op=ALU.mult):
                return V.tensor_tensor(o, a, b, op)

            def stt(o, a, s, b, p=ALU.mult, q=ALU.add):
                return V.scalar_tensor_tensor(out=o, in0=a, scalar=s, in1=b, op0=p, op1=q)

            def rstd(y, x, inv_n, scale=None):
                n = x.shape[-1]
                v, xh = (wn[:, i, 0:n] for i in range(2))
                link(ts(v, x, inv_n, EPS))
                ts(xh, v, -0.5)
                link(ts(y.bitcast(I32), v.bitcast(I32), -0.5, 1597463007.0))
                for _ in range(3):
                    link(tt_(v, y, y))
                    link(tt_(v, v, xh))
                    link(stt(y, v, 1.5, y, ALU.add, ALU.mult))
                if scale is not None:
                    link(ts(y, y, scale))

            def norm_heads(ph):
                for n, (x, gain, scale, *_) in enumerate(head_calls(ph)):
                    c = hc0[ph] + n
                    h, d = x.shape[1], x.shape[2]
                    dve.wait_ge(S("heads_sq"), c + 1)
                    V.reduce_sum(ss[:, 16:16 + h], sqb[:, c % 2, 0:h * d].rearrange("p (h d) -> p h d", h=h), axis=AX) \
                        .then_inc(S("heads_summed"), 1)
                    dve.wait_ge(S("heads_summed"), c + 1)
                    rstd(wn[:, 2, 0:h], ss[:, 16:16 + h], 1.0 / d, scale)
                    link(tt_(x, x, spread(wn[:, 2, 0:h], 2, d)))
                    tt_(x, x, spread(gain, 1, h)).then_inc(S("heads_scaled"), 1)

            def mod_acc(q, k0=0, k1=KT):
                l, j = MODSEQ[q]
                w = arrived(dve, ("mod", min(l, 2), j))
                a = acc[:, q % 2, :]
                c0 = {0: 0, 1: 0, 2: 8, 3: 16}[l]
                for k in range(k0, k1):
                    c = cond[:, c0 + k:c0 + k + 1]
                    ins = ts(a, w[:, k, :], c) if k == 0 else stt(a, w[:, k, :], c, a)
                    if k < KT - 1:
                        link(ins)
                    else:
                        ins.then_inc(S("mod_acc"), 1)

            def mod_between(ph, i):
                _, q0, n = MOD_IN_ATT[ph]
                r = i - span(ph)[0]
                if r % 4 == 3 and r >= 7:
                    mod_fin(q0 + r // 4 - 1)
                if r < 4 * n:
                    mod_acc(q0 + r // 4, 2 * (r % 4), 2 * (r % 4) + 2)

            def mod_fin(q):
                l, j = MODSEQ[q]
                v, hf = j // 2, j % 2
                dve.wait_ge(S("mod_sum"), q + 1)
                p = ps[:, mod_bank(q), :]
                if v in (2, 5):
                    dve.wait_ge(S(f"gate_bias{l}"), 32)
                    g = G[:, 2 * (l % 2) + v // 3, hf * W:(hf + 1) * W]
                    tt_(g, g, p, ALU.add).then_inc(S("mod_fin"), 1)
                    dve.wait_ge(S("mod_fin"), q + 1)
                    return
                w4 = mtmp.rearrange("p (c n) -> p c n", c=4)
                link(tt_(w4, p.rearrange("p (c n) -> p c n", c=4), spread(ident, 1, 4)))
                m = modc[:, l, v, 4 * hf:4 * hf + 4]
                link(V.reduce_sum(m, w4, axis=AX))
                bias = col("adab")[:, 48 * min(l, 2) + 8 * v + 4 * hf:48 * min(l, 2) + 8 * v + 4 * hf + 4]
                tt_(m, m, bias, ALU.add).then_inc(S("mod_fin"), 1)
                dve.wait_ge(S("mod_fin"), q + 1)

            def norm(i, src):
                l, v = ((0, 1), (0, 4), (1, 1), (1, 4), (2, 1), (3, 1), (2, 4))[i]
                gain = (col("nmix")[:, 0:8], col("nmlp")[:, 0:8], col("nmix")[:, 8:16], col("nmlp")[:, 8:16],
                        col("n1"), col("n1"), col("n2"))[i]
                stt(coef[:, i, :], modc[:, l, v, :], 1.0, gain, ALU.add, ALU.mult).then_inc(S("coef"), 1)
                dve.wait_ge(S("norm_sq"), 2 * i + 2)
                r = ss[:, 4:6]
                rstd(r, ss[:, 2 * (i % 2):2 * (i % 2) + 2], 1.0 / D)
                for tt in range(TT):
                    ts(xs[:, tt, :], src[:, tt, :], r[:, tt:tt + 1]).then_inc(S("norm_scaled"), 1)

            def split_x(i, n):
                for k in range(KT):
                    dve.wait_ge(S("norm_out"), KT * i + k + 1)
                    last = tt_(XL[:, k, :], hT[:, k, :], XH[:, k, :].bitcast(F32), ALU.subtract)
                last.then_inc(S("split_x"), 1)

            def mlp_lo(l, j):
                for f in range(4):
                    n = 32 * l + 4 * j + f
                    dve.wait_ge(S("hid_read"), 3 * n + 3)
                    tt_(HL[:, f, :], tmp[:, n % 2, SEQ:2 * SEQ], HH[:, f, :].bitcast(F32), ALU.subtract) \
                        .then_inc(S("hid_out"), 1)

            def mlp(l, q):
                q0 = q
                for j in range(FF // W):
                    mlp_lo(l, j)
                    for m in mod_in_mlp(l, j):
                        for _ in range(2 if l == 1 and m < 4 else 1):
                            mod_acc(q)
                            if q > q0:
                                mod_fin(q - 1)
                            q += 1
                mod_fin(q - 1)

            def residual(r, s):
                for n in range(2):
                    for tt in range(TT):
                        m = 2 * n + tt
                        dve.wait_ge(S("res"), 4 * r + m + 1)
                        link(tt_(xs[:, tt, n * W:(n + 1) * W], ps[:, m, :], G[:, s, n * W:(n + 1) * W]))
                        x = X[:, tt, n * W:(n + 1) * W]
                        tt_(x, x, xs[:, tt, n * W:(n + 1) * W], ALU.add).then_inc(S("res_out"), 1)
                dve.wait_ge(S("res_out"), 4 * r + 4)

            def attention(ph, between=None):
                a, b = span(ph)
                for i in range(a, b + 4):
                    if i < b:
                        dve.wait_ge(S("scored"), i + 1)
                        if i >= 3:
                            dve.wait_ge(S("pt"), i - 2)
                        if ph == "na" and i % 2 == 0:
                            dve.wait_ge(S("nab"), (i - a) // 2 + 1)
                        for j, (c, n, mask) in enumerate(softmax_of(UNITS[i])):
                            pc = j * W
                            last = V.tensor_tensor_reduce(out=Eb[:, i % 3, c:c + n], in0=s_bank(i)[:, pc:pc + n], in1=mask[:, 0:n],
                                                          scale=-1.0, scalar=3e38, op0=ALU.add, op1=ALU.min,
                                                          accum_out=mx[:, i % NST, j:j + 1])
                        last.then_inc(S("masked"), 1)
                    if a <= i - 4:
                        m = i - 4
                        dve.wait_ge(S("weighed"), m + 1)
                        o = ps[:, 6 + m % 2, :]
                        n = 2 if ph == "diff" else 1
                        link(V.reciprocal(rc[:, m % NST, 0:n], sm[:, m % NST, 0:n]))
                        if ph == "diff":
                            t2 = wn[:, 2, 0:P]
                            link(stt(t2, o[:, P:2 * P], rc[:, m % NST, 1:2], spread(lam[:, 5], 1, P), ALU.mult, ALU.mult))
                            stt(output_of(UNITS[m]), o[:, 0:P], rc[:, m % NST, 0:1], t2).then_inc(S("o_out"), 1)
                        else:
                            ts(output_of(UNITS[m]), o[:, 0:HD], rc[:, m % NST, 0:1]).then_inc(S("o_out"), 1)
                    if between:
                        between(i)

            def sub_norm():
                dve.wait_ge(S("o_out"), span("diff")[1])
                sq = hTb[:, 0:1024].rearrange("p (t h d) -> p t h d", t=2, h=4)
                o = OkO[:, :, 0:512].rearrange("p t (h d) -> p t h d", h=4)
                for tt in range(TT):
                    last = tt_(sq[:, tt], o[:, tt], o[:, tt])
                link(last)
                link(V.reduce_sum(ss[:, 16:24], hTb[:, 0:1024].rearrange("p (g d) -> p g d", d=P), axis=AX))
                rstd(wn[:, 2, 0:8], ss[:, 16:24], 1.0 / P, 1.0 - LAM_INIT)
                for tt in range(TT):
                    last = tt_(o[:, tt], o[:, tt], spread(wn[:, 2, 4 * tt:4 * tt + 4], 2, P))
                last.then_inc(S("sub_done"), 1)

            cw = col("convw").rearrange("p (c j) -> p c j", c=4)
            TAP_ORDER = [TAPS // 2] + [j for j in range(TAPS) if j != TAPS // 2]

            def conv_tap(n):
                if n >= TAPS:
                    return
                j = TAP_ORDER[n]
                if n:
                    dve.wait_ge(S("conv_tap"), n)
                lo, hi = max(0, TAPS // 2 - j), min(SEQ, SEQ + TAPS // 2 - j)
                for k in range(4):
                    z = Z[:, k, lo + j - TAPS // 2:hi + j - TAPS // 2]
                    if n == 0:
                        last = ts(convy[:, k, :], z, cw[:, k, j:j + 1], col("convb")[:, k:k + 1])
                    else:
                        last = stt(convy[:, k, lo:hi], z, cw[:, k, j:j + 1], convy[:, k, lo:hi])
                last.then_inc(S("conv_tap"), 1)

            mtmp = wn[:, 0:2, :].rearrange("p s n -> p (s n)")
            dve.wait_ge(S("cols_in"), 16)
            dve.wait_ge(S("cond"), 1)
            for q in range(4):
                mod_acc(q)
                if q == 1:
                    dve.wait_ge(S("ident_in"), 16)
                if q:
                    mod_fin(q - 1)
            mod_fin(3)
            dve.wait_ge(S("consts_in"), 16 * NSMALL)
            dve.wait_ge(S("ones_set"), 2)
            norm(0, X)
            link(V.tensor_copy(posf[:, :], posi[:, :]))
            an, kk, tm = rw[:, 0, :], rw[:, 1, :], rw[:, 2, :]
            for tt in range(TT):
                last = ts(an[:, 48 * tt:48 * tt + 48], con("invf"), posf[:, tt:tt + 1])
            link(last)
            link(ts(kk, an, 1.0 / TWO_PI, 12582912.0))
            link(ts(kk, kk, 12582912.0, None, ALU.subtract))
            c1 = 6.28125
            c2 = float(np.float32(np.round((TWO_PI - c1) * 2 ** 20) / 2 ** 20))
            c3 = TWO_PI - c1 - c2
            for c in (c1, c2, c3):
                link(stt(an, kk, -c, an))
            sn, cs = rope[:, 96:192], rope[:, 0:96]
            link(ts(sn, an, PI_LO, -PI_LO, ALU.min, ALU.max))
            link(ts(tm, sn, -1.0))
            link(tt_(tm, tm, sn, ALU.max))
            ts(cs, tm, -1.0, float(np.pi / 2)).then_inc(S("angles"), 1)
            lv = row("lam").rearrange("p (i d) -> p i d", i=4)
            for i in range(2):
                link(V.tensor_tensor_reduce(out=rw[:, 3, 0:64], in0=lv[:, 2 * i, :], in1=lv[:, 2 * i + 1, :], scale=1.0,
                                            scalar=0.0, op0=ALU.mult, op1=ALU.add, accum_out=lam[:, i:i + 1]))
            V.engine_nop().then_inc(S("angles"), 1)
            dve.wait_ge(S("lam_exp"), 1)
            link(tt_(lam[:, 4:5], lam[:, 3:4], lam[:, 2:3], ALU.subtract))
            link(ts(lam[:, 5:6], lam[:, 4:5], LAM_INIT, None, ALU.subtract))
            for q in (4, 5):
                mod_acc(q)
                if q > 4:
                    mod_fin(q - 1)
            dve.wait_ge(S("lat_sq"), 4)
            rstd(ss[:, 12:14], ss[:, 8:10], 1.0 / QR)
            rstd(ss[:, 14:16], ss[:, 10:12], 1.0 / KVR)
            for tt in range(TT):
                ts(Ue[:, tt, 0:QR], Ue[:, tt, 0:QR], ss[:, 12 + tt:13 + tt])
                last = ts(Ue[:, tt, QR:QR + KVR], Ue[:, tt, QR:QR + KVR], ss[:, 14 + tt:15 + tt])
            last.then_inc(S("lat_scaled"), 1)
            for tt in range(TT):
                V.tensor_copy(Km[:, tt, :, NOPE:QKD], spread(Ue[:, tt, QR + KVR:QR + KVR + ROPE], 1, MH)) \
                    .then_inc(S("krope"), 1)
            mod_acc(6)
            mod_fin(5)
            norm_heads("dilq")
            for q in (7, 8):
                mod_acc(q)
                mod_fin(q - 1)
            norm_heads("dilk")
            for q in (9, 10, 11):
                mod_acc(q)
                mod_fin(q - 1)
            mod_fin(11)
            norm_heads("mla")
            attention("dil")
            attention("mla", between=lambda i: mod_between("mla", i))
            residual(0, 0)
            norm(1, X)
            split_x(1, 0)
            mlp(0, 16)
            residual(1, 1)
            norm(2, X)
            for c in (0, 1, 3, 4):
                norm_heads(f"odd{c}")
            attention("diff")

            def between_moba(i):
                if i == span("moba")[0] + 4:
                    sub_norm()
                mod_between("moba", i)

            attention("moba", between=between_moba)
            residual(2, 2)
            norm(3, X)
            split_x(3, 1)
            mlp(1, 28)
            residual(3, 3)
            norm(4, X)
            dve.wait_ge(S("ctx_in"), 16)
            dve.wait_ge(S("norm_tr"), 5 * KT)
            norm(5, ctx_x)
            norm_heads("gq")
            norm_heads("gk")
            for f in range(4):
                dve.wait_ge(S("glu_sig"), f + 1)
                tt_(Z[:, f, :], tmp[:, f % 2, 0:SEQ], ps[:, 4 + f % 2, 0:SEQ]).then_inc(S("glu_out"), 1)
            dve.wait_ge(S("glu_out"), 4)
            attention("gqa", between=lambda i: conv_tap(i - span("gqa")[0]) if i < span("gqa")[1] else None)
            attention("na", between=lambda i: conv_tap(i - span("gqa")[0]) if i < span("na")[1] else None)
            dve.wait_ge(S("conv_sum"), 1)
            rstd(wn[:, 2, 0:256], ps[:, 6, 0:SEQ], 1.0 / 512)
            tt_(convs[:, :, :], convy[:, :, :], spread(wn[:, 2, :], 1, 4)).then_inc(S("conv_scaled"), 1)

            def branch_lo(b):
                dve.wait_ge(S("y_hi"), b + 1)
                hi, lo = branch_split(b)
                tt_(lo, branch_out[b], hi.bitcast(F32), ALU.subtract).then_inc(S("y_lo"), 1)

            branch_lo(0)
            dve.wait_ge(S("mx_hi"), 2)
            dve.wait_ge(S("conv_out"), 4)
            tt_(XL[:, :, :], hT[:, :, :], XH[:, :, :].bitcast(F32), ALU.subtract).then_inc(S("mx_lo"), 1)
            for n in range(32):
                dve.wait_ge(S("merge_act"), n + 1)
                f = n % 8
                z = ps[:, 4 + n % 2, SEQ:2 * SEQ]
                g = tmp[:, n % 2, 0:SEQ]
                if n < 8:
                    tt_(M2[:, f, :], g, z).then_inc(S("merge_out"), 1)
                else:
                    tt_(xs[:, 0, 256 * (n % 2):256 * (n % 2) + 256], g, z).then_inc(S("merge_out"), 1)
                    dve.wait_ge(S("merge_out"), n + 1)
                    link(tt_(M2[:, f, :], M2[:, f, :], xs[:, 0, 256 * (n % 2):256 * (n % 2) + 256], ALU.add))
                if n % 8 == 2 and n < 24:
                    branch_lo(n // 8 + 1)
            V.engine_nop().then_inc(S("merged"), 1)
            residual(4, 0)
            norm(6, X)
            split_x(6, 2)
            dve.wait_ge(S("router_sig"), 1)
            sc = moe[:, 0:32]
            sel = moe[:, 32:64]
            link(tt_(sel.rearrange("p (t e) -> p t e", t=2), sc.rearrange("p (t e) -> p t e", t=2),
                     spread(row("rbias"), 1, 2), ALU.add))
            s4 = sel.rearrange("p (g e) -> p g e", e=4)
            pr = moe[:, 64:112].rearrange("p (g i) -> p g i", i=6)
            for i, (a, b) in enumerate(((0, 1), (0, 2), (0, 3), (1, 2), (1, 3), (2, 3))):
                last = tt_(pr[:, :, i:i + 1], s4[:, :, a:a + 1], s4[:, :, b:b + 1], ALU.add)
            link(last)
            gs = moe[:, 112:120]
            link(V.reduce_max(gs, pr, axis=AX))
            tri = con("tri").rearrange("p (a b) -> p a b", a=4)

            def ranks(dst, v, n, w1, w2):
                for g in range(n):
                    a = spread(v[:, g, :], 1, 4)
                    b = spread(v[:, g, :], 2, 4)
                    tt_(w1[:, g], a, b, ALU.is_gt)
                    last = tt_(w2[:, g], a, b, ALU.is_equal)
                link(last)
                link(tt_(w2, w2, spread(tri, 1, n)))
                link(tt_(w1, w1, w2, ALU.add))
                link(V.reduce_sum(dst, w1, axis=AX))

            rk = moe[:, 120:152]
            ranks(rk.rearrange("p (g e) -> p g e", e=4), s4, 8, moe[:, 152:280].rearrange("p (g a b) -> p g a b", g=8, a=4),
                  moe[:, 280:408].rearrange("p (g a b) -> p g a b", g=8, a=4))
            gk = moe[:, 408:416]
            ranks(gk.rearrange("p (g e) -> p g e", e=4), gs.rearrange("p (g e) -> p g e", e=4), 2,
                  moe[:, 416:448].rearrange("p (g a b) -> p g a b", g=2, a=4),
                  moe[:, 448:480].rearrange("p (g a b) -> p g a b", g=2, a=4))
            link(ts(rk, rk, 2.0, None, ALU.is_lt))
            link(ts(gk, gk, 1.0, None, ALU.is_lt))
            gt = moe[:, 480:512]
            link(tt_(gt, sc, rk))
            g8 = gt.rearrange("p (g e) -> p g e", e=4)
            link(tt_(g8, g8, spread(gk, 2, 4)))
            link(V.reduce_sum(moe[:, 512:514], gt.rearrange("p (t e) -> p t e", t=2), axis=AX))
            link(V.reciprocal(moe[:, 514:516], moe[:, 512:514]))
            link(tt_(gt.rearrange("p (t e) -> p t e", t=2), gt.rearrange("p (t e) -> p t e", t=2),
                     spread(moe[:, 514:516], 2, 16)))
            link(V.memset(accY[:, :, :], 0.0))
            with dve.Fori(0, NEXP // 4) as it:
                e = it * 4
                for j in range(4):
                    for f in range(4):
                        dve.wait_ge(S("merge_act"), 32 + 4 * j + f + 1 + e * 4)
                        up = ps[:, 4 + f % 2, SEQ:2 * SEQ]
                        tt_(HH[:, f, :], tmp[:, f % 2, 0:SEQ], up).then_inc(S("hidden"), 1)
                        tt_(tmp[:, f % 2, SEQ:2 * SEQ], tmp[:, f % 2, 0:SEQ], up).then_inc(S("hidden"), 1)
                        dve.wait_ge(S("hidden"), 8 * j + 2 * f + 2 + e * 8)
                        tt_(HL[:, f, :], tmp[:, f % 2, SEQ:2 * SEQ], HH[:, f, :].bitcast(F32), ALU.subtract) \
                            .then_inc(S("merge_out"), 1)
                    for n in range(2):
                        for tt in range(TT):
                            m = 2 * n + tt
                            dve.wait_ge(S("res"), 20 + 4 * j + m + 1 + e * 4)
                            if m == 0:
                                dve.wait_ge(S("res_out"), 20 + 4 * j + e * 4)
                            y = accY[:, tt, n * W:(n + 1) * W]
                            stt(y, ps[:, m, :], gt[:, bass.ds(16 * tt + e + j, 1)], y).then_inc(S("res_out"), 1)
            dve.wait_ge(S("res_out"), 20 + 4 * NEXP)
            for tt in range(TT):
                link(tt_(accY[:, tt, :], accY[:, tt, :], G[:, 1, :]))
                last = tt_(X[:, tt, :], X[:, tt, :], accY[:, tt, :], ALU.add)
            last.then_inc(S("final_x"), 1)
            dve.wait_ge(S("norm_sq"), 16)
            rstd(ss[:, 4:6], ss[:, 2:4], 1.0 / D)
            dve.wait_ge(S("final_gain"), 16)
            for tt in range(TT):
                stt(xs[:, tt, :], X[:, tt, :], ss[:, 4 + tt:5 + tt], G[:, 2, :], ALU.mult, ALU.mult).then_inc(S("final_done"), 1)


def kernel(**inputs):
    import concourse.bacc as _bacc
    from concourse.bass_utils import run_bass_kernel_spmd as _run

    a = {n: np.asarray(v) for n, v in inputs.items()}
    nc = _bacc.Bacc("TRN2", target_bir_lowering=False, num_devices=1)

    def col(v):
        return v.reshape(-1, P).T

    whole = ("x", "ctx_2", "ada_w", "ada_b", "mlp_w1", "mlp_w2", "even_w_in", "even_w_out", "mla_w_uq", "mla_w_ukv",
             "odd_w_in", "odd_w_out", "w_mod_2", "b_mod_2", "w_in_2", "w_branch_2", "w_out_2", "w_router_2",
             "w_expert_gu_2", "w_expert_down_2", "final_norm_g_2")
    arr = {n: np.ascontiguousarray(a[n]) for n in whole}
    arr["positions"] = np.ascontiguousarray(a["positions"].reshape(TT, P).T)
    arr["cols"] = np.ascontiguousarray(np.concatenate(
        [col(a["c"]), col(a["c_2"]), col(a["c_ctx_2"]), col(a["ada_b"]), col(a["b_mod_2"]), col(a["norm_mix"]),
         col(a["norm_mlp"]), col(a["norm1_g_2"]), col(a["norm2_g_2"]), col(a["mla_q_lat_norm"]), col(a["mla_kv_lat_norm"]),
         col(a["diff_subln"]), a["conv_w_2"][0].reshape(TAPS, 4, P).transpose(2, 1, 0).reshape(P, -1), col(a["conv_b_2"]),
         col(a["conv_norm_g_2"])], 1))
    arr["rows"] = np.ascontiguousarray(np.concatenate(
        [a[n].reshape(-1) for n in ("mla_q_norm", "mla_k_norm", "dil_q_norm", "dil_k_norm", "diff_q_norm", "diff_k_norm",
                                    "moba_q_norm", "moba_k_norm", "q_norm_g_2", "k_norm_g_2", "diff_lambda",
                                    "router_bias_2")]))
    rpb = np.ascontiguousarray(a["na_rpb_2"][0])
    i = rpb.itemsize
    flat = np.lib.stride_tricks.as_strided(rpb.reshape(-1)[7 * 31 + 15:], shape=(8, 4, 64, 4, 64),
                                           strides=(15 * 31 * i, -31 * i, -i, 31 * i, i))
    arr["na_bias"] = np.ascontiguousarray(flat).reshape(8, SEQ, SEQ)
    arr["consts"], arr["dft"] = shape_constants()
    aps = {n: nc.dram_tensor("in_" + n, v.shape, mybir.dt.from_np(v.dtype), kind="ExternalInput").ap() for n, v in arr.items()}
    out = nc.dram_tensor("out_0", (1, SEQ, D), F32, kind="ExternalOutput").ap()
    program(nc, aps, out)
    r = _run(nc, [{"in_" + n: v for n, v in arr.items()}], core_ids=[0])
    return r.results[0]["out_0"]
```
